# Optimizing a Trainium2 kernel written in Bass

```python
import math, functools
import jax, jax.numpy as jnp
from jax import lax
import numpy as np

D_MODEL = 1024
BATCH = 1
SEQ = 512
DEPTH = 1
DEC_BATCH = 8
DEC_SEQ = 8
PAST_LEN = 256
PAGE_SIZE = 128

N_HEADS = 8
N_KV = 2
GROUP = N_HEADS // N_KV
HEAD_DIM = 64
ATTN_W = N_HEADS * HEAD_DIM
KV_W = N_KV * HEAD_DIM
CMP_LEN = 32
CMP_STRIDE = 16
SEL_LEN = 64
N_SEL = 8
WINDOW = 512
Q_BLOCK = 128
FORCE_BONUS = 1000.0
CONV_CH = D_MODEL // 2
CONV_WIDTH = 31
D_FF = 2816
FFN_CONV_WIDTH = 3
IN_W = ATTN_W + 6 * KV_W + 3 * N_HEADS + 2 * CONV_CH + 2 * D_MODEL
EPS = 1e-6
NEG = -1e30
TINY = 1e-30

kernel_name = "nsa_conformer_gated_hybrid_step"

def rmsnorm(x, g):
    x32 = x.astype(jnp.float32)
    y = x32 * lax.rsqrt(jnp.mean(x32 * x32, -1, keepdims=True) + EPS) * g.astype(jnp.float32)
    return y.astype(x.dtype)

def layernorm(x, g, b):
    x32 = x.astype(jnp.float32)
    mu = jnp.mean(x32, -1, keepdims=True)
    xc = x32 - mu
    var = jnp.mean(xc * xc, -1, keepdims=True)
    return (xc * lax.rsqrt(var + EPS) * g.astype(jnp.float32) + b.astype(jnp.float32)).astype(x.dtype)

def masked_softmax(s, mask):
    s = jnp.where(mask, s.astype(jnp.float32), NEG)
    m = jnp.max(s, -1, keepdims=True)
    e = jnp.where(mask, jnp.exp(s - m), 0.0)
    return e / jnp.maximum(jnp.sum(e, -1, keepdims=True), TINY)

def causal_dwconv(u_ext, w, b):
    C = u_ext.shape[-1]
    y = lax.conv_general_dilated(u_ext, w[:, None, :], (1,), 'VALID',
                                 dimension_numbers=('NWC', 'WIO', 'NWC'), feature_group_count=C)
    return y + b

def compress_blocks(k, w, b):
    B, T, G, HD = k.shape
    n_cmp = (T - CMP_LEN) // CMP_STRIDE + 1
    idx = (jnp.arange(n_cmp) * CMP_STRIDE)[:, None] + jnp.arange(CMP_LEN)[None, :]
    blk = jnp.transpose(k[:, idx], (0, 1, 3, 2, 4)).reshape(B, n_cmp, G, CMP_LEN * HD)
    return blk @ w + b

def sel_blocks(k):
    B, T, G, HD = k.shape
    n_slc = -(-T // SEL_LEN)
    k = jnp.pad(k, ((0, 0), (0, n_slc * SEL_LEN - T), (0, 0), (0, 0)))
    return jnp.transpose(k.reshape(B, n_slc, SEL_LEN, G, HD), (0, 3, 1, 2, 4))

def cmp_to_sel_map(n_cmp, n_slc):
    s = jnp.arange(n_cmp) * CMP_STRIDE
    e = s + CMP_LEN - 1
    js = jnp.arange(n_slc) * SEL_LEN
    je = js + SEL_LEN - 1
    return ((s[:, None] <= je[None, :]) & (e[:, None] >= js[None, :])).astype(jnp.float32)

def nsa_core(q, t, gates, kcmp, vcmp, cmp_end, sel_map, ks_blk, vs_blk, kw, vw, kw_pos):
    B, Tq = q.shape[:2]
    q = q * (HEAD_DIM ** -0.5)
    s_c = jnp.einsum('bqgrd,bngd->bqgrn', q, kcmp)
    p_c = masked_softmax(s_c, (cmp_end[None, :] <= t[:, None])[None, :, None, None, :])
    o_c = jnp.einsum('bqgrn,bngd->bqgrd', p_c.astype(vcmp.dtype), vcmp)
    imp = jnp.einsum('bqgrn,nj->bqgj', p_c, sel_map)
    n_slc = sel_map.shape[1]
    jb = jnp.arange(n_slc)
    cur = (t // SEL_LEN)[:, None]
    valid = (jb[None, :] * SEL_LEN) <= t[:, None]
    forced = (jb[None, :] == 0) | (jb[None, :] == cur) | (jb[None, :] == cur - 1)
    score = jnp.where(valid[None, :, None, :],
                      imp + FORCE_BONUS * forced[None, :, None, :].astype(jnp.float32), -1.0)
    n_top = min(N_SEL, n_slc)
    _, sel = lax.top_k(score, n_top)
    bi = jnp.arange(B)[:, None, None, None]
    gi = jnp.arange(N_KV)[None, None, :, None]
    k_s = ks_blk[bi, gi, sel]
    v_s = vs_blk[bi, gi, sel]
    kpos = sel[..., None] * SEL_LEN + jnp.arange(SEL_LEN)
    mask_s = (kpos <= t[None, :, None, None, None]).reshape(B, Tq, N_KV, 1, n_top * SEL_LEN)
    s_s = jnp.einsum('bqgrd,bqgnkd->bqgrnk', q, k_s).reshape(B, Tq, N_KV, GROUP, n_top * SEL_LEN)
    p_s = masked_softmax(s_s, mask_s).reshape(B, Tq, N_KV, GROUP, n_top, SEL_LEN)
    o_s = jnp.einsum('bqgrnk,bqgnkd->bqgrd', p_s.astype(v_s.dtype), v_s)
    dt = t[:, None] - kw_pos[None, :]
    mask_w = ((dt >= 0) & (dt <= WINDOW) & (kw_pos >= 0)[None, :])[None, :, None, None, :]
    s_w = jnp.einsum('bqgrd,bkgd->bqgrk', q, kw)
    p_w = masked_softmax(s_w, mask_w)
    o_w = jnp.einsum('bqgrk,bkgd->bqgrd', p_w.astype(vw.dtype), vw)
    return (gates[:, :, 0][..., None] * o_c + gates[:, :, 1][..., None] * o_s
            + gates[:, :, 2][..., None] * o_w)

def nsa_prompt(q, gates, kc, vc, ks, vs, kw, vw, phi):
    w_pk, b_pk, w_pv, b_pv = phi
    B, S = q.shape[:2]
    kcmp = compress_blocks(kc, w_pk, b_pk)
    vcmp = compress_blocks(vc, w_pv, b_pv)
    n_cmp = kcmp.shape[1]
    cmp_end = jnp.arange(n_cmp) * CMP_STRIDE + (CMP_LEN - 1)
    ks_blk = sel_blocks(ks)
    vs_blk = sel_blocks(vs)
    sel_map = cmp_to_sel_map(n_cmp, ks_blk.shape[2])
    kw_pad = jnp.pad(kw, ((0, 0), (WINDOW, 0), (0, 0), (0, 0)))
    vw_pad = jnp.pad(vw, ((0, 0), (WINDOW, 0), (0, 0), (0, 0)))
    nb = S // Q_BLOCK
    qb = q.reshape(B, nb, Q_BLOCK, N_KV, GROUP, HEAD_DIM).swapaxes(0, 1)
    gb = gates.reshape(B, nb, Q_BLOCK, 3, N_KV, GROUP).swapaxes(0, 1)

    def one_block(args):
        q_i, g_i, i = args
        start = i * Q_BLOCK
        t = start + jnp.arange(Q_BLOCK)
        kw_i = lax.dynamic_slice_in_dim(kw_pad, start, WINDOW + Q_BLOCK, axis=1)
        vw_i = lax.dynamic_slice_in_dim(vw_pad, start, WINDOW + Q_BLOCK, axis=1)
        kw_pos = start - WINDOW + jnp.arange(WINDOW + Q_BLOCK)
        return nsa_core(q_i, t, g_i, kcmp, vcmp, cmp_end, sel_map, ks_blk, vs_blk, kw_i, vw_i, kw_pos)

    o = lax.map(one_block, (qb, gb, jnp.arange(nb)))
    o = o.swapaxes(0, 1).reshape(B, S, ATTN_W)
    win = jnp.stack([kw, vw], 2)[:, -WINDOW:]
    return o, win

def nsa_sample(q, gates, kc, vc, ks, vs, kw, vw, phi, past, win_buf):
    w_pk, b_pk, w_pv, b_pv = phi
    P = past.shape[1]
    WB = win_buf.shape[1]
    Tq = q.shape[1]
    kc_all = jnp.concatenate([past[:, :, 0], kc], 1)
    vc_all = jnp.concatenate([past[:, :, 1], vc], 1)
    ks_all = jnp.concatenate([past[:, :, 2], ks], 1)
    vs_all = jnp.concatenate([past[:, :, 3], vs], 1)
    kcmp = compress_blocks(kc_all, w_pk, b_pk)
    vcmp = compress_blocks(vc_all, w_pv, b_pv)
    n_cmp = kcmp.shape[1]
    cmp_end = jnp.arange(n_cmp) * CMP_STRIDE + (CMP_LEN - 1)
    ks_blk = sel_blocks(ks_all)
    vs_blk = sel_blocks(vs_all)
    sel_map = cmp_to_sel_map(n_cmp, ks_blk.shape[2])
    new_w = jnp.stack([kw, vw], 2)
    win_all = jnp.concatenate([win_buf, new_w], 1)
    kw_pos = P - WB + jnp.arange(WB + Tq)
    t = P + jnp.arange(Tq)
    o = nsa_core(q, t, gates, kcmp, vcmp, cmp_end, sel_map, ks_blk, vs_blk,
                 win_all[:, :, 0], win_all[:, :, 1], kw_pos)
    return o.reshape(q.shape[0], Tq, ATTN_W), win_all[:, -WINDOW:]

def mixer_inputs(z, w_in):
    B, T = z.shape[:2]
    sizes = [ATTN_W] + [KV_W] * 6 + [3 * N_HEADS, 2 * CONV_CH]
    cuts = [int(c) for c in np.cumsum(sizes)]
    pieces = jnp.split(z @ w_in, cuts, axis=-1)
    q = pieces[0].reshape(B, T, N_KV, GROUP, HEAD_DIM)
    kc, vc, ks, vs, kw, vw = [p.reshape(B, T, N_KV, HEAD_DIM) for p in pieces[1:7]]
    g_nsa = jax.nn.sigmoid(pieces[7]).reshape(B, T, 3, N_KV, GROUP)
    u2 = pieces[8]
    u = u2[..., :CONV_CH] * jax.nn.sigmoid(u2[..., CONV_CH:])
    g_mrg = jax.nn.sigmoid(pieces[9]).reshape(B, T, 2, D_MODEL)
    return q, kc, vc, ks, vs, kw, vw, g_nsa, u, g_mrg

def conformer_conv(u, hist, conv_w, conv_b, ln_g, ln_b):
    ext = jnp.concatenate([hist, u], 1)
    y = jax.nn.silu(layernorm(causal_dwconv(ext, conv_w, conv_b), ln_g, ln_b))
    return y, ext[:, -(CONV_WIDTH - 1):]

def conv_ffn(z, hist, w_up, cw, cb, w_down):
    ext = jnp.concatenate([hist, z @ w_up], 1)
    h = causal_dwconv(ext, cw, cb)
    g, v = jnp.split(h, 2, axis=-1)
    return (jax.nn.gelu(g, approximate=True) * v) @ w_down, ext[:, -(FFN_CONV_WIDTH - 1):]

def trunk_layer(x, attend, conv_hist, ffn_hist, g_mix_pre, g_mix_post, g_ffn_pre, g_ffn_post, w_in,
                w_attn_out, conv_w, conv_b, conv_ln_g, conv_ln_b, w_conv_out, w_out, w_up,
                ffn_conv_w, ffn_conv_b, w_down):
    z = rmsnorm(x, g_mix_pre)
    q, kc, vc, ks, vs, kw, vw, g_nsa, u, g_mrg = mixer_inputs(z, w_in)
    o_attn, win_state = attend(q, g_nsa, kc, vc, ks, vs, kw, vw)
    o_conv, conv_state = conformer_conv(u, conv_hist, conv_w, conv_b, conv_ln_g, conv_ln_b)
    h = (g_mrg[:, :, 0] * (o_attn @ w_attn_out) + g_mrg[:, :, 1] * (o_conv @ w_conv_out)) @ w_out
    x = x + rmsnorm(h, g_mix_post)
    f, ffn_state = conv_ffn(rmsnorm(x, g_ffn_pre), ffn_hist, w_up, ffn_conv_w, ffn_conv_b, w_down)
    x = x + rmsnorm(f, g_ffn_post)
    kv_rows = jnp.stack([kc, vc, ks, vs], 2)
    return x, kv_rows, win_state, conv_state, ffn_state

def setup_inputs(seed: int = 0) -> dict:
    key = jax.random.key(seed)
    ks = list(jax.random.split(key, 32))
    f32 = jnp.float32

    def nrm(k, shape, scale):
        return jax.random.normal(k, shape, f32) * scale

    n_pages = PAST_LEN // PAGE_SIZE
    n_used = DEC_BATCH * n_pages
    n_phys = n_used + max(1, n_used // 4)
    win_buf = min(WINDOW, PAST_LEN)
    page_table = jax.random.permutation(ks[0], n_phys)[:n_used].reshape(DEC_BATCH, n_pages).astype(jnp.int32)
    return {
        "x_prompt": nrm(ks[1], (BATCH, SEQ, D_MODEL), 1.0),
        "x_sample": nrm(ks[2], (DEC_BATCH, DEC_SEQ, D_MODEL), 1.0),
        "cache_kv": nrm(ks[3], (DEPTH, n_phys, PAGE_SIZE, 4, N_KV, HEAD_DIM), 1.0),
        "state_kv_win": nrm(ks[4], (DEPTH, DEC_BATCH, win_buf, 2, N_KV, HEAD_DIM), 1.0),
        "state_conv": nrm(ks[5], (DEPTH, DEC_BATCH, CONV_WIDTH - 1, CONV_CH), 0.5),
        "state_ffn": nrm(ks[6], (DEPTH, DEC_BATCH, FFN_CONV_WIDTH - 1, 2 * D_FF), 1.0),
        "page_table": page_table,
        "norm_mix_pre": 1.0 + nrm(ks[7], (DEPTH, D_MODEL), 0.05),
        "norm_mix_post": 1.0 + nrm(ks[8], (DEPTH, D_MODEL), 0.05),
        "norm_ffn_pre": 1.0 + nrm(ks[9], (DEPTH, D_MODEL), 0.05),
        "norm_ffn_post": 1.0 + nrm(ks[10], (DEPTH, D_MODEL), 0.05),
        "w_in": nrm(ks[11], (DEPTH, D_MODEL, IN_W), D_MODEL ** -0.5),
        "w_phi_k": nrm(ks[12], (DEPTH, CMP_LEN * HEAD_DIM, HEAD_DIM), (CMP_LEN * HEAD_DIM) ** -0.5),
        "b_phi_k": nrm(ks[13], (DEPTH, HEAD_DIM), 0.02),
        "w_phi_v": nrm(ks[14], (DEPTH, CMP_LEN * HEAD_DIM, HEAD_DIM), (CMP_LEN * HEAD_DIM) ** -0.5),
        "b_phi_v": nrm(ks[15], (DEPTH, HEAD_DIM), 0.02),
        "w_attn_out": nrm(ks[16], (DEPTH, ATTN_W, D_MODEL), ATTN_W ** -0.5),
        "conv_w": nrm(ks[17], (DEPTH, CONV_WIDTH, CONV_CH), CONV_WIDTH ** -0.5),
        "conv_b": nrm(ks[18], (DEPTH, CONV_CH), 0.02),
        "conv_ln_g": 1.0 + nrm(ks[19], (DEPTH, CONV_CH), 0.05),
        "conv_ln_b": nrm(ks[20], (DEPTH, CONV_CH), 0.02),
        "w_conv_out": nrm(ks[21], (DEPTH, CONV_CH, D_MODEL), CONV_CH ** -0.5),
        "w_out": nrm(ks[22], (DEPTH, D_MODEL, D_MODEL), D_MODEL ** -0.5),
        "w_up": nrm(ks[23], (DEPTH, D_MODEL, 2 * D_FF), D_MODEL ** -0.5),
        "ffn_conv_w": nrm(ks[24], (DEPTH, FFN_CONV_WIDTH, 2 * D_FF), FFN_CONV_WIDTH ** -0.5),
        "ffn_conv_b": nrm(ks[25], (DEPTH, 2 * D_FF), 0.02),
        "w_down": nrm(ks[26], (DEPTH, D_FF, D_MODEL), D_FF ** -0.5),
    }

def reference(x_prompt, x_sample, cache_kv, state_kv_win, state_conv, state_ffn, page_table,
              norm_mix_pre, norm_mix_post, norm_ffn_pre, norm_ffn_post, w_in,
              w_phi_k, b_phi_k, w_phi_v, b_phi_v, w_attn_out, conv_w, conv_b, conv_ln_g, conv_ln_b,
              w_conv_out, w_out, w_up, ffn_conv_w, ffn_conv_b, w_down):
    B = x_prompt.shape[0]
    DB = x_sample.shape[0]
    xp, xs = x_prompt, x_sample
    kv_p, kv_s, win_p, win_s, conv_p, conv_s, ffn_p, ffn_s = [], [], [], [], [], [], [], []
    for l in range(DEPTH):
        lw = (norm_mix_pre[l], norm_mix_post[l], norm_ffn_pre[l], norm_ffn_post[l], w_in[l],
              w_attn_out[l], conv_w[l], conv_b[l], conv_ln_g[l], conv_ln_b[l], w_conv_out[l], w_out[l],
              w_up[l], ffn_conv_w[l], ffn_conv_b[l], w_down[l])
        phi = (w_phi_k[l], b_phi_k[l], w_phi_v[l], b_phi_v[l])
        attend_p = functools.partial(nsa_prompt, phi=phi)
        conv_h0 = jnp.zeros((B, CONV_WIDTH - 1, CONV_CH), xp.dtype)
        ffn_h0 = jnp.zeros((B, FFN_CONV_WIDTH - 1, 2 * D_FF), xp.dtype)
        xp, r_kv, r_win, r_conv, r_ffn = trunk_layer(xp, attend_p, conv_h0, ffn_h0, *lw)
        kv_p.append(r_kv); win_p.append(r_win); conv_p.append(r_conv); ffn_p.append(r_ffn)
        past = cache_kv[l][page_table].reshape(DB, -1, 4, N_KV, HEAD_DIM)
        attend_s = functools.partial(nsa_sample, phi=phi, past=past, win_buf=state_kv_win[l])
        xs, r_kv, r_win, r_conv, r_ffn = trunk_layer(xs, attend_s, state_conv[l], state_ffn[l], *lw)
        kv_s.append(r_kv); win_s.append(r_win); conv_s.append(r_conv); ffn_s.append(r_ffn)
    return (xp, xs, jnp.stack(kv_p), jnp.stack(kv_s), jnp.stack(win_p), jnp.stack(win_s),
            jnp.stack(conv_p), jnp.stack(conv_s), jnp.stack(ffn_p), jnp.stack(ffn_s))


_drawn_inputs = setup_inputs


def setup_inputs(seed=0):
    import zlib

    import numpy as np

    out = dict(_drawn_inputs(seed))
    spreads = {}
    factors = {'b_phi_k': 8.0, 'b_phi_v': 4.341, 'conv_ln_b': 3.728, 'ffn_conv_b': 3.388}
    for name, (base, spread) in spreads.items():
        noise = np.random.default_rng([zlib.crc32(name.encode()), seed]).standard_normal(out[name].shape)
        drawn = base * np.exp(spread * noise) if base else spread * noise
        out[name] = __import__('jax').numpy.asarray(drawn.astype(out[name].dtype))
    for name, factor in factors.items():
        out[name] = (out[name] * factor).astype(out[name].dtype)
    return out
```

```python
from contextlib import ExitStack

import concourse.bass as bass
from concourse import mybir

F32 = mybir.dt.float32
F32R = mybir.dt.float32r
BF16 = mybir.dt.bfloat16
I32 = mybir.dt.int32
ALU = mybir.AluOpType
ACT = mybir.ActivationFunctionType
AX = mybir.AxisListType

P = 128
D = 1024
KT = D // P
SEQ = 512
DB, DT = 8, 8
NS = DB * DT
NT = SEQ + NS
TT = 5
HALF = NT // 2
PAST = 256
PAGE = 128
NPG = DB * PAST // PAGE
HEADS, KVH, G, HD = 8, 2, 4, 64
CL, CS = 32, 16
NCP = (SEQ - CL) // CS + 1
NCS = (PAST + DT - CL) // CS + 1
CC_T = SEQ + DB * PAST
NCALL = (CC_T - CL) // CS + 1
CH = 512
CT = CH // P
CW = 31
HIST = CW - 1
SB_S = HIST + DT
EXT = HIST + SEQ + DB * SB_S
FF = 2816
FT = FF // P
FW = 3
UEXT = 2 + SEQ + DB * (2 + DT)
CEXT = UEXT - 2
EPS = 1e-6
NEG = -1e30
TINY = 1e-30
OFF_KV = 512
OFF_GATE = OFF_KV + 6 * 128
OFF_GLU = OFF_GATE + 24
OFF_MRG = OFF_GLU + 2 * CH
IN_W = OFF_MRG + 2 * D
ROWS = [P] * 4 + [NS]

P_FW = 0
P_CW = P_FW + FW * 2 * FT
P_FB = P_CW + CW * CT
P_CB = P_FB + 2 * FT
P_GPRE = P_CB + CT
P_GFFN = P_GPRE + KT
P_LNG = P_GFFN + KT
P_LNB = P_LNG + CT
P_ALL = P_LNB + CT

S_GLU = 0
S_KV = S_GLU + 2 * CT
S_Q = S_KV + 6
S_GATE = S_Q + 4
S_MRG = S_GATE + 1
S_OUT = S_MRG + 3 * KT
S_UP = S_OUT + KT
S_DOWN = S_UP + 2 * FT
S_END = S_DOWN + FT
MRG_DMAS = [1, 1, 3]
SEQ_GROUPS = [(0, 3), (3, 3), (6, 2)]


def slot_dmas(s):
    if S_Q <= s < S_GATE:
        return 2
    if S_MRG <= s < S_OUT:
        return MRG_DMAS[(s - S_MRG) % 3]
    return 1


def raw_value(s):
    return 16 * sum(slot_dmas(x) for x in range(s % 2, s + 1, 2))


UNITS = [(i, r, g, c) for i in range(4) for r in range(G) for g in range(KVH) for c in (1, 2)]
UNITS += [(4 + hf, 0, g, c) for hf in range(2) for g in range(KVH) for c in (0, 1, 2)]
NU = len(UNITS)
LAST = [max(n for n, u in enumerate(UNITS) if u[0] == q) for q in range(6)]
FIRST = [min(n for n, u in enumerate(UNITS) if u[0] == q) for q in range(6)]


def width(n):
    q, _, _, c = UNITS[n]
    return (q + 1) * P if q < 4 else (DB * NCS if c == 0 else PAST + NS)


def build_layer(nc, x_prompt, x_sample, cache_kv, state_kv_win, state_conv, state_ffn, page_table,
                g_mix_pre, g_mix_post, g_ffn_pre, g_ffn_post, w_in, w_phi_k, b_phi_k, w_phi_v, b_phi_v,
                w_attn_out, conv_w, conv_b, conv_ln_g, conv_ln_b, w_conv_out, w_out, w_up,
                ffn_conv_w, ffn_conv_b, w_down,
                y_prompt, y_sample, kv_prompt, kv_sample, win_prompt, win_sample,
                conv_prompt, conv_sample, ffn_prompt, ffn_sample):
    ctx = ExitStack()
    with ctx:
        base = (nc.sbuf_base + 63) // 32 * 32

        def at(name, shape, dt, col):
            return nc.alloc_sbuf_tensor_at(name, shape, dt, offset=base + 4 * col)

        A = 0
        B = A + 2 * KT * NT
        C = B + 6 * 1024
        DD = C + 4 * NT
        E = DD + 6 * NT
        FV = E + TT * 768
        GK = FV + NPG * P
        H = GK + 2 * DB * PAST
        I = H + NPG * P
        J = I + 4096 + 2 * CC_T + 2 * 768
        K = J + CT * EXT + CT * NT

        zh = at("zh", [P, KT, NT], F32R, A)
        zl = at("zl", [P, KT, NT], F32R, A + KT * NT)
        sq_x = at("sq_x", [P, TT, D], F32, A)
        raw = at("raw", [P, 2, 1024], F32, B)
        wh = at("wh", [P, 2, 1024], F32R, B + 2048)
        wl = at("wl", [P, 2, 1024], F32R, B + 4096)
        x = at("x", [P, TT, D], F32, C)
        qT = at("qT", [P, G, NT], F32, C)
        kvT = at("kvT", [P, 6, NT], F32, DD)
        ktok = at("ktok", [P, TT, 768], F32, E)
        par_raw = at("par_raw", [P, 3, P], F32, E)
        scv = at("scv", [P, 2, CH], F32, E + 384)
        sg = at("sg", [P, NT], F32, E + 384 + 1024)
        gT = at("gT", [24, NT], F32, E + 384 + 1024 + NT)
        vwin = at("vwin", [P, NPG, P], F32, FV)
        kpast = at("kpast", [P, 2, DB * PAST], F32, GK)
        vsel = at("vsel", [P, NPG, P], F32, H)
        phi = at("phi", [P, CL, P], F32, I)
        cc = at("cc", [P, 2, CC_T], F32, I + 4096)
        page = at("page", [P, 2, 768], F32, I + 4096 + 2 * CC_T)
        cst = at("cst", [P, 3, CH], F32, I + 4096 + 2 * CC_T)
        oh = at("oh", [P, G, NT], F32R, I)
        ol = at("ol", [P, G, NT], F32R, I + G * NT)
        probs = at("probs", [P, 3, 512], F32, I + 4608)
        pT = at("pT", [P, 3, 512], F32, I + 6144)
        pcT = at("pcT", [NCP, 2, HEADS, P], F32, I + 7680)
        sc = at("sc", [P, HEADS, NCP], F32, I + 9728)
        se = at("se", [P, HEADS, NCP], F32, I + 9728 + 256)
        sm = at("sm", [P, HEADS, NCP], F32, I + 9728 + 512)
        ext = at("ext", [P, CT, EXT], F32, J)
        yc = at("yc", [P, CT, NT], F32, J + CT * EXT)
        lnsq = at("lnsq", [P, CT, NT], F32, DD)
        lnv = at("lnv", [P, NT], F32, DD + CT * NT)
        lnr = at("lnr", [P, NT], F32, DD + CT * NT + NT)
        ch = at("ch", [P, CT, NT], F32R, FV)
        cl = at("cl", [P, CT, NT], F32R, FV + CT * NT)
        mh = at("mh", [P, KT, NT], F32R, C)
        ml = at("ml", [P, KT, NT], F32R, C + KT * NT)
        ms = at("ms", [P, 2, 2, NT], F32, J)
        msum = at("msum", [P, 2, NT], F32, J + 4 * NT)
        hb = at("hb", [P, TT, D], F32, FV)
        sf = at("sf", [2 * DB, 2 * FF], F32, H)
        gpost = at("gpost", [P, D], F32, H + 2 * FF)
        junk = at("junk", [P, TT, D], F32, H + 2 * FF + D)
        x1 = at("x1", [P, TT, D], F32, K - TT * D)
        hh = at("hh", [P, FT, NT], F32R, C)
        hl = at("hl", [P, FT, NT], F32R, C + FT * NT)
        u = at("u", [P, 2, UEXT], F32, C + 2 * FT * NT)
        U2 = C + 2 * FT * NT + (2 * UEXT + 7) // 8 * 8
        cv = at("cv", [P, 2, CEXT], F32, U2)
        hs = at("hs", [P, NT], F32, U2 + 2 * CEXT)
        ulast = at("ulast", [P, 2 * FT, 18], F32, U2 + 2 * CEXT + NT)
        assert U2 + 2 * CEXT + NT + 2 * FT * 18 <= K - TT * D
        fb = at("fb", [P, TT, D], F32, A)
        ustage = at("ustage", [18, 2 * FF], F32, A + 2 * KT * NT - 2 * FF)
        junk2 = at("junk2", [P, 4, D], F32, A + TT * D)
        gpost2 = at("gpost2", [P, D], F32, C + 2 * FT * NT)
        junk3 = at("junk3", [P, D], F32, C + 2 * FT * NT + D)

        used = [K]

        def small(name, shape, dt=F32):
            cols = 1
            for d in shape[1:]:
                cols *= d
            if dt == BF16:
                cols = (cols + 1) // 2
            t = at(name, shape, dt, used[0])
            used[0] += (cols + 7) // 8 * 8
            return t

        ident = small("ident", [P, P])
        identb = small("identb", [P, P], BF16)
        causal = small("causal", [P, P], BF16)
        rowsel = small("rowsel", [P, 2, P])
        newmask = small("newmask", [P, NS])
        cmpmask = small("cmpmask", [P, DB * NCS])
        rselT = small("rselT", [G, P])
        rsel = small("rsel", [P, G])
        cneg = small("cneg", [P, 4, NCP])
        c01 = small("c01", [P, 4, NCP])
        mean_w = small("mean_w", [P, P])
        par = small("par", [P, P_ALL])
        bphi = small("bphi", [P, 2])
        ss = small("ss", [P, TT])
        rstd = small("rstd", [P, TT])
        nmax = small("nmax", [P, NU])
        esum = small("esum", [P, NU])
        rinv = small("rinv", [P, NU])
        gtok = small("gtok", [P, TT, 24])
        gsel4 = small("gsel4", [P, 2, 6, G])
        gsel = small("gsel", [P, 2, 6])
        kcmp = small("kcmp", [P, NCP + DB * NCS])
        vcmpT = small("vcmpT", [P, NCP + DB * NCS])
        vcp = small("vcp", [NCP, P])
        vcs = small("vcs", [DB * NCS, P])
        qs = small("qs", [P, 2, P])
        cmax = small("cmax", [P, HEADS])
        csum = small("csum", [P, HEADS])
        cgate = small("cgate", [P, HEADS])
        ptab = small("ptab", [1, NPG], I32)
        sfT = small("sfT", [P, 2 * FT, 2 * DB])
        assert base + 4 * used[0] <= nc.sbuf_usable_end, (base + 4 * used[0], nc.sbuf_usable_end)

        ps = ctx.enter_context(nc.psum_tensor("ps", [P, 8, 512], F32))
        pf = ps[:, :, :].rearrange("p b n -> p (b n)")
        LO = 512 - HALF

        def pair(q, a=0, b=NT, m=P):
            return pf[0:m, 1024 * q + LO + a:1024 * q + LO + b]

        def sem(name):
            return ctx.enter_context(nc.semaphore(name))

        raw_in = [sem("raw_in0"), sem("raw_in1")]
        hi_done = sem("hi_done")
        lo_done = sem("lo_done")
        slot_used = sem("slot_used")
        par_in = sem("par_in")
        scv_in = sem("scv_in")
        x_in = sem("x_in")
        ptab_in = sem("ptab_in")
        bphi_in = sem("bphi_in")
        page_in = [sem("page_in0"), sem("page_in1")]
        phi_in = sem("phi_in")
        pool_init = sem("pool_init")
        const_ok = sem("const_ok")
        par_t = sem("par_t")
        par_ok = sem("par_ok")
        scv_t = sem("scv_t")
        hist_ok = sem("hist_ok")
        sq_done = sem("sq_done")
        rs_step = sem("rs_step")
        rs_ok = sem("rs_ok")
        xn_ok = sem("xn_ok")
        z_full = sem("z_full")
        zhi_ok = sem("zhi_ok")
        z_ok = sem("z_ok")
        past_t = sem("past_t")
        past_ev = sem("past_ev")
        vcopy = sem("vcopy")
        sg_ok = sem("sg_ok")
        glu_ok = sem("glu_ok")
        ext0 = sem("ext0")
        glu_p = sem("glu_p")
        conv_n = sem("conv_n")
        kv_ok = sem("kv_ok")
        cc_ok = sem("cc_ok")
        q_ok = sem("q_ok")
        gt_ok = sem("gt_ok")
        mid_t = sem("mid_t")
        gtok_ok = sem("gtok_ok")
        ktok_t = sem("ktok_t")
        ktok_ok = sem("ktok_ok")
        cst_t = sem("cst_t")
        cst_ok = sem("cst_ok")
        cst_out = sem("cst_out")
        kv_out = sem("kv_out")
        win_out = sem("win_out")
        cmp_mm = sem("cmp_mm")
        cmp_ok = sem("cmp_ok")
        vc_t = sem("vc_t")
        vc_ok = sem("vc_ok")
        rsel_ok = sem("rsel_ok")
        gsel_mm = sem("gsel_mm")
        gsel_ok = sem("gsel_ok")
        qs_ok = sem("qs_ok")
        s_full = sem("s_full")
        nmax_ok = sem("nmax_ok")
        exp_ok = sem("exp_ok")
        rinv_ok = sem("rinv_ok")
        scaled = sem("scaled")
        pt_full = sem("pt_full")
        pt_part = sem("pt_part")
        pt_ok = sem("pt_ok")
        pv_done = sem("pv_done")
        cs_half = sem("cs_half")
        cs_full = sem("cs_full")
        cs_step = sem("cs_step")
        ce_in = sem("ce_in")
        ce_ok = sem("ce_ok")
        pc_ok = sem("pc_ok")
        pct_full = sem("pct_full")
        pct_ok = sem("pct_ok")
        oh_ok = sem("oh_ok")
        ol_ok = sem("ol_ok")
        ln_mean = sem("ln_mean")
        ln_xc = sem("ln_xc")
        ln_sq = sem("ln_sq")
        ln_var = sem("ln_var")
        ln_step = sem("ln_step")
        ln_rs = sem("ln_rs")
        ln_xn = sem("ln_xn")
        silu_ok = sem("silu_ok")
        c_step = sem("c_step")
        m_attn = sem("m_attn")
        m_sig = sem("m_sig")
        m_mul = sem("m_mul")
        m_sum = sem("m_sum")
        m_hi = sem("m_hi")
        m_ok = sem("m_ok")
        x1_in = sem("x1_in")
        sf_in = sem("sf_in")
        gp_in = sem("gp_in")
        o_ev = sem("o_ev")
        sf_t = sem("sf_t")
        sf_ok = sem("sf_ok")
        sq2 = sem("sq2")
        rs2_step = sem("rs2_step")
        rs2 = sem("rs2")
        x1_step = sem("x1_step")
        sq3 = sem("sq3")
        rs3_step = sem("rs3_step")
        rs3 = sem("rs3")
        xn2 = sem("xn2")
        z2_full = sem("z2_full")
        z2_hi = sem("z2_hi")
        z2_ok = sem("z2_ok")
        u_ev = [sem("u_ev0"), sem("u_ev1")]
        u_hist = sem("u_hist")
        u_kept = sem("u_kept")
        u_pad = sem("u_pad")
        cv_step = sem("cv_step")
        act_ok = sem("act_ok")
        h_mul = sem("h_mul")
        h_hi = sem("h_hi")
        h_ok = sem("h_ok")
        ul_t = sem("ul_t")
        ul_ev = sem("ul_ev")
        ffn_out = sem("ffn_out")
        d_ev = sem("d_ev")
        gp2_in = sem("gp2_in")
        sq4 = sem("sq4")
        rs4_step = sem("rs4_step")
        rs4 = sem("rs4")
        y_step = sem("y_step")
        y_out = sem("y_out")

        w_in_v = w_in[0].rearrange("(k p) n -> p k n", p=P)
        w_up_v = w_up[0].rearrange("(k p) n -> p k n", p=P)
        w_ao_v = w_attn_out[0].rearrange("(g r h) n -> g h r n", g=KVH, r=G)
        w_co_v = w_conv_out[0].rearrange("(k p) n -> p k n", p=P)
        w_out_v = w_out[0].rearrange("(k p) n -> p k n", p=P)
        w_down_v = w_down[0].rearrange("(k p) n -> p k n", p=P)
        xs_v = x_sample.rearrange("b t d -> (b t) d")
        ys_v = y_sample.rearrange("b t d -> (b t) d")
        cache_v = cache_kv[0].rearrange("n t a g h -> n t (a g h)")
        swin_v = state_kv_win[0].rearrange("b (j t) a g h -> (b j) t (a g h)", t=PAGE)
        kvp_v = kv_prompt[0, 0].rearrange("t a g h -> t (a g h)")
        kvs_v = kv_sample[0].rearrange("b t a g h -> (b t) (a g h)")
        winp_v = win_prompt[0, 0].rearrange("t a g h -> t (a g h)")
        wins_v = win_sample[0].rearrange("b t a g h -> b t (a g h)")
        rawk = raw[:, :, :].rearrange("p s (k n) -> p s k n", n=P)
        whk = wh[:, :, :].rearrange("p s (k n) -> p s k n", n=P)
        wlk = wl[:, :, :].rearrange("p s (k n) -> p s k n", n=P)
        rawc = raw[:, :, :].rearrange("p s (k n) -> p s k n", n=512)
        whc = wh[:, :, :].rearrange("p s (k n) -> p s k n", n=512)
        wlc = wl[:, :, :].rearrange("p s (k n) -> p s k n", n=512)

        def mrg_step(b):
            return sum(MRG_DMAS[j % 3] for j in range(6) if (S_MRG + j) % 2 == b)

        def mrg_raw(j):
            return raw_value(S_MRG + j)

        block = ctx.enter_context(nc.Block())

        @block.sync
        def _(sp):
            for i in range(4):
                sp.dma_start(x[:, i, :], x_prompt[0, i * P:(i + 1) * P, :]).then_inc(x_in, 16)
            sp.dma_start(x[0:NS, 4, :], xs_v).then_inc(x_in, 16)

            def ring_free(s):
                sp.wait_ge(hi_done, s - 1)
                sp.wait_ge(lo_done, s - 1)

            def col_tile(s, v, c0, n=P):
                if s >= 2:
                    ring_free(s)
                dst = rawk[:, s % 2] if n == P else raw[:, s % 2, 0:KT * n].rearrange("p (k n) -> p k n", n=n)
                sp.dma_start(dst, v[:, :, c0:c0 + n]).then_inc(raw_in[s % 2], 16)

            for c in range(CT):
                col_tile(S_GLU + 2 * c, w_in_v, OFF_GLU + CH + c * P)
                col_tile(S_GLU + 2 * c + 1, w_in_v, OFF_GLU + c * P)
            for j in range(6):
                col_tile(S_KV + j, w_in_v, OFF_KV + j * P)
            for r in range(G):
                s = S_Q + r
                ring_free(s)
                for g in range(KVH):
                    c0 = (g * G + r) * HD
                    sp.dma_start(rawk[:, s % 2, :, g * HD:(g + 1) * HD], w_in_v[:, :, c0:c0 + HD])\
                      .then_inc(raw_in[s % 2], 16)
            col_tile(S_GATE, w_in_v, OFF_GATE, 24)
            with sp.Fori(0, KT // 2) as i:
                for j in range(6):
                    b = (S_MRG + j) % 2
                    c1 = sp.snap((2 * i + j // 3 + 1) * P + (OFF_MRG + (j % 3) * D if j % 3 < 2 else 0))
                    split = sp.snap(6 * i + (S_MRG + j - 1))
                    sp.wait_ge(lo_done, split)
                    if j % 3 < 2:
                        sp.dma_start(rawk[:, b], w_in_v[:, :, bass.ds(c1 - P, P)]).then_inc(raw_in[b], 16)
                    else:
                        for g in range(KVH):
                            sp.dma_start(rawk[g * HD:(g + 1) * HD, b, 0:G], w_ao_v[g, :, :, bass.ds(c1 - P, P)])\
                              .then_inc(raw_in[b], 16)
                        sp.dma_start(rawk[:, b, G:KT], w_co_v[:, :, bass.ds(c1 - P, P)]).then_inc(raw_in[b], 16)
            for half in range(2):
                for kc in range(KT // 2):
                    s = S_OUT + half * (KT // 2) + kc
                    ring_free(s)
                    sp.dma_start(rawc[:, s % 2], w_out_v[:, 2 * kc:2 * kc + 2, half * 512:(half + 1) * 512])\
                      .then_inc(raw_in[s % 2], 16)
            with sp.Fori(0, FT) as i:
                for j in range(2):
                    b = (S_UP + j) % 2
                    c1 = sp.snap((i + 1) * P + j * FF)
                    split = sp.snap(2 * i + (S_UP + j - 1))
                    sp.wait_ge(lo_done, split)
                    sp.dma_start(rawk[:, b], w_up_v[:, :, bass.ds(c1 - P, P)]).then_inc(raw_in[b], 16)
            for half in range(2):
                for kc in range(FT // 2):
                    s = S_DOWN + half * (FT // 2) + kc
                    ring_free(s)
                    sp.dma_start(rawc[:, s % 2], w_down_v[:, 2 * kc:2 * kc + 2, half * 512:(half + 1) * 512])\
                      .then_inc(raw_in[s % 2], 16)
            for i in range(TT):
                sp.wait_ge(y_step, 2 * (i + 1))
                dst = y_prompt[0, i * P:(i + 1) * P, :] if i < 4 else ys_v
                sp.dma_start(dst, x1[0:ROWS[i], i, :]).then_inc(y_out, 16)
            sp.wait_ge(y_out, 16 * TT)

        @block.gpsimd
        def _(pool):
            pool.dma_start(ptab[:, :], page_table.rearrange("b j -> (b j)").unsqueeze(0)).then_inc(ptab_in, 16)
            init = [0]

            def fill(t, v):
                pool.wait_ge(pool_init, init[0])
                nc.gpsimd.memset(t, v).then_inc(pool_init, 1)
                init[0] += 1

            def select(t, op, fillv, b0, pattern, cm):
                pool.wait_ge(pool_init, init[0])
                nc.gpsimd.affine_select(out=t, in_=t, compare_op=op, fill=fillv, base=b0, pattern=pattern,
                                        channel_multiplier=cm).then_inc(pool_init, 1)
                init[0] += 1

            fill(ident[:, :], 0.0)
            select(ident[:, :], ALU.not_equal, 1.0, 0, [[-1, P]], 1)
            pool.wait_ge(pool_init, init[0])
            nc.gpsimd.tensor_copy(identb[:, :], ident[:, :]).then_inc(const_ok, 1)
            pool.wait_ge(ptab_in, 16)

            def load_page(n):
                if n >= 2:
                    pool.wait_ge(past_t, n - 1)
                    pool.wait_ge(vcopy, 2 * (n - 1))
                pg = pool.value_load(ptab[0:1, n:n + 1], min_val=0, max_val=cache_kv.shape[1] - 1)
                pool.dma_start(page[:, n % 2, 0:512], cache_v[bass.ds(pg, 1)].rearrange("a t n -> (a t) n"))\
                    .then_inc(page_in[n % 2], 16)
                pool.dma_start(page[:, n % 2, 512:768], swin_v[n]).then_inc(page_in[n % 2], 16)

            load_page(0)
            load_page(1)
            fill(causal[:, :], 0.0)
            select(causal[:, :], ALU.is_ge, NEG, 0, [[-1, P]], 1)
            fill(rowsel[:, :, :], 1.0)
            for g in range(KVH):
                select(rowsel[g * HD:(g + 1) * HD, :, :].rearrange("k h p -> k (h p)"), ALU.is_equal, 0.0, 0,
                       [[-DT, DB], [0, G], [-1, DT]], 1)
            fill(newmask[:, :], 0.0)
            for g in range(KVH):
                rows = slice(g * HD, (g + 1) * HD)
                select(newmask[rows, :], ALU.is_ge, NEG, 0, [[-1, NS]], 1)
                select(newmask[rows, :], ALU.is_ge, NEG, DT - 1, [[DT, DB], [0, DT]], -1)
            fill(cmpmask[:, :], 0.0)
            for g in range(KVH):
                rows = slice(g * HD, (g + 1) * HD)
                select(cmpmask[rows, :], ALU.is_ge, NEG, 0, [[-DT, DB], [0, NCS]], 1)
                select(cmpmask[rows, :], ALU.is_ge, NEG, DT - 1, [[DT, DB], [0, NCS]], -1)
            fill(rselT[:, :], 1.0)
            select(rselT[:, :], ALU.is_equal, 0.0, 0, [[0, 4], [-1, G], [0, DT]], 1)
            fill(cneg[:, :, :], 0.0)
            select(cneg[:, :, :], ALU.is_ge, NEG, 1 - CL, [[P, 4], [-CS, NCP]], 1)
            fill(c01[:, :, :], 1.0)
            select(c01[:, :, :], ALU.is_ge, 0.0, 1 - CL, [[P, 4], [-CS, NCP]], 1)
            fill(phi[:, :, :], 0.0)
            pool.wait_ge(pool_init, init[0])
            nc.gpsimd.memset(mean_w[:, :], 1.0 / CH).then_inc(const_ok, 1)

            def load_phi(w):
                for g in range(KVH):
                    pool.dma_start(phi[g * HD:(g + 1) * HD, :, g * HD:(g + 1) * HD],
                                   w[0].rearrange("(l h) e -> h l e", h=HD)).then_inc(phi_in, 16)

            load_phi(w_phi_k)
            for g in range(KVH):
                for q, b in enumerate((b_phi_k, b_phi_v)):
                    pool.dma_start(bphi[g * HD:(g + 1) * HD, q:q + 1], b[0].unsqueeze(1)).then_inc(bphi_in, 16)
            for n in range(NPG):
                pool.wait_ge(page_in[n % 2], 32 * (n // 2 + 1))
                nc.gpsimd.tensor_copy(vsel[:, n, :], page[:, n % 2, 384:512]).then_inc(vcopy, 1)
                nc.gpsimd.tensor_copy(vwin[:, n, :], page[:, n % 2, 640:768]).then_inc(vcopy, 1)
                if n + 2 < NPG:
                    load_page(n + 2)
            pool.dma_start(wins_v[:, 0:PAST, :], state_kv_win[0].rearrange("b t a g h -> b t (a g h)"))\
                .then_inc(win_out, 16)
            for j in range(2):
                pool.wait_ge(kv_ok, j + 1)
                nc.gpsimd.tensor_copy(cc[:, j, 0:SEQ], kvT[:, j, 0:SEQ]).then_inc(cc_ok, 1)
            pool.wait_ge(q_ok, G)
            nc.gpsimd.tensor_copy(qs[:, :, :].rearrange("p h (b r t) -> p (h b) r t", r=G, t=DT),
                                  qT[:, :, SEQ:NT].rearrange("p r (b t) -> p b r t", t=DT)).then_inc(qs_ok, 1)
            for i in range(TT):
                pool.wait_ge(ktok_ok, i + 1)
                if i < 4:
                    pool.dma_start(kvp_v[i * P:(i + 1) * P, :], ktok[:, i, 0:512]).then_inc(kv_out, 16)
                    pool.dma_start(winp_v[i * P:(i + 1) * P, :], ktok[:, i, 512:768]).then_inc(kv_out, 16)
                else:
                    pool.dma_start(kvs_v, ktok[0:NS, i, 0:512]).then_inc(kv_out, 16)
                    for b in range(DB):
                        pool.dma_start(wins_v[b, PAST:PAST + DT, :], ktok[b * DT:(b + 1) * DT, i, 512:768])\
                            .then_inc(kv_out, 16)
            pool.wait_ge(cmp_mm, 1)
            load_phi(w_phi_v)
            pool.wait_ge(cst_ok, 4)
            pool.dma_start(conv_prompt[0, 0], cst[96:96 + HIST, 2, :]).then_inc(cst_out, 16)
            for b in range(DB):
                r0 = (b % 3) * SB_S + DT
                pool.dma_start(conv_sample[0, b], cst[r0:r0 + HIST, b // 3, :]).then_inc(cst_out, 16)
            for n, (q, r, g, c) in enumerate(UNITS):
                pool.wait_ge(rinv_ok, n + 1)
                gate = gtok[:, q, c * HEADS + g * G + r:c * HEADS + g * G + r + 1] if q < 4 \
                    else gsel[:, q - 4, c * KVH + g:c * KVH + g + 1]
                w = probs[:, n % 3, 0:width(n)]
                nc.gpsimd.tensor_scalar(w, w, rinv[:, n:n + 1], gate, ALU.mult, ALU.mult).then_inc(scaled, 1)
            with pool.Fori(0, KT // 2) as i:
                for j in range(2):
                    pool.wait_ge(m_ok, 2 * i + j)
                    pool.wait_ge(m_mul, 4 * i + 2 * j + 2)
                    nc.gpsimd.tensor_tensor(msum[:, j, :], ms[:, j, 0, :], ms[:, j, 1, :], ALU.add)\
                        .then_inc(m_sum, 1)
            pool.wait_ge(m_ok, KT)
            for i in range(TT):
                src = x_prompt[0, i * P:(i + 1) * P, :] if i < 4 else xs_v
                pool.dma_start(x1[0:ROWS[i], i, :], src).then_inc(x1_in, 16)
            pool.wait_ge(slot_used, S_OUT)
            pool.dma_start(sf[:, :], state_ffn[0].rearrange("b t f -> (b t) f")).then_inc(sf_in, 16)
            pool.dma_start(gpost[:, :], g_mix_post[0].partition_broadcast(P)).then_inc(gp_in, 16)
            with pool.Fori(0, FT) as i:
                pool.wait_ge(h_ok, i)
                pool.wait_ge(cv_step, 6 * i + 6)
                pool.wait_ge(act_ok, i + 1)
                nc.gpsimd.tensor_tensor(hs[:, 0:SEQ], cv[:, 0, 0:SEQ], cv[:, 1, 0:SEQ], ALU.mult)\
                    .then_inc(h_mul, 1)
                nc.gpsimd.tensor_tensor(
                    hs[:, SEQ:NT].rearrange("p (b t) -> p b t", t=DT),
                    cv[:, 0, SEQ:CEXT].rearrange("p (b t) -> p b t", t=DT + 2)[:, :, 2:DT + 2],
                    cv[:, 1, SEQ:CEXT].rearrange("p (b t) -> p b t", t=DT + 2)[:, :, 2:DT + 2],
                    ALU.mult).then_inc(h_mul, 1)
            pool.wait_ge(h_ok, FT)
            pool.dma_start(gpost2[:, :], g_ffn_post[0].partition_broadcast(P)).then_inc(gp2_in, 16)
            pool.wait_ge(ul_ev, 11)
            pool.dma_start(ffn_prompt[0, 0], ustage[0:2, :]).then_inc(ffn_out, 16)
            pool.dma_start(ffn_sample[0].rearrange("b t f -> (b t) f"), ustage[2:18, :]).then_inc(ffn_out, 16)
            pool.wait_ge(win_out, 16)
            pool.wait_ge(kv_out, 16 * (4 * 2 + 1 + DB))
            pool.wait_ge(cst_out, 16 * (1 + DB))
            pool.wait_ge(ffn_out, 32)

        @block.scalar
        def _(act):
            v = ffn_conv_w[0].rearrange("w (t p) -> (w t) p", p=P)
            act.dma_start(par_raw[:, 0, :], v[0:P, :]).then_inc(par_in, 16)
            act.dma_start(par_raw[0:P_CW - P, 1, :], v[P:P_CW, :]).then_inc(par_in, 16)
            act.dma_start(par_raw[P_CW - P:P_FB - P, 1, :], conv_w[0].rearrange("w (t p) -> (w t) p", p=P))\
                .then_inc(par_in, 16)
            for vec, col in ((ffn_conv_b, P_FB), (conv_b, P_CB), (g_mix_pre, P_GPRE), (g_ffn_pre, P_GFFN),
                             (conv_ln_g, P_LNG), (conv_ln_b, P_LNB)):
                rows = vec[0].rearrange("(t p) -> t p", p=P)
                act.dma_start(par_raw[col - 2 * P:col - 2 * P + rows.shape[0], 2, :], rows).then_inc(par_in, 16)
            for hf in range(2):
                act.dma_start(scv[0:4 * HIST, hf, :], state_conv[0, 4 * hf:4 * hf + 4].rearrange("b t c -> (b t) c"))\
                    .then_inc(scv_in, 16)

            def hi(s):
                act.wait_ge(raw_in[s % 2], raw_value(s))
                if s >= 2:
                    act.wait_ge(slot_used, s - 1)
                n = KT * 24 if s == S_GATE else 1024
                nc.scalar.copy(wh[:, s % 2, 0:n], raw[:, s % 2, 0:n]).then_inc(hi_done, 1)

            act.wait_ge(x_in, 16 * TT)
            act.wait_ge(rs_step, 1)
            for i in range(TT):
                nc.scalar.activation(sq_x[0:ROWS[i], i, :], x[0:ROWS[i], i, :], ACT.Square,
                                     accum_out=ss[0:ROWS[i], i:i + 1]).then_inc(sq_done, 1)
            act.wait_ge(rs_step, 3)
            nc.scalar.activation(rstd[:, :], ss[:, :], ACT.Sqrt).then_inc(rs_ok, 1)
            hi(0)
            hi(1)
            act.wait_ge(par_ok, 2)
            act.wait_ge(sq_done, TT)
            for k in range(KT):
                act.wait_ge(z_full, k + 1)
                nc.scalar.activation(zh[:, k, :], pf[:, 1024 * (k % 2):1024 * (k % 2) + NT], ACT.Copy,
                                     scale=par[:, P_GPRE + k:P_GPRE + k + 1]).then_inc(zhi_ok, 1)
            for s in range(S_MRG):
                if s + 1 < S_MRG and s > 0:
                    hi(s + 1)
                e = s
                act.wait_ge(slot_used, s + 1)
                if s < S_KV:
                    if s % 2 == 0:
                        act.wait_ge(glu_p, s // 2)
                        act.wait_ge(glu_ok, s // 2)
                        nc.scalar.activation(sg[:, :], pair(e % 2), ACT.Sigmoid).then_inc(sg_ok, 1)
                elif s < S_Q:
                    nc.scalar.copy(kvT[:, s - S_KV, :], pair(e % 2)).then_inc(kv_ok, 1)
                elif s < S_GATE:
                    nc.scalar.mul(qT[:, s - S_Q, :], pair(e % 2), HD ** -0.5).then_inc(q_ok, 1)
                else:
                    nc.scalar.activation(gT[:, :], pair(e % 2, m=24), ACT.Sigmoid).then_inc(gt_ok, 1)
            act.wait_ge(mid_t, 1)
            nc.scalar.copy(gtok[:, 0:4, :], ps[:, 4, 0:96].rearrange("p (i c) -> p i c", c=24)).then_inc(gtok_ok, 1)
            nc.scalar.copy(gtok[0:NS, 4, :], ps[0:NS, 4, 96:120]).then_inc(gtok_ok, 1)
            act.wait_ge(vcopy, 2 * NPG)
            act.wait_ge(cst_t, 1)
            nc.scalar.copy(cst[96:96 + HIST, 2, :], ps[0:HIST, 5, :]).then_inc(cst_ok, 1)
            for q, (_, nb) in enumerate(SEQ_GROUPS):
                act.wait_ge(cst_t, q + 2)
                nc.scalar.copy(cst[0:nb * SB_S, q, :], ps[0:nb * SB_S, 5 + (q + 1) % 3, :]).then_inc(cst_ok, 1)
            for i in range(TT):
                act.wait_ge(ktok_t, i + 1)
                b0 = 1024 * (i % 2)
                nc.scalar.copy(ktok[0:ROWS[i], i, :], pf[0:ROWS[i], b0:b0 + 768]).then_inc(ktok_ok, 1)
            act.wait_ge(bphi_in, 64)
            for j, dst in enumerate((kcmp, vcmpT)):
                act.wait_ge(cmp_mm, j + 1)
                nc.scalar.activation(dst[:, 0:NCP], ps[:, 4 + j, 0:NCP], ACT.Identity, bias=bphi[:, j:j + 1])\
                    .then_inc(cmp_ok, 1)
                nc.scalar.activation(
                    dst[:, NCP:].rearrange("p (b n) -> p b n", n=NCS),
                    ps[:, 4 + j, SEQ // CS:SEQ // CS + DB * PAST // CS].rearrange("p (b n) -> p b n", b=DB)[:, :, 0:NCS],
                    ACT.Identity, bias=bphi[:, j:j + 1]).then_inc(cmp_ok, 1)
            act.wait_ge(vc_t, 1)
            nc.scalar.copy(vcp[:, :], ps[0:NCP, 6, 0:P]).then_inc(vc_ok, 1)
            nc.scalar.copy(vcs[:, :], ps[0:DB * NCS, 6, P:2 * P]).then_inc(vc_ok, 1)

            def cmp_exp(i):
                act.wait_ge(ce_in, i + 1)
                if i >= 1:
                    act.wait_ge(pc_ok, i)
                nc.scalar.activation(se[:, :, :], sc[:, :, :], ACT.Exp).then_inc(ce_ok, 1)

            act.wait_ge(cst_out, 16 * (1 + DB))
            cmp_exp(0)
            for n in range(NU + 4):
                if n < NU:
                    act.wait_ge(nmax_ok, n + 1)
                    if n >= 3:
                        act.wait_ge(pt_full, n - 2)
                    nc.scalar.activation(probs[:, n % 3, 0:width(n)], ps[:, n % 3, 0:width(n)], ACT.Exp,
                                         bias=nmax[:, n:n + 1], accum_out=esum[:, n:n + 1]).then_inc(exp_ok, 1)
                for i in range(1, 4):
                    if n == FIRST[i] - 6:
                        cmp_exp(i)
                for q in range(6):
                    if n == LAST[q] + 3:
                        act.wait_ge(pv_done, LAST[q] + 1)
                        if q < 4:
                            nc.scalar.copy(oh[:, :, q * P:(q + 1) * P],
                                           ps[:, 5 + q % 2, :].rearrange("p (r t) -> p r t", r=G)).then_inc(oh_ok, 1)
                        else:
                            t0 = SEQ + (q - 4) * (NS // 2)
                            nc.scalar.copy(oh[:, :, t0:t0 + NS // 2].rearrange("p r (b t) -> p b r t", t=DT),
                                           ps[:, 5 + q % 2, 0:P].rearrange("p (b r t) -> p b r t", r=G, t=DT))\
                                .then_inc(oh_ok, 1)
            for c in range(CT):
                act.wait_ge(ln_xc, c + 1)
                nc.scalar.activation(lnsq[:, c, :], yc[:, c, :], ACT.Square).then_inc(ln_sq, 1)
            act.wait_ge(ln_step, 2)
            nc.scalar.activation(lnr[:, :], lnv[:, :], ACT.Sqrt).then_inc(ln_rs, 1)
            act.wait_ge(ln_var, 1)
            for c in range(CT):
                act.wait_ge(ln_xn, c + 1)
                nc.scalar.activation(lnsq[:, c, :], yc[:, c, :], ACT.Silu, bias=par[:, P_LNB + c:P_LNB + c + 1],
                                     scale=par[:, P_LNG + c:P_LNG + c + 1]).then_inc(silu_ok, 1)
            hi(S_MRG)
            with act.Fori(0, KT // 2) as i:
                for j in range(6):
                    b = (S_MRG + j + 1) % 2
                    act.wait_ge(raw_in[b], 16 * mrg_step(b) * i + mrg_raw(j + 1))
                    act.wait_ge(slot_used, 6 * i + (S_MRG + j))
                    nc.scalar.copy(wh[:, b, :], raw[:, b, :]).then_inc(hi_done, 1)
                    if j % 3 < 2:
                        act.wait_ge(m_sum, 2 * i + j // 3)
                        act.wait_ge(slot_used, 6 * i + (S_MRG + j + 1))
                        nc.scalar.activation(ms[:, j // 3, j % 3, :], pair(j % 3), ACT.Sigmoid).then_inc(m_sig, 1)

            for half in range(2):
                for kc in range(KT // 2):
                    s = S_OUT + half * (KT // 2) + kc
                    hi(s + 1)
                for i in range(TT):
                    act.wait_ge(slot_used, S_OUT + (half + 1) * (KT // 2))
                    bk = (half * TT + i) % 8
                    nc.scalar.copy(hb[0:ROWS[i], i, half * 512:(half + 1) * 512], ps[0:ROWS[i], bk, :])\
                        .then_inc(o_ev, 1)
            act.wait_ge(o_ev, 2 * TT)
            for i in range(TT):
                nc.scalar.activation(junk[0:ROWS[i], i, :], hb[0:ROWS[i], i, :], ACT.Square,
                                     accum_out=ss[0:ROWS[i], i:i + 1]).then_inc(sq2, 1)
            act.wait_ge(rs2_step, 2)
            nc.scalar.activation(rstd[:, :], ss[:, :], ACT.Sqrt).then_inc(rs2, 1)
            act.wait_ge(rs2, 1)
            for i in range(TT):
                act.wait_ge(x1_step, 2 * i + 2)
                nc.scalar.activation(junk[0:ROWS[i], i, :], x1[0:ROWS[i], i, :], ACT.Square,
                                     accum_out=ss[0:ROWS[i], i:i + 1]).then_inc(sq3, 1)
            act.wait_ge(rs3_step, 2)
            nc.scalar.activation(rstd[:, :], ss[:, :], ACT.Sqrt).then_inc(rs3, 1)
            for k in range(KT):
                act.wait_ge(z2_full, k + 1)
                nc.scalar.activation(zh[:, k, :], pf[:, 1024 * (k % 2):1024 * (k % 2) + NT], ACT.Copy,
                                     scale=par[:, P_GFFN + k:P_GFFN + k + 1]).then_inc(z2_hi, 1)
            act.wait_ge(u_pad, 1)
            with act.Fori(0, FT) as i:
                for j in range(2):
                    b = (S_UP + j + 1) % 2
                    act.wait_ge(raw_in[b], 16 * i + raw_value(S_UP + j + 1))
                    act.wait_ge(slot_used, 2 * i + (S_UP + j))
                    nc.scalar.copy(wh[:, b, :], raw[:, b, :]).then_inc(hi_done, 1)
                    act.wait_ge(cv_step, 6 * i)
                    act.wait_ge(slot_used, 2 * i + (S_UP + j + 1))
                    nc.scalar.copy(u[:, j, 2:2 + SEQ], pair(j, 0, SEQ)).then_inc(u_ev[j], 1)
                    nc.scalar.copy(u[:, j, 2 + SEQ:UEXT].rearrange("p (b t) -> p b t", t=DT + 2)[:, :, 2:DT + 2],
                                   pair(j, SEQ, NT).rearrange("p (b t) -> p b t", t=DT)).then_inc(u_ev[j], 1)
                act.wait_ge(cv_step, 6 * i + 3)
                nc.scalar.activation(cv[:, 0, :], cv[:, 0, :], ACT.Gelu_apprx_tanh).then_inc(act_ok, 1)

            for q in range(11):
                act.wait_ge(ul_t, q + 1)
                nc.scalar.copy(ustage[:, q * 512:(q + 1) * 512], ps[0:18, 5 + q % 3, :]).then_inc(ul_ev, 1)
            for half in range(2):
                for kc in range(FT // 2):
                    s = S_DOWN + half * (FT // 2) + kc
                    if s + 1 < S_END:
                        hi(s + 1)
                if half == 0:
                    act.wait_ge(ffn_out, 32)
                for i in range(TT):
                    act.wait_ge(slot_used, S_DOWN + (half + 1) * (FT // 2))
                    bk = (half * TT + i) % 8
                    nc.scalar.copy(fb[0:ROWS[i], i, half * 512:(half + 1) * 512], ps[0:ROWS[i], bk, :])\
                        .then_inc(d_ev, 1)
            act.wait_ge(d_ev, 2 * TT)
            act.wait_ge(gp2_in, 16)
            for i in range(TT):
                jk = junk2[0:ROWS[i], i, :] if i < 4 else junk3[0:ROWS[i], :]
                nc.scalar.activation(jk, fb[0:ROWS[i], i, :], ACT.Square,
                                     accum_out=ss[0:ROWS[i], i:i + 1]).then_inc(sq4, 1)
            act.wait_ge(rs4_step, 2)
            nc.scalar.activation(rstd[:, :], ss[:, :], ACT.Sqrt).then_inc(rs4, 1)

        @block.vector
        def _(dve):
            def lo(s):
                dve.wait_ge(hi_done, s + 1)
                n = KT * 24 if s == S_GATE else 1024
                nc.vector.tensor_tensor(wl[:, s % 2, 0:n], raw[:, s % 2, 0:n], wh[:, s % 2, 0:n].bitcast(F32),
                                        ALU.subtract).then_inc(lo_done, 1)

            nc.vector.memset(ss[:, :], 1.0).then_inc(rs_step, 1)
            nc.vector.memset(ext[:, :, 0:HIST], 0.0).then_inc(ext0, 1)
            dve.wait_ge(par_t, 1)
            nc.vector.tensor_copy(par[:, 0:2 * P], ps[:, 6, 0:2 * P]).then_inc(par_ok, 1)
            nc.vector.tensor_copy(par[:, 2 * P:P_ALL], ps[:, 6, 2 * P:P_ALL]).then_inc(par_ok, 1)
            for hf in range(2):
                dve.wait_ge(scv_t, hf + 1)
                for c in range(CT):
                    b0 = HIST + SEQ + 4 * hf * SB_S
                    nc.vector.tensor_copy(
                        ext[:, c, b0:b0 + 4 * SB_S].rearrange("p (b t) -> p b t", t=SB_S)[:, :, 0:HIST],
                        ps[:, 4 + hf, c * 120:(c + 1) * 120].rearrange("p (b t) -> p b t", t=HIST)).then_inc(hist_ok, 1)
            dve.wait_ge(sq_done, TT)
            nc.vector.tensor_scalar(ss[:, :], ss[:, :], 1.0 / D, EPS, ALU.mult, ALU.add).then_inc(rs_step, 1)
            dve.wait_ge(rs_step, 2)
            nc.vector.reciprocal(ss[:, :], ss[:, :]).then_inc(rs_step, 1)
            dve.wait_ge(rs_ok, 1)
            for i in range(TT):
                nc.vector.tensor_scalar(x[0:ROWS[i], i, :], x[0:ROWS[i], i, :], rstd[0:ROWS[i], i:i + 1], None,
                                        ALU.mult).then_inc(xn_ok, 1)
            for k in range(KT):
                dve.wait_ge(zhi_ok, k + 1)
                nc.vector.scalar_tensor_tensor(zl[:, k, :], pf[:, 1024 * (k % 2):1024 * (k % 2) + NT],
                                               par[:, P_GPRE + k:P_GPRE + k + 1], zh[:, k, :].bitcast(F32),
                                               ALU.mult, ALU.subtract).then_inc(z_ok, 1)
            lo(0)
            lo(1)

            def past(n):
                dve.wait_ge(past_t, n + 1)
                bk = 4 + n % 4
                nc.vector.tensor_copy(cc[:, :, SEQ + n * P:SEQ + (n + 1) * P],
                                      ps[:, bk, 0:256].rearrange("p (j t) -> p j t", j=2)).then_inc(past_ev, 1)
                nc.vector.tensor_copy(kpast[:, :, n * P:(n + 1) * P],
                                      ps[:, bk, 256:512].rearrange("p (j t) -> p j t", j=2)).then_inc(past_ev, 1)

            def conv(k0, k1):
                for k in range(k0, min(k1, 2 * CW)):
                    cp, l = k // CW, k % CW
                    for part in range(2):
                        for c in (2 * cp, 2 * cp + 1):
                            w = par[:, P_CW + l * CT + c:P_CW + l * CT + c + 1]
                            if part == 0:
                                src = ext[:, c, l:l + SEQ]
                                dst = yc[:, c, 0:SEQ]
                            else:
                                src = ext[:, c, HIST + SEQ:EXT].rearrange("p (b t) -> p b t", t=SB_S)[:, :, l:l + DT]
                                dst = yc[:, c, SEQ:NT].rearrange("p (b t) -> p b t", t=DT)
                            if l == 0:
                                if k == 0:
                                    dve.wait_ge(ext0, 1)
                                    dve.wait_ge(hist_ok, 2 * CT)
                                    dve.wait_ge(glu_p, CT)
                                    dve.wait_ge(glu_ok, CT)
                                nc.vector.tensor_scalar(dst, src, w, par[:, P_CB + c:P_CB + c + 1], ALU.mult,
                                                        ALU.add).then_inc(conv_n, 1)
                            else:
                                dve.wait_ge(conv_n, 4 * k + 2 * part + c % 2 + 1 - 4)
                                nc.vector.scalar_tensor_tensor(dst, src, w, dst, ALU.mult, ALU.add).then_inc(conv_n, 1)

            for s in range(S_MRG):
                if s + 1 < S_MRG and s > 0:
                    lo(s + 1)
                e = s
                if s < S_KV:
                    past(2 * s)
                    past(2 * s + 1)
                    if s % 2:
                        c = s // 2
                        dve.wait_ge(sg_ok, c + 1)
                        dve.wait_ge(slot_used, s + 1)
                        nc.vector.tensor_tensor(ext[:, c, HIST:HIST + SEQ], sg[:, 0:SEQ], pair(e % 2, 0, SEQ),
                                                ALU.mult).then_inc(glu_p, 1)
                        nc.vector.tensor_tensor(
                            ext[:, c, HIST + SEQ:EXT].rearrange("p (b t) -> p b t", t=SB_S)[:, :, HIST:SB_S],
                            sg[:, SEQ:NT].rearrange("p (b t) -> p b t", t=DT),
                            pair(e % 2, SEQ, NT).rearrange("p (b t) -> p b t", t=DT), ALU.mult)\
                            .then_inc(glu_ok, 1)
                else:
                    conv(4 * (s - S_KV), 4 * (s - S_KV + 1))
            conv(4 * (S_MRG - S_KV), 2 * CW)
            dve.wait_ge(gsel_mm, 1)
            nc.vector.tensor_copy(rsel[:, :], ps[:, 7, 256:256 + G]).then_inc(rsel_ok, 1)
            dve.wait_ge(rsel_ok, 1)
            for hf in range(2):
                nc.vector.tensor_tensor(
                    gsel4[:, hf], ps[:, 7, 32 * hf:32 * hf + 24].rearrange("p (c r) -> p c r", r=G),
                    rsel[:, :].unsqueeze(1).broadcast_to([P, 6, G]), ALU.mult).then_inc(rsel_ok, 1)
            dve.wait_ge(rsel_ok, 3)
            nc.vector.tensor_reduce(gsel[:, :, :].rearrange("p h c -> p (h c)"),
                                    gsel4[:, :, :, :].rearrange("p h c r -> p (h c) r"), AX.X, ALU.add)\
                .then_inc(gsel_ok, 1)
            dve.wait_ge(gsel_ok, 1)
            dve.wait_ge(cst_out, 16 * (1 + DB))

            cstep = [0]

            def link(ins):
                cstep[0] += 1
                ins.then_inc(cs_step, 1)
                dve.wait_ge(cs_step, cstep[0])

            def cmp_soft(i):
                dve.wait_ge(cs_full, i + 1)
                link(nc.vector.tensor_tensor(
                    sc[:, :, :], ps[:, 7, 0:HEADS * 32].rearrange("p (h n) -> p h n", n=32)[:, :, 0:NCP],
                    cneg[:, i, :].unsqueeze(1).broadcast_to([P, HEADS, NCP]), ALU.add))
                link(nc.vector.tensor_reduce(cmax[:, :], sc[:, :, :], AX.X, ALU.max))
                nc.vector.tensor_tensor(sc[:, :, :], sc[:, :, :],
                                        cmax[:, :].unsqueeze(2).broadcast_to([P, HEADS, NCP]),
                                        ALU.subtract).then_inc(ce_in, 1)

            def cmp_norm(i):
                dve.wait_ge(ce_ok, i + 1)
                if i >= 1:
                    dve.wait_ge(pct_full, 2 * i)
                link(nc.vector.tensor_tensor(se[:, :, :], se[:, :, :],
                                             c01[:, i, :].unsqueeze(1).broadcast_to([P, HEADS, NCP]), ALU.mult))
                link(nc.vector.tensor_reduce(csum[:, :], se[:, :, :], AX.X, ALU.add))
                link(nc.vector.tensor_scalar(csum[:, :], csum[:, :], TINY, None, ALU.max))
                link(nc.vector.reciprocal(csum[:, :], csum[:, :]))
                link(nc.vector.tensor_tensor(cgate[:, :], csum[:, :], gtok[:, i, 0:HEADS], ALU.mult))
                nc.vector.tensor_tensor(sm[:, :, :], se[:, :, :],
                                        cgate[:, :].unsqueeze(2).broadcast_to([P, HEADS, NCP]),
                                        ALU.mult).then_inc(pc_ok, 1)

            def cmp_turn(i, hf):
                dve.wait_ge(pct_full, 2 * i + hf + 1)
                if i >= 2:
                    dve.wait_ge(pv_done, LAST[i - 2] + 1)
                nc.vector.tensor_copy(pcT[:, i % 2, 4 * hf:4 * hf + 4, :].rearrange("p h t -> p (h t)"),
                                      ps[0:NCP, 7, :]).then_inc(pct_ok, 1)

            dve.wait_ge(gtok_ok, 2)
            cmp_soft(0)
            cmp_norm(0)
            cmp_turn(0, 0)
            cmp_turn(0, 1)
            for n in range(NU + 4):
                if n < NU:
                    dve.wait_ge(s_full, n + 1)
                    nc.vector.tensor_reduce(nmax[:, n:n + 1], ps[:, n % 3, 0:width(n)], AX.X, ALU.max, negate=True)\
                        .then_inc(nmax_ok, 1)
                if 1 <= n <= NU:
                    dve.wait_ge(exp_ok, n)
                    nc.vector.reciprocal(rinv[:, n - 1:n], esum[:, n - 1:n]).then_inc(rinv_ok, 1)
                if 2 <= n < NU + 2:
                    m = n - 2
                    q, _, _, c = UNITS[m]
                    dve.wait_ge(pt_full, m + 1)
                    if m >= 3:
                        dve.wait_ge(pv_done, m - 2)
                    if q < 4:
                        nc.vector.tensor_copy(pT[:, m % 3, 0:width(m)], ps[:, 3 + m % 2, 0:width(m)]).then_inc(pt_ok, 1)
                    elif c == 0:
                        nc.vector.tensor_copy(pT[0:DB * NCS, m % 3, 0:P], ps[0:DB * NCS, 3 + m % 2, 0:P])\
                            .then_inc(pt_ok, 1)
                    else:
                        nc.vector.tensor_copy(pT[:, m % 3, 0:PAST], ps[:, 3 + m % 2, 0:PAST]).then_inc(pt_part, 1)
                        nc.vector.tensor_copy(pT[0:NS, m % 3, PAST:PAST + P], ps[0:NS, 3 + m % 2, PAST:PAST + P])\
                            .then_inc(pt_ok, 1)
                for i in range(1, 4):
                    if n == FIRST[i] - 7:
                        cmp_soft(i)
                    if n == FIRST[i] - 5:
                        cmp_norm(i)
                    if n == FIRST[i] - 2:
                        cmp_turn(i, 0)
                    if n == FIRST[i]:
                        cmp_turn(i, 1)
                for q in range(6):
                    if n == LAST[q] + 3:
                        dve.wait_ge(oh_ok, q + 1)
                        if q < 4:
                            nc.vector.tensor_tensor(
                                ol[:, :, q * P:(q + 1) * P], ps[:, 5 + q % 2, :].rearrange("p (r t) -> p r t", r=G),
                                oh[:, :, q * P:(q + 1) * P].bitcast(F32), ALU.subtract).then_inc(ol_ok, 1)
                        else:
                            t0 = SEQ + (q - 4) * (NS // 2)
                            nc.vector.tensor_tensor(
                                ol[:, :, t0:t0 + NS // 2].rearrange("p r (b t) -> p b r t", t=DT),
                                ps[:, 5 + q % 2, 0:P].rearrange("p (b r t) -> p b r t", r=G, t=DT),
                                oh[:, :, t0:t0 + NS // 2].bitcast(F32).rearrange("p r (b t) -> p b r t", t=DT),
                                ALU.subtract).then_inc(ol_ok, 1)
            dve.wait_ge(ln_mean, 1)
            for c in range(CT):
                nc.vector.tensor_tensor(yc[:, c, :], yc[:, c, :], pair(0), ALU.subtract).then_inc(ln_xc, 1)
            dve.wait_ge(ln_var, 1)
            nc.vector.tensor_scalar(lnv[:, :], pair(1), EPS, None, ALU.add).then_inc(ln_step, 1)
            dve.wait_ge(ln_step, 1)
            nc.vector.reciprocal(lnv[:, :], lnv[:, :]).then_inc(ln_step, 1)
            dve.wait_ge(ln_rs, 1)
            dve.wait_ge(ln_sq, CT)
            dve.wait_ge(ln_xc, CT)
            for c in range(CT):
                nc.vector.tensor_tensor(yc[:, c, :], yc[:, c, :], lnr[:, :], ALU.mult).then_inc(ln_xn, 1)
            for c in range(CT):
                dve.wait_ge(silu_ok, c + 1)
                nc.vector.tensor_copy(ch[:, c, :], lnsq[:, c, :]).then_inc(c_step, 1)
                dve.wait_ge(c_step, 2 * c + 1)
                nc.vector.tensor_tensor(cl[:, c, :], lnsq[:, c, :], ch[:, c, :].bitcast(F32), ALU.subtract)\
                    .then_inc(c_step, 1)
            lo(S_MRG)
            with dve.Fori(0, KT // 2) as i:
                for j in range(6):
                    b = (S_MRG + j + 1) % 2
                    dve.wait_ge(hi_done, 6 * i + (S_MRG + j + 2))
                    nc.vector.tensor_tensor(wl[:, b, :], raw[:, b, :], wh[:, b, :].bitcast(F32), ALU.subtract)\
                        .then_inc(lo_done, 1)
                    if j % 3 == 2:
                        h = j // 3
                        m = 2 * i + h
                        for q in range(2):
                            dve.wait_ge(m_sig, 4 * i + 2 * h + q + 1)
                            if q == 0:
                                dve.wait_ge(m_attn, 2 * i + h + 1)
                            else:
                                dve.wait_ge(slot_used, 6 * i + (S_MRG + 3 * h + 3))
                            nc.vector.tensor_tensor(ms[:, h, q, :], ms[:, h, q, :], pair(2 + q), ALU.mult)\
                                .then_inc(m_mul, 1)
                        dve.wait_ge(m_sum, 2 * i + h + 1)
                        nc.vector.tensor_scalar(mh[:, bass.ds(m, 1), :], msum[:, h:h + 1, :], 1.0, None, ALU.mult)\
                            .then_inc(m_hi, 1)
                        dve.wait_ge(m_hi, 2 * i + h + 1)
                        nc.vector.tensor_tensor(ml[:, bass.ds(m, 1), :], msum[:, h:h + 1, :],
                                                mh[:, bass.ds(m, 1), :].bitcast(F32), ALU.subtract).then_inc(m_ok, 1)
            for s in range(S_OUT, S_UP):
                lo(s + 1)
            dve.wait_ge(sq2, TT)
            nc.vector.tensor_scalar(ss[:, :], ss[:, :], 1.0 / D, EPS, ALU.mult, ALU.add).then_inc(rs2_step, 1)
            dve.wait_ge(rs2_step, 1)
            nc.vector.reciprocal(ss[:, :], ss[:, :]).then_inc(rs2_step, 1)
            dve.wait_ge(rs2, 1)
            dve.wait_ge(gp_in, 16)
            dve.wait_ge(x1_in, 16 * TT)
            for i in range(TT):
                m = ROWS[i]
                nc.vector.scalar_tensor_tensor(hb[0:m, i, :], hb[0:m, i, :], rstd[0:m, i:i + 1], gpost[0:m, :],
                                               ALU.mult, ALU.mult).then_inc(x1_step, 1)
                dve.wait_ge(x1_step, 2 * i + 1)
                nc.vector.tensor_tensor(x1[0:m, i, :], x1[0:m, i, :], hb[0:m, i, :], ALU.add).then_inc(x1_step, 1)
            dve.wait_ge(sf_t, 1)
            nc.vector.tensor_copy(sfT[:, :, :].rearrange("p t r -> p (t r)"), pf[:, 1024:1024 + 2 * FT * 16])\
                .then_inc(sf_ok, 1)
            dve.wait_ge(sq3, TT)
            nc.vector.tensor_scalar(ss[:, :], ss[:, :], 1.0 / D, EPS, ALU.mult, ALU.add).then_inc(rs3_step, 1)
            dve.wait_ge(rs3_step, 1)
            nc.vector.reciprocal(ss[:, :], ss[:, :]).then_inc(rs3_step, 1)
            dve.wait_ge(rs3, 1)
            for i in range(TT):
                m = ROWS[i]
                nc.vector.tensor_scalar(hb[0:m, i, :], x1[0:m, i, :], rstd[0:m, i:i + 1], None, ALU.mult)\
                    .then_inc(xn2, 1)
            for k in range(KT):
                dve.wait_ge(z2_hi, k + 1)
                nc.vector.scalar_tensor_tensor(zl[:, k, :], pf[:, 1024 * (k % 2):1024 * (k % 2) + NT],
                                               par[:, P_GFFN + k:P_GFFN + k + 1], zh[:, k, :].bitcast(F32),
                                               ALU.mult, ALU.subtract).then_inc(z2_ok, 1)
            dve.wait_ge(sf_ok, 1)
            nc.vector.memset(u[:, :, 0:2], 0.0).then_inc(u_pad, 1)
            with dve.Fori(0, FT) as i:
                for j in range(2):
                    b = (S_UP + j + 1) % 2
                    dve.wait_ge(hi_done, 2 * i + (S_UP + j + 2))
                    nc.vector.tensor_tensor(wl[:, b, :], raw[:, b, :], wh[:, b, :].bitcast(F32), ALU.subtract)\
                        .then_inc(lo_done, 1)
                    t = i + FT * j
                    hist = u[:, j, 2 + SEQ:UEXT].rearrange("p (b t) -> p b t", t=DT + 2)
                    dve.wait_ge(cv_step, 6 * i + 3 * j)
                    nc.vector.tensor_scalar(hist[:, :, 0:2],
                                            sfT[:, bass.ds(t, 1), :].rearrange("p o (b t) -> p (o b) t", t=2),
                                            1.0, None, ALU.mult).then_inc(u_hist, 1)
                    dve.wait_ge(u_ev[j], 2 * i + 2)
                    nc.vector.tensor_scalar(ulast[:, bass.ds(t, 1), 0:2], u[:, j:j + 1, SEQ:SEQ + 2], 1.0, None,
                                            ALU.mult).then_inc(u_kept, 1)
                    nc.vector.tensor_scalar(
                        ulast[:, bass.ds(t, 1), 2:18].rearrange("p o (b t) -> p (o b) t", t=2),
                        hist[:, :, DT:DT + 2], 1.0, None, ALU.mult).then_inc(u_kept, 1)
                    if j == 0:
                        dve.wait_ge(h_mul, 2 * i)
                    dve.wait_ge(u_hist, 2 * i + j + 1)
                    nc.vector.tensor_scalar(cv[:, j, :], u[:, j, 0:CEXT], par[:, bass.ds(t + P_FW, 1)],
                                            par[:, bass.ds(t + P_FB, 1)], ALU.mult, ALU.add).then_inc(cv_step, 1)
                    for l in (1, 2):
                        dve.wait_ge(cv_step, 6 * i + 3 * j + l)
                        nc.vector.scalar_tensor_tensor(cv[:, j, :], u[:, j, l:l + CEXT],
                                                       par[:, bass.ds(t + P_FW + l * 2 * FT, 1)],
                                                       cv[:, j, :], ALU.mult, ALU.add).then_inc(cv_step, 1)
                dve.wait_ge(h_mul, 2 * i + 2)
                nc.vector.tensor_scalar(hh[:, bass.ds(i, 1), :], hs[:, :].unsqueeze(1), 1.0, None, ALU.mult)\
                    .then_inc(h_hi, 1)
                dve.wait_ge(h_hi, i + 1)
                nc.vector.tensor_tensor(hl[:, bass.ds(i, 1), :], hs[:, :].unsqueeze(1),
                                        hh[:, bass.ds(i, 1), :].bitcast(F32), ALU.subtract).then_inc(h_ok, 1)
            for s in range(S_DOWN, S_END - 1):
                lo(s + 1)
            dve.wait_ge(sq4, TT)
            nc.vector.tensor_scalar(ss[:, :], ss[:, :], 1.0 / D, EPS, ALU.mult, ALU.add).then_inc(rs4_step, 1)
            dve.wait_ge(rs4_step, 1)
            nc.vector.reciprocal(ss[:, :], ss[:, :]).then_inc(rs4_step, 1)
            dve.wait_ge(rs4, 1)
            for i in range(TT):
                m = ROWS[i]
                nc.vector.scalar_tensor_tensor(fb[0:m, i, :], fb[0:m, i, :], rstd[0:m, i:i + 1], gpost2[0:m, :],
                                               ALU.mult, ALU.mult).then_inc(y_step, 1)
                dve.wait_ge(y_step, 2 * i + 1)
                nc.vector.tensor_tensor(x1[0:m, i, :], x1[0:m, i, :], fb[0:m, i, :], ALU.add).then_inc(y_step, 1)

        @block.tensor
        def _(pe):
            def three(out, a, b, start, stop):
                (ah, al), (bh, bl) = a, b
                nc.tensor.matmul(out, ah, bh, start=start, stop=False)
                nc.tensor.matmul(out, ah, bl, start=False, stop=False)
                return nc.tensor.matmul(out, al, bh, start=False, stop=stop)

            def tile(q, slot, k0, kn, src, m=P, view=None):
                for h in range(2):
                    cols = slice(h * HALF, (h + 1) * HALF)
                    for k in range(kn):
                        if view is None:
                            w = (whk[:, slot, k0 + k, :], wlk[:, slot, k0 + k, :])
                        else:
                            w = (view[0][:, k, :], view[1][:, k, :])
                        last = three(pair(q, h * HALF, (h + 1) * HALF, m), w,
                                     (src[0][:, k, cols], src[1][:, k, cols]), k == 0, k == kn - 1)
                return last

            pe.wait_ge(const_ok, 1)
            pe.wait_ge(par_in, 16 * 9)
            nc.tensor.transpose(ps[:, 6, 0:P], par_raw[:, 0, :], ident[:, :])
            nc.tensor.transpose(ps[:, 6, P:2 * P], par_raw[:, 1, :], ident[:, :])
            m = P_ALL - 2 * P
            nc.tensor.transpose(ps[:, 6, 2 * P:P_ALL], par_raw[0:m, 2, :], ident[0:m, 0:m]).then_inc(par_t, 1)
            pe.wait_ge(scv_in, 32)
            for hf in range(2):
                for c in range(CT):
                    mm = nc.tensor.transpose(ps[:, 4 + hf, c * 120:(c + 1) * 120],
                                             scv[0:120, hf, c * P:(c + 1) * P], ident[0:120, 0:120])
                mm.then_inc(scv_t, 1)
            def turn_x(src, full, taken):
                for k in range(KT):
                    if k >= 2:
                        pe.wait_ge(taken, k - 1)
                    for i in range(TT):
                        c0 = 1024 * (k % 2) + i * P
                        mm = nc.tensor.transpose(pf[:, c0:c0 + ROWS[i]], src[0:ROWS[i], i, k * P:(k + 1) * P],
                                                 ident[0:ROWS[i], 0:ROWS[i]])
                    mm.then_inc(full, 1)
                pe.wait_ge(taken, KT)

            pe.wait_ge(xn_ok, TT)
            turn_x(x, z_full, z_ok)

            def past(n):
                pe.wait_ge(page_in[n % 2], 32 * (n // 2 + 1))
                if n == 0:
                    pe.wait_ge(hist_ok, 2 * CT)
                    pe.wait_ge(par_ok, 2)
                if n >= 4:
                    pe.wait_ge(past_ev, 2 * (n - 3))
                for j, c0 in enumerate((0, 128, 256, 512)):
                    mm = nc.tensor.transpose(ps[:, 4 + n % 4, j * P:(j + 1) * P], page[:, n % 2, c0:c0 + P],
                                             ident[:, :])
                mm.then_inc(past_t, 1)

            z = (zh, zl)
            for s in range(S_MRG):
                pe.wait_ge(lo_done, s + 1)
                if s >= 2:
                    t = s - 2
                    if t < S_KV and t % 2 == 0:
                        pe.wait_ge(sg_ok, t // 2 + 1)
                    elif t < S_KV:
                        pe.wait_ge(glu_p, t // 2 + 1)
                        pe.wait_ge(glu_ok, t // 2 + 1)
                    elif t < S_Q:
                        pe.wait_ge(kv_ok, t - S_KV + 1)
                    else:
                        pe.wait_ge(q_ok, t - S_Q + 1)
                if s == S_GATE:
                    vh = wh[:, s % 2, 0:KT * 24].rearrange("p (k n) -> p k n", n=24)
                    vl = wl[:, s % 2, 0:KT * 24].rearrange("p (k n) -> p k n", n=24)
                    tile(s % 2, s % 2, 0, KT, z, 24, (vh, vl)).then_inc(slot_used, 1)
                else:
                    tile(s % 2, s % 2, 0, KT, z).then_inc(slot_used, 1)
                if s < S_KV:
                    past(2 * s)
                    past(2 * s + 1)
            pe.wait_ge(gt_ok, 1)
            pe.wait_ge(past_ev, 2 * NPG)
            for i in range(TT):
                mm = nc.tensor.transpose(ps[0:ROWS[i], 4, i * 24:(i + 1) * 24], gT[:, i * P:i * P + ROWS[i]],
                                         ident[0:24, 0:24])
            mm.then_inc(mid_t, 1)
            for c in range(CT):
                mm = nc.tensor.transpose(ps[0:HIST, 5, c * P:(c + 1) * P], ext[:, c, SEQ:SEQ + HIST], ident[:, :])
            mm.then_inc(cst_t, 1)
            for q, (b0, nb) in enumerate(SEQ_GROUPS):
                if q == 2:
                    pe.wait_ge(cst_ok, 1)
                for c in range(CT):
                    c0 = HIST + SEQ + b0 * SB_S
                    mm = nc.tensor.transpose(ps[0:nb * SB_S, 5 + (q + 1) % 3, c * P:(c + 1) * P],
                                             ext[:, c, c0:c0 + nb * SB_S], ident[:, :])
                mm.then_inc(cst_t, 1)
            pe.wait_ge(kv_ok, 6)
            pe.wait_ge(q_ok, G)
            for i in range(TT):
                if i >= 2:
                    pe.wait_ge(ktok_ok, i - 1)
                for j in range(6):
                    c0 = 1024 * (i % 2) + j * P
                    mm = nc.tensor.transpose(pf[0:ROWS[i], c0:c0 + P], kvT[:, j, i * P:i * P + ROWS[i]], ident[:, :])
                mm.then_inc(ktok_t, 1)
            pe.wait_ge(const_ok, 2)
            pe.wait_ge(cst_ok, 4)
            pe.wait_ge(gtok_ok, 2)
            nc.tensor.transpose(ps[:, 7, 256:256 + G], rselT[:, :], ident[0:G, 0:G])
            for hf in range(2):
                mm = nc.tensor.matmul(ps[:, 7, 32 * hf:32 * hf + 24], rowsel[0:NS, hf, :], gtok[0:NS, 4, :],
                                      start=True, stop=True)
            mm.then_inc(gsel_mm, 1)
            for j in range(2):
                pe.wait_ge(phi_in, 32 * (j + 1))
                pe.wait_ge(cc_ok, j + 1)
                for t in range(CL):
                    mm = nc.tensor.matmul(ps[:, 4 + j, 0:NCALL], phi[:, t, :],
                                          cc[:, j, t:t + CS * (NCALL - 1) + 1:CS],
                                          start=(t == 0), stop=(t == CL - 1))
                mm.then_inc(cmp_mm, 1)
            pe.wait_ge(cmp_ok, 4)
            nc.tensor.transpose(ps[0:NCP, 6, 0:P], vcmpT[:, 0:NCP], ident[:, :])
            nc.tensor.transpose(ps[0:DB * NCS, 6, P:2 * P], vcmpT[:, NCP:], ident[:, :]).then_inc(vc_t, 1)

            def cmp_scores(i):
                if i == 0:
                    pe.wait_ge(gsel_ok, 1)
                else:
                    pe.wait_ge(pct_ok, 2 * i)
                for h in range(HEADS):
                    g, r = h // G, h % G
                    if h == G:
                        pe.wait_ge(cs_half, i + 1)
                    mm = nc.tensor.matmul(ps[:, 7, h * 32:h * 32 + NCP], qT[g * HD:(g + 1) * HD, r, i * P:(i + 1) * P],
                                          kcmp[g * HD:(g + 1) * HD, 0:NCP], start=True, stop=True)
                    if h == G - 1:
                        mm.then_inc(cs_half, 1)
                mm.then_inc(cs_full, 1)

            def cmp_turn(i, hf):
                if hf == 0:
                    pe.wait_ge(pc_ok, i + 1)
                else:
                    pe.wait_ge(pct_ok, 2 * i + 1)
                for h in range(4):
                    mm = nc.tensor.transpose(ps[0:NCP, 7, h * P:(h + 1) * P], sm[:, 4 * hf + h, :], ident[:, :])
                mm.then_inc(pct_full, 1)

            def scores(n):
                q, r, g, c = UNITS[n]
                if n >= 3:
                    pe.wait_ge(exp_ok, n - 2)
                rows = slice(g * HD, (g + 1) * HD)
                bk, w = n % 3, width(n)
                if q < 4:
                    if q:
                        nc.tensor.matmul(ps[:, bk, 0:w - P], qT[rows, r, q * P:(q + 1) * P], kvT[rows, 2 * c, 0:w - P],
                                         start=True, stop=True)
                    nc.tensor.matmul(ps[:, bk, w - P:w], qT[rows, r, q * P:(q + 1) * P], kvT[rows, 2 * c, w - P:w],
                                     start=True, stop=False)
                    nc.tensor.matmul(ps[:, bk, w - P:w], identb[:, :], causal[:, :], start=False, stop=True)\
                        .then_inc(s_full, 1)
                    return
                hf = q - 4
                if c == 0:
                    nc.tensor.matmul(ps[:, bk, 0:w], qs[rows, hf, :], kcmp[rows, NCP:], start=True, stop=False)
                    nc.tensor.matmul(ps[:, bk, 0:w], rowsel[rows, hf, :], cmpmask[rows, :], start=False, stop=True)\
                        .then_inc(s_full, 1)
                    return
                for b in range(4):
                    k0 = (4 * hf + b) * PAST
                    nc.tensor.matmul(ps[32 * b:32 * b + 32, bk, 0:PAST], qs[rows, hf, 32 * b:32 * b + 32],
                                     kpast[rows, c - 1, k0:k0 + PAST], start=True, stop=True)
                nc.tensor.matmul(ps[:, bk, PAST:w], qs[rows, hf, :], kvT[rows, 2 * c, SEQ:NT], start=True, stop=False)
                nc.tensor.matmul(ps[:, bk, PAST:w], rowsel[rows, hf, :], newmask[rows, :], start=False, stop=True)\
                    .then_inc(s_full, 1)

            def turn(n):
                q, _, _, c = UNITS[n]
                pe.wait_ge(scaled, n + 1)
                if n >= 2:
                    pe.wait_ge(pt_ok, n - 1)
                bk, w = 3 + n % 2, width(n)
                c0 = 0
                while c0 < w:
                    m = min(P, w - c0)
                    mm = nc.tensor.transpose(ps[0:m, bk, c0:c0 + P], probs[:, n % 3, c0:c0 + m], ident[:, :])
                    c0 += P
                mm.then_inc(pt_full, 1)

            def values(n):
                q, r, g, c = UNITS[n]
                if q >= 2 and n == FIRST[q]:
                    pe.wait_ge(ol_ok, q - 1)
                pe.wait_ge(pt_ok, n + 1)
                rows = slice(g * HD, (g + 1) * HD)
                v0 = (2 * c + 1) * P + g * HD
                pt = pT[:, n % 3, :]
                if q < 4:
                    out = ps[rows, 5 + q % 2, r * P:(r + 1) * P]
                    if c == 1:
                        pe.wait_ge(pct_ok, 2 * q + 2)
                        nc.tensor.matmul(out, vcp[:, rows], pcT[:, q % 2, g * G + r, :], start=True, stop=False)
                    for j in range(q + 1):
                        mm = nc.tensor.matmul(out, ktok[:, j, v0:v0 + HD], pt[:, j * P:(j + 1) * P],
                                              start=False, stop=(c == 2 and j == q))
                    mm.then_inc(pv_done, 1)
                    return
                out = ps[rows, 5 + q % 2, 0:P]
                if c == 0:
                    nc.tensor.matmul(out, vcs[:, rows], pt[0:DB * NCS, 0:P], start=True, stop=False)\
                        .then_inc(pv_done, 1)
                    return
                vp = vsel if c == 1 else vwin
                for b in range(4):
                    for j in range(2):
                        nc.tensor.matmul(ps[rows, 5 + q % 2, 32 * b:32 * b + 32],
                                         vp[:, 2 * (4 * (q - 4) + b) + j, rows],
                                         pt[:, j * P + 32 * b:j * P + 32 * b + 32], start=False, stop=False)
                mm = nc.tensor.matmul(out, ktok[0:NS, 4, v0:v0 + HD], pt[0:NS, PAST:PAST + P],
                                      start=False, stop=(c == 2))
                mm.then_inc(pv_done, 1)

            pe.wait_ge(ktok_ok, TT)
            pe.wait_ge(vc_ok, 2)
            pe.wait_ge(qs_ok, 1)
            cmp_scores(0)
            cmp_turn(0, 0)
            cmp_turn(0, 1)
            for n in range(NU + 3):
                if n < NU:
                    scores(n)
                if 2 <= n < NU + 2:
                    turn(n - 2)
                if n >= 3:
                    values(n - 3)
                for i in range(1, 4):
                    if n == FIRST[i] - 8:
                        cmp_scores(i)
                    if n == FIRST[i] - 3:
                        cmp_turn(i, 0)
                    if n == FIRST[i] - 1:
                        cmp_turn(i, 1)
            pe.wait_ge(conv_n, 4 * 2 * CW)
            pe.wait_ge(exp_ok, NU)
            pe.wait_ge(pt_ok, NU)
            for q, (src, done) in enumerate(((yc, ln_mean), (lnsq, ln_var))):
                if q == 1:
                    pe.wait_ge(ln_sq, CT)
                for h in range(2):
                    for c in range(CT):
                        mm = nc.tensor.matmul(pair(q, h * HALF, (h + 1) * HALF), mean_w[:, :],
                                              src[:, c, h * HALF:(h + 1) * HALF], start=(c == 0), stop=(c == CT - 1))
                mm.then_inc(done, 1)
            pe.wait_ge(ln_step, 1)
            pe.wait_ge(c_step, 2 * CT)
            pe.wait_ge(ol_ok, 6)
            with pe.Fori(0, KT // 2) as i:
                for j in range(6):
                    b = (S_MRG + j) % 2
                    h = j // 3
                    pe.wait_ge(lo_done, 6 * i + (S_MRG + j + 1))
                    if j % 3 < 2:
                        pe.wait_ge(m_sig, 4 * i + 2 * h)
                        tile(j % 3, b, 0, KT, z).then_inc(slot_used, 1)
                    else:
                        pe.wait_ge(m_mul, 4 * i + 2 * h)
                        tile(2, b, 0, CT, (oh, ol)).then_inc(m_attn, 1)
                        tile(3, b, CT, CT, (ch, cl)).then_inc(slot_used, 1)

            def token_major(s0, kn, lhs, ev):
                for half in range(2):
                    for kc in range(kn // 2):
                        s = s0 + half * (kn // 2) + kc
                        pe.wait_ge(lo_done, s + 1)
                        for kk in range(2):
                            k = 2 * kc + kk
                            for i in range(TT):
                                bk = half * TT + i
                                if k == 0 and bk >= 8:
                                    pe.wait_ge(ev, bk - 8 + 1)
                                mm = three(ps[0:ROWS[i], bk % 8, :],
                                           (lhs[0][:, k, i * P:i * P + ROWS[i]], lhs[1][:, k, i * P:i * P + ROWS[i]]),
                                           (whc[:, s % 2, kk, :], wlc[:, s % 2, kk, :]), k == 0, k == kn - 1)
                        mm.then_inc(slot_used, 1)

            pe.wait_ge(m_ok, KT)
            pe.wait_ge(m_mul, 2 * KT)
            token_major(S_OUT, KT, (mh, ml), o_ev)
            pe.wait_ge(sf_in, 16)
            pe.wait_ge(o_ev, TT)
            for t in range(2 * FT):
                mm = nc.tensor.transpose(pf[:, 1024 + 16 * t:1024 + 16 * (t + 1)], sf[:, t * P:(t + 1) * P],
                                         ident[0:16, 0:16])
            mm.then_inc(sf_t, 1)
            pe.wait_ge(sf_ok, 1)
            pe.wait_ge(o_ev, 2 * TT)
            pe.wait_ge(xn2, TT)
            turn_x(hb, z2_full, z2_ok)
            with pe.Fori(0, FT) as i:
                for j in range(2):
                    pe.wait_ge(lo_done, 2 * i + (S_UP + j + 1))
                    pe.wait_ge(u_ev[j], 2 * i)
                    tile(j, (S_UP + j) % 2, 0, KT, z).then_inc(slot_used, 1)
            pe.wait_ge(u_kept, 4 * FT)
            for q in range(11):
                if q >= 3:
                    pe.wait_ge(ul_ev, q - 2)
                for t in range(4):
                    mm = nc.tensor.transpose(ps[0:18, 5 + q % 3, t * P:(t + 1) * P], ulast[:, 4 * q + t, :],
                                             ident[:, :])
                mm.then_inc(ul_t, 1)
            pe.wait_ge(h_ok, FT)
            pe.wait_ge(u_ev[0], 2 * FT)
            pe.wait_ge(u_ev[1], 2 * FT)
            pe.wait_ge(ul_ev, 11)
            token_major(S_DOWN, FT, (hh, hl), d_ev)


_INS = ["x_prompt", "x_sample", "cache_kv", "state_kv_win", "state_conv", "state_ffn", "page_table",
        "norm_mix_pre", "norm_mix_post", "norm_ffn_pre", "norm_ffn_post", "w_in", "w_phi_k", "b_phi_k",
        "w_phi_v", "b_phi_v", "w_attn_out", "conv_w", "conv_b", "conv_ln_g", "conv_ln_b", "w_conv_out",
        "w_out", "w_up", "ffn_conv_w", "ffn_conv_b", "w_down"]
_OUTS = [(1, SEQ, D), (DB, DT, D), (1, 1, SEQ, 4, KVH, HD), (1, DB, DT, 4, KVH, HD), (1, 1, SEQ, 2, KVH, HD),
         (1, DB, PAST + DT, 2, KVH, HD), (1, 1, HIST, CH), (1, DB, HIST, CH), (1, 1, FW - 1, 2 * FF),
         (1, DB, FW - 1, 2 * FF)]


def kernel(**inputs):
    import numpy as _np
    import concourse.bacc as _bacc
    from concourse import mybir as _mybir
    from concourse.bass_utils import run_bass_kernel_spmd as _run

    nc = _bacc.Bacc("TRN2", target_bir_lowering=False, num_devices=1)
    arrays, args = {}, []
    for name in _INS:
        a = _np.ascontiguousarray(inputs[name])
        arrays[f"in_{name}_dram"] = a
        args.append(nc.dram_tensor(f"in_{name}_dram", a.shape, _mybir.dt.from_np(a.dtype), kind="ExternalInput").ap())
    for i, shape in enumerate(_OUTS):
        args.append(nc.dram_tensor(f"out_{i}_dram", shape, _mybir.dt.float32, kind="ExternalOutput").ap())
    build_layer(nc, *args)
    r = _run(nc, [arrays], core_ids=[0])
    return tuple(r.results[0][f"out_{i}_dram"] for i in range(len(_OUTS)))
```

```python
from contextlib import ExitStack

import concourse.bass as bass
from concourse import mybir

F32 = mybir.dt.float32
F32R = mybir.dt.float32r
BF16 = mybir.dt.bfloat16
I32 = mybir.dt.int32
ALU = mybir.AluOpType
ACT = mybir.ActivationFunctionType
AX = mybir.AxisListType

P = 128
D = 1024
KT = D // P
SEQ = 512
DB, DT = 8, 8
NS = DB * DT
NT = SEQ + NS
TT = 5
HALF = NT // 2
PAST = 256
PAGE = 128
NPG = DB * PAST // PAGE
HEADS, KVH, G, HD = 8, 2, 4, 64
CL, CS = 32, 16
NCP = (SEQ - CL) // CS + 1
NCS = (PAST + DT - CL) // CS + 1
CC_T = SEQ + DB * PAST
NCALL = (CC_T - CL) // CS + 1
CH = 512
CT = CH // P
CW = 31
HIST = CW - 1
SB_S = HIST + DT
EXT = HIST + SEQ + DB * SB_S
FF = 2816
FT = FF // P
FW = 3
UEXT = 2 + SEQ + DB * (2 + DT)
CEXT = UEXT - 2
EPS = 1e-6
NEG = -1e30
TINY = 1e-30
OFF_KV = 512
OFF_GATE = OFF_KV + 6 * 128
OFF_GLU = OFF_GATE + 24
OFF_MRG = OFF_GLU + 2 * CH
IN_W = OFF_MRG + 2 * D
ROWS = [P] * 4 + [NS]

P_FW = 0
P_CW = P_FW + FW * 2 * FT
P_FB = P_CW + CW * CT
P_CB = P_FB + 2 * FT
P_GPRE = P_CB + CT
P_GFFN = P_GPRE + KT
P_LNG = P_GFFN + KT
P_LNB = P_LNG + CT
P_ALL = P_LNB + CT

S_GLU = 0
S_KV = S_GLU + 2 * CT
S_Q = S_KV + 6
S_GATE = S_Q + 4
S_MRG = S_GATE + 1
S_OUT = S_MRG + 3 * KT
S_UP = S_OUT + KT
S_DOWN = S_UP + 2 * FT
S_END = S_DOWN + FT
MRG_DMAS = [1, 1, 3]
S_CMP_K = S_KV + 1
S_CMP_V = S_Q + 1
S_CST = S_KV + 4
S_TOK = S_Q
SEQ_GROUPS = [(0, 3), (3, 3), (6, 2)]


def slot_dmas(s):
    if S_Q <= s < S_GATE:
        return 2
    if S_MRG <= s < S_OUT:
        return MRG_DMAS[(s - S_MRG) % 3]
    return 1


def raw_value(s):
    return 16 * sum(slot_dmas(x) for x in range(s % 2, s + 1, 2))


UNITS = [(i, r, g, c) for i in range(4) for r in range(G) for g in range(KVH) for c in (1, 2)]
UNITS += [(4 + hf, 0, g, c) for hf in range(2) for g in range(KVH) for c in (0, 1, 2)]
NU = len(UNITS)
LAST = [max(n for n, u in enumerate(UNITS) if u[0] == q) for q in range(6)]
FIRST = [min(n for n, u in enumerate(UNITS) if u[0] == q) for q in range(6)]


def width(n):
    q, _, _, c = UNITS[n]
    return (q + 1) * P if q < 4 else (DB * NCS if c == 0 else PAST + NS)


def build_layer(nc, x_prompt, x_sample, cache_kv, state_kv_win, state_conv, state_ffn, page_table,
                g_mix_pre, g_mix_post, g_ffn_pre, g_ffn_post, w_in, w_phi_k, b_phi_k, w_phi_v, b_phi_v,
                w_attn_out, conv_w, conv_b, conv_ln_g, conv_ln_b, w_conv_out, w_out, w_up,
                ffn_conv_w, ffn_conv_b, w_down,
                y_prompt, y_sample, kv_prompt, kv_sample, win_prompt, win_sample,
                conv_prompt, conv_sample, ffn_prompt, ffn_sample):
    ctx = ExitStack()
    with ctx:
        base = (nc.sbuf_base + 63) // 32 * 32

        def at(name, shape, dt, col):
            return nc.alloc_sbuf_tensor_at(name, shape, dt, offset=base + 4 * col)

        A = 0
        B = A + 2 * KT * NT
        C = B + 6 * 1024
        DD = C + 4 * NT
        E = DD + 6 * NT
        FV = E + TT * 768
        GK = FV + NPG * P
        H = GK + 2 * DB * PAST
        I = H + NPG * P
        J = I + 4096 + 2 * CC_T + 2 * 768
        K = J + CT * EXT + CT * NT

        zh = at("zh", [P, KT, NT], F32R, A)
        zl = at("zl", [P, KT, NT], F32R, A + KT * NT)
        sq_x = at("sq_x", [P, TT, D], F32, A)
        raw = at("raw", [P, 2, 1024], F32, B)
        wh = at("wh", [P, 2, 1024], F32R, B + 2048)
        wl = at("wl", [P, 2, 1024], F32R, B + 4096)
        x = at("x", [P, TT, D], F32, C)
        qT = at("qT", [P, G, NT], F32, C)
        kvT = at("kvT", [P, 6, NT], F32, DD)
        ktok = at("ktok", [P, TT, 768], F32, E)
        par_raw = at("par_raw", [P, 3, P], F32, E)
        scv = at("scv", [P, 2, CH], F32, E + 384)
        sg = at("sg", [P, NT], F32, E + 384 + 1024)
        gT = at("gT", [24, NT], F32, I + 7680)
        vwin = at("vwin", [P, NPG, P], F32, FV)
        kpast = at("kpast", [P, 2, DB * PAST], F32, GK)
        vsel = at("vsel", [P, NPG, P], F32, H)
        phi = at("phi", [P, CL, P], F32, I)
        cc = at("cc", [P, 2, CC_T], F32, I + 4096)
        page = at("page", [P, 2, 768], F32, I + 4096 + 2 * CC_T)
        cst = at("cst", [P, 3, CH], F32, I + 4096 + 2 * CC_T)
        oh = at("oh", [P, G, NT], F32R, I)
        ol = at("ol", [P, G, NT], F32R, I + G * NT)
        probs = at("probs", [P, 3, 512], F32, I + 4608)
        cprod = at("cprod", [P, 4, NT], F32, I + 4096)
        pT = at("pT", [P, 3, 512], F32, I + 6144)
        pcT = at("pcT", [NCP, 2, HEADS, P], F32, I + 7680)
        sc = at("sc", [P, HEADS, NCP], F32, I + 9728)
        se = at("se", [P, HEADS, NCP], F32, I + 9728 + 256)
        sm = at("sm", [P, HEADS, NCP], F32, I + 9728 + 512)
        ext = at("ext", [P, CT, EXT], F32, J)
        yc = at("yc", [P, CT, NT], F32, J + CT * EXT)
        lnsq = at("lnsq", [P, CT, NT], F32, DD)
        lnv = at("lnv", [P, NT], F32, DD + CT * NT)
        lnr = at("lnr", [P, NT], F32, DD + CT * NT + NT)
        ch = at("ch", [P, CT, NT], F32R, FV)
        cl = at("cl", [P, CT, NT], F32R, FV + CT * NT)
        mh = at("mh", [P, KT, NT], F32R, C)
        ml = at("ml", [P, KT, NT], F32R, C + KT * NT)
        ms = at("ms", [P, 2, 2, NT], F32, J)
        msum = at("msum", [P, 2, NT], F32, J + 4 * NT)
        hb = at("hb", [P, TT, D], F32, FV)
        sf = at("sf", [2 * DB, 2 * FF], F32, H)
        gpost = at("gpost", [P, D], F32, H + 2 * FF)
        junk = at("junk", [P, TT, D], F32, H + 2 * FF + D)
        x1 = at("x1", [P, TT, D], F32, K - TT * D)
        hh = at("hh", [P, FT, NT], F32R, C)
        hl = at("hl", [P, FT, NT], F32R, C + FT * NT)
        u = at("u", [P, 2, UEXT], F32, C + 2 * FT * NT)
        U2 = C + 2 * FT * NT + (2 * UEXT + 7) // 8 * 8
        cv = at("cv", [P, 2, CEXT], F32, U2)
        hs = at("hs", [P, NT], F32, U2 + 2 * CEXT)
        ulast = at("ulast", [P, 2 * FT, 18], F32, U2 + 2 * CEXT + NT)
        assert U2 + 2 * CEXT + NT + 2 * FT * 18 <= K - TT * D
        fb = at("fb", [P, TT, D], F32, A)
        ustage = at("ustage", [18, 2 * FF], F32, A + 2 * KT * NT - 2 * FF)
        junk2 = at("junk2", [P, 4, D], F32, A + TT * D)
        gpost2 = at("gpost2", [P, D], F32, C + 2 * FT * NT)
        junk3 = at("junk3", [P, D], F32, C + 2 * FT * NT + D)

        used = [K]

        def small(name, shape, dt=F32):
            cols = 1
            for d in shape[1:]:
                cols *= d
            if dt == BF16:
                cols = (cols + 1) // 2
            t = at(name, shape, dt, used[0])
            used[0] += (cols + 7) // 8 * 8
            return t

        ident = small("ident", [P, P])
        identb = small("identb", [P, P], BF16)
        causal = small("causal", [P, P], BF16)
        rowsel = small("rowsel", [P, 2, P])
        newmask = small("newmask", [P, NS])
        cmpmask = small("cmpmask", [P, DB * NCS])
        rselT = small("rselT", [G, P])
        rsel = small("rsel", [P, G])
        cneg = small("cneg", [P, 4, NCP])
        c01 = small("c01", [P, 4, NCP])
        mean_w = small("mean_w", [P, P])
        par = small("par", [P, P_ALL])
        bphi = small("bphi", [P, 2])
        ss = small("ss", [P, TT])
        ssh = small("ssh", [P, 2, TT])
        rstd = small("rstd", [P, TT])
        nmax = small("nmax", [P, NU])
        esum = small("esum", [P, NU])
        rinv = small("rinv", [P, NU])
        gtok = small("gtok", [P, TT, 24])
        gsel4 = small("gsel4", [P, 2, 6, G])
        gsel = small("gsel", [P, 2, 6])
        kcmp = small("kcmp", [P, NCP + DB * NCS])
        vcmpT = small("vcmpT", [P, NCP + DB * NCS])
        vcp = small("vcp", [NCP, P])
        vcs = small("vcs", [DB * NCS, P])
        qs = small("qs", [P, 2, P])
        cmax = small("cmax", [P, HEADS])
        csum = small("csum", [P, HEADS])
        cgate = small("cgate", [P, HEADS])
        ptab = small("ptab", [1, NPG], I32)
        sfT = small("sfT", [P, 2 * FT, 2 * DB])
        assert base + 4 * used[0] <= nc.sbuf_usable_end, (base + 4 * used[0], nc.sbuf_usable_end)

        ps = ctx.enter_context(nc.psum_tensor("ps", [P, 8, 512], F32))
        pf = ps[:, :, :].rearrange("p b n -> p (b n)")
        LO = 512 - HALF

        def pair(q, a=0, b=NT, m=P):
            return pf[0:m, 1024 * q + LO + a:1024 * q + LO + b]

        def sem(name):
            return ctx.enter_context(nc.semaphore(name))

        raw_in = [sem("raw_in0"), sem("raw_in1")]
        hi_done = sem("hi_done")
        lo_done = sem("lo_done")
        slot_used = sem("slot_used")
        par_in = sem("par_in")
        scv_in = sem("scv_in")
        x_in = [sem(f"x_in{i}") for i in range(TT)]
        ptab_in = sem("ptab_in")
        bphi_in = sem("bphi_in")
        page_in = [sem("page_in0"), sem("page_in1")]
        phi_in = sem("phi_in")
        pool_init = sem("pool_init")
        const_ok = sem("const_ok")
        par_t = sem("par_t")
        par_ok = sem("par_ok")
        scv_t = sem("scv_t")
        hist_ok = sem("hist_ok")
        sq_done = sem("sq_done")
        rs_step = sem("rs_step")
        rs_ok = sem("rs_ok")
        xn_ok = sem("xn_ok")
        z_full = sem("z_full")
        zhi_ok = sem("zhi_ok")
        z_ok = sem("z_ok")
        past_t = sem("past_t")
        past_ev = sem("past_ev")
        vcopy = sem("vcopy")
        sg_ok = sem("sg_ok")
        glu_ok = sem("glu_ok")
        ext0 = sem("ext0")
        glu_p = sem("glu_p")
        conv_01 = sem("conv_01")
        conv_2 = sem("conv_2")
        conv_3 = sem("conv_3")
        conv_prod = sem("conv_prod")
        kv_ok = sem("kv_ok")
        cc_ok = sem("cc_ok")
        q_ok = sem("q_ok")
        gt_ok = sem("gt_ok")
        mid_t = sem("mid_t")
        gtok_ok = sem("gtok_ok")
        ktok_t = sem("ktok_t")
        ktok_ok = sem("ktok_ok")
        cst_t = sem("cst_t")
        cst_ok = sem("cst_ok")
        cst_out = sem("cst_out")
        kv_out = sem("kv_out")
        win_out = sem("win_out")
        cmp_mm = sem("cmp_mm")
        cmp_ok = sem("cmp_ok")
        vc_t = sem("vc_t")
        vc_ok = sem("vc_ok")
        rsel_ok = sem("rsel_ok")
        gsel_mm = sem("gsel_mm")
        gsel_ok = sem("gsel_ok")
        qs_ok = sem("qs_ok")
        s_full = sem("s_full")
        nmax_ok = sem("nmax_ok")
        exp_ok = sem("exp_ok")
        rinv_ok = sem("rinv_ok")
        scaled = sem("scaled")
        pt_full = sem("pt_full")
        pt_part = sem("pt_part")
        pt_ok = sem("pt_ok")
        pv_done = sem("pv_done")
        cs_half = sem("cs_half")
        cs_full = sem("cs_full")
        cs_step = sem("cs_step")
        ce_in = sem("ce_in")
        ce_ok = sem("ce_ok")
        pc_ok = sem("pc_ok")
        pct_full = sem("pct_full")
        pct_ok = sem("pct_ok")
        oh_ok = sem("oh_ok")
        ol_ok = sem("ol_ok")
        ln_mean = sem("ln_mean")
        ln_xc = sem("ln_xc")
        ln_sq = sem("ln_sq")
        ln_var = sem("ln_var")
        ln_step = sem("ln_step")
        ln_rs = sem("ln_rs")
        ln_xn = sem("ln_xn")
        silu_ok = sem("silu_ok")
        c_step = sem("c_step")
        m_attn = sem("m_attn")
        m_sig = sem("m_sig")
        m_mul = sem("m_mul")
        m_sum = sem("m_sum")
        m_hi = sem("m_hi")
        m_ok = sem("m_ok")
        x1_in = sem("x1_in")
        sf_in = sem("sf_in")
        gp_in = sem("gp_in")
        o_ev = sem("o_ev")
        sf_t = sem("sf_t")
        sf_ok = sem("sf_ok")
        o_tile = sem("o_tile")
        o_sq = sem("o_sq")
        rs2_pre = sem("rs2_pre")
        rs2_step = sem("rs2_step")
        rs2 = sem("rs2")
        x1_ok = sem("x1_ok")
        sq3 = sem("sq3")
        rs3_step = sem("rs3_step")
        rs3 = sem("rs3")
        xn2 = sem("xn2")
        z2_full = sem("z2_full")
        z2_hi = sem("z2_hi")
        z2_ok = sem("z2_ok")
        u_ev = [sem("u_ev0"), sem("u_ev1")]
        u_hist = sem("u_hist")
        u_kept = sem("u_kept")
        u_pad = sem("u_pad")
        cv_step = sem("cv_step")
        act_ok = sem("act_ok")
        h_mul = sem("h_mul")
        h_hi = sem("h_hi")
        h_ok = sem("h_ok")
        ul_t = sem("ul_t")
        ul_ev = sem("ul_ev")
        ffn_out = sem("ffn_out")
        d_ev = sem("d_ev")
        gp2_in = sem("gp2_in")
        d_tile = sem("d_tile")
        d_sq = sem("d_sq")
        rs4_pre = sem("rs4_pre")
        rs4_step = sem("rs4_step")
        rs4 = sem("rs4")
        y_ok = sem("y_ok")
        y_out = sem("y_out")

        w_in_v = w_in[0].rearrange("(k p) n -> p k n", p=P)
        w_up_v = w_up[0].rearrange("(k p) n -> p k n", p=P)
        w_ao_v = w_attn_out[0].rearrange("(g r h) n -> g h r n", g=KVH, r=G)
        w_co_v = w_conv_out[0].rearrange("(k p) n -> p k n", p=P)
        w_out_v = w_out[0].rearrange("(k p) n -> p k n", p=P)
        w_down_v = w_down[0].rearrange("(k p) n -> p k n", p=P)
        xs_v = x_sample.rearrange("b t d -> (b t) d")
        ys_v = y_sample.rearrange("b t d -> (b t) d")
        cache_v = cache_kv[0].rearrange("n t a g h -> n t (a g h)")
        swin_v = state_kv_win[0].rearrange("b (j t) a g h -> (b j) t (a g h)", t=PAGE)
        kvp_v = kv_prompt[0, 0].rearrange("t a g h -> t (a g h)")
        kvs_v = kv_sample[0].rearrange("b t a g h -> (b t) (a g h)")
        winp_v = win_prompt[0, 0].rearrange("t a g h -> t (a g h)")
        wins_v = win_sample[0].rearrange("b t a g h -> b t (a g h)")
        rawk = raw[:, :, :].rearrange("p s (k n) -> p s k n", n=P)
        whk = wh[:, :, :].rearrange("p s (k n) -> p s k n", n=P)
        wlk = wl[:, :, :].rearrange("p s (k n) -> p s k n", n=P)
        rawc = raw[:, :, :].rearrange("p s (k n) -> p s k n", n=512)
        whc = wh[:, :, :].rearrange("p s (k n) -> p s k n", n=512)
        wlc = wl[:, :, :].rearrange("p s (k n) -> p s k n", n=512)

        def mrg_step(b):
            return sum(MRG_DMAS[j % 3] for j in range(6) if (S_MRG + j) % 2 == b)

        def mrg_raw(j):
            return raw_value(S_MRG + j)

        def tap(c, l, part):
            w = par[:, P_CW + l * CT + c:P_CW + l * CT + c + 1]
            if part == 0:
                return w, ext[:, c, l:l + SEQ], yc[:, c, 0:SEQ]
            return (w, ext[:, c, HIST + SEQ:EXT].rearrange("p (b t) -> p b t", t=SB_S)[:, :, l:l + DT],
                    yc[:, c, SEQ:NT].rearrange("p (b t) -> p b t", t=DT))

        block = ctx.enter_context(nc.Block())

        @block.sync
        def _(sp):
            for i in range(4):
                sp.dma_start(x[:, i, :], x_prompt[0, i * P:(i + 1) * P, :]).then_inc(x_in[i], 16)
            sp.dma_start(x[0:NS, 4, :], xs_v).then_inc(x_in[4], 16)

            def ring_free(s):
                sp.wait_ge(hi_done, s - 1)
                sp.wait_ge(lo_done, s - 1)

            def col_tile(s, v, c0, n=P):
                if s >= 2:
                    ring_free(s)
                dst = rawk[:, s % 2] if n == P else raw[:, s % 2, 0:KT * n].rearrange("p (k n) -> p k n", n=n)
                sp.dma_start(dst, v[:, :, c0:c0 + n]).then_inc(raw_in[s % 2], 16)

            for c in range(CT):
                col_tile(S_GLU + 2 * c, w_in_v, OFF_GLU + CH + c * P)
                col_tile(S_GLU + 2 * c + 1, w_in_v, OFF_GLU + c * P)
            for j in range(6):
                col_tile(S_KV + j, w_in_v, OFF_KV + j * P)
            for r in range(G):
                s = S_Q + r
                ring_free(s)
                for g in range(KVH):
                    c0 = (g * G + r) * HD
                    sp.dma_start(rawk[:, s % 2, :, g * HD:(g + 1) * HD], w_in_v[:, :, c0:c0 + HD])\
                      .then_inc(raw_in[s % 2], 16)
            col_tile(S_GATE, w_in_v, OFF_GATE, 24)
            with sp.Fori(0, KT // 2) as i:
                for j in range(6):
                    b = (S_MRG + j) % 2
                    c1 = sp.snap((2 * i + j // 3 + 1) * P + (OFF_MRG + (j % 3) * D if j % 3 < 2 else 0))
                    split = sp.snap(6 * i + (S_MRG + j - 1))
                    sp.wait_ge(lo_done, split)
                    if j % 3 < 2:
                        sp.dma_start(rawk[:, b], w_in_v[:, :, bass.ds(c1 - P, P)]).then_inc(raw_in[b], 16)
                    else:
                        for g in range(KVH):
                            sp.dma_start(rawk[g * HD:(g + 1) * HD, b, 0:G], w_ao_v[g, :, :, bass.ds(c1 - P, P)])\
                              .then_inc(raw_in[b], 16)
                        sp.dma_start(rawk[:, b, G:KT], w_co_v[:, :, bass.ds(c1 - P, P)]).then_inc(raw_in[b], 16)
            for half in range(2):
                for kc in range(KT // 2):
                    s = S_OUT + half * (KT // 2) + kc
                    ring_free(s)
                    sp.dma_start(rawc[:, s % 2], w_out_v[:, 2 * kc:2 * kc + 2, half * 512:(half + 1) * 512])\
                      .then_inc(raw_in[s % 2], 16)
            with sp.Fori(0, FT) as i:
                for j in range(2):
                    b = (S_UP + j) % 2
                    c1 = sp.snap((i + 1) * P + j * FF)
                    split = sp.snap(2 * i + (S_UP + j - 1))
                    sp.wait_ge(lo_done, split)
                    sp.dma_start(rawk[:, b], w_up_v[:, :, bass.ds(c1 - P, P)]).then_inc(raw_in[b], 16)
            for half in range(2):
                for kc in range(FT // 2):
                    s = S_DOWN + half * (FT // 2) + kc
                    ring_free(s)
                    sp.dma_start(rawc[:, s % 2], w_down_v[:, 2 * kc:2 * kc + 2, half * 512:(half + 1) * 512])\
                      .then_inc(raw_in[s % 2], 16)
            for i in range(TT):
                sp.wait_ge(y_ok, i + 1)
                dst = y_prompt[0, i * P:(i + 1) * P, :] if i < 4 else ys_v
                sp.dma_start(dst, x1[0:ROWS[i], i, :]).then_inc(y_out, 16)
            sp.wait_ge(y_out, 16 * TT)

        @block.gpsimd
        def _(pool):
            pool.dma_start(ptab[:, :], page_table.rearrange("b j -> (b j)").unsqueeze(0)).then_inc(ptab_in, 16)
            init = [0]

            def fill(t, v):
                pool.wait_ge(pool_init, init[0])
                nc.gpsimd.memset(t, v).then_inc(pool_init, 1)
                init[0] += 1

            def select(t, op, fillv, b0, pattern, cm):
                pool.wait_ge(pool_init, init[0])
                nc.gpsimd.affine_select(out=t, in_=t, compare_op=op, fill=fillv, base=b0, pattern=pattern,
                                        channel_multiplier=cm).then_inc(pool_init, 1)
                init[0] += 1

            fill(ident[:, :], 0.0)
            select(ident[:, :], ALU.not_equal, 1.0, 0, [[-1, P]], 1)
            pool.wait_ge(pool_init, init[0])
            nc.gpsimd.tensor_copy(identb[:, :], ident[:, :]).then_inc(const_ok, 1)
            pool.wait_ge(ptab_in, 16)

            def load_page(n):
                if n >= 2:
                    pool.wait_ge(past_t, n - 1)
                    pool.wait_ge(vcopy, 2 * (n - 1))
                pg = pool.value_load(ptab[0:1, n:n + 1], min_val=0, max_val=cache_kv.shape[1] - 1)
                pool.dma_start(page[:, n % 2, 0:512], cache_v[bass.ds(pg, 1)].rearrange("a t n -> (a t) n"))\
                    .then_inc(page_in[n % 2], 16)
                pool.dma_start(page[:, n % 2, 512:768], swin_v[n]).then_inc(page_in[n % 2], 16)

            load_page(0)
            load_page(1)
            fill(causal[:, :], 0.0)
            select(causal[:, :], ALU.is_ge, NEG, 0, [[-1, P]], 1)
            fill(rowsel[:, :, :], 1.0)
            for g in range(KVH):
                select(rowsel[g * HD:(g + 1) * HD, :, :].rearrange("k h p -> k (h p)"), ALU.is_equal, 0.0, 0,
                       [[-DT, DB], [0, G], [-1, DT]], 1)
            fill(newmask[:, :], 0.0)
            for g in range(KVH):
                rows = slice(g * HD, (g + 1) * HD)
                select(newmask[rows, :], ALU.is_ge, NEG, 0, [[-1, NS]], 1)
                select(newmask[rows, :], ALU.is_ge, NEG, DT - 1, [[DT, DB], [0, DT]], -1)
            fill(cmpmask[:, :], 0.0)
            for g in range(KVH):
                rows = slice(g * HD, (g + 1) * HD)
                select(cmpmask[rows, :], ALU.is_ge, NEG, 0, [[-DT, DB], [0, NCS]], 1)
                select(cmpmask[rows, :], ALU.is_ge, NEG, DT - 1, [[DT, DB], [0, NCS]], -1)
            fill(rselT[:, :], 1.0)
            select(rselT[:, :], ALU.is_equal, 0.0, 0, [[0, 4], [-1, G], [0, DT]], 1)
            fill(cneg[:, :, :], 0.0)
            select(cneg[:, :, :], ALU.is_ge, NEG, 1 - CL, [[P, 4], [-CS, NCP]], 1)
            fill(c01[:, :, :], 1.0)
            select(c01[:, :, :], ALU.is_ge, 0.0, 1 - CL, [[P, 4], [-CS, NCP]], 1)
            fill(phi[:, :, :], 0.0)
            pool.wait_ge(pool_init, init[0])
            nc.gpsimd.memset(mean_w[:, :], 1.0 / CH).then_inc(const_ok, 1)

            def load_phi(w):
                for g in range(KVH):
                    pool.dma_start(phi[g * HD:(g + 1) * HD, :, g * HD:(g + 1) * HD],
                                   w[0].rearrange("(l h) e -> h l e", h=HD)).then_inc(phi_in, 16)

            load_phi(w_phi_k)
            for g in range(KVH):
                for q, b in enumerate((b_phi_k, b_phi_v)):
                    pool.dma_start(bphi[g * HD:(g + 1) * HD, q:q + 1], b[0].unsqueeze(1)).then_inc(bphi_in, 16)
            for n in range(NPG):
                pool.wait_ge(page_in[n % 2], 32 * (n // 2 + 1))
                nc.gpsimd.tensor_copy(vsel[:, n, :], page[:, n % 2, 384:512]).then_inc(vcopy, 1)
                nc.gpsimd.tensor_copy(vwin[:, n, :], page[:, n % 2, 640:768]).then_inc(vcopy, 1)
                if n + 2 < NPG:
                    load_page(n + 2)
            pool.dma_start(wins_v[:, 0:PAST, :], state_kv_win[0].rearrange("b t a g h -> b t (a g h)"))\
                .then_inc(win_out, 16)
            for j in range(2):
                pool.wait_ge(kv_ok, j + 1)
                nc.gpsimd.tensor_copy(cc[:, j, 0:SEQ], kvT[:, j, 0:SEQ]).then_inc(cc_ok, 1)
            pool.wait_ge(cmp_mm, 1)
            load_phi(w_phi_v)
            for l in range(1, CW):
                pool.wait_ge(conv_prod, 2 * (l + 1))
                if l > 1:
                    pool.wait_ge(conv_3, l - 1)
                nc.gpsimd.tensor_tensor(yc[:, CT - 1, :], yc[:, CT - 1, :], cprod[:, l % 4, :], ALU.add)\
                    .then_inc(conv_3, 1)
            for n, (q, r, g, c) in enumerate(UNITS):
                pool.wait_ge(rinv_ok, n + 1)
                gate = gtok[:, q, c * HEADS + g * G + r:c * HEADS + g * G + r + 1] if q < 4 \
                    else gsel[:, q - 4, c * KVH + g:c * KVH + g + 1]
                w = probs[:, n % 3, 0:width(n)]
                nc.gpsimd.tensor_scalar(w, w, rinv[:, n:n + 1], gate, ALU.mult, ALU.mult).then_inc(scaled, 1)
            with pool.Fori(0, KT // 2) as i:
                for j in range(2):
                    pool.wait_ge(m_ok, 2 * i + j)
                    pool.wait_ge(m_mul, 4 * i + 2 * j + 2)
                    nc.gpsimd.tensor_tensor(msum[:, j, :], ms[:, j, 0, :], ms[:, j, 1, :], ALU.add)\
                        .then_inc(m_sum, 1)
            pool.wait_ge(m_ok, KT)
            for i in range(TT):
                src = x_prompt[0, i * P:(i + 1) * P, :] if i < 4 else xs_v
                pool.dma_start(x1[0:ROWS[i], i, :], src).then_inc(x1_in, 16)
            pool.wait_ge(slot_used, S_OUT)
            pool.dma_start(sf[:, :], state_ffn[0].rearrange("b t f -> (b t) f")).then_inc(sf_in, 16)
            pool.dma_start(gpost[:, :], g_mix_post[0].partition_broadcast(P)).then_inc(gp_in, 16)
            with pool.Fori(0, FT) as i:
                pool.wait_ge(h_ok, i)
                pool.wait_ge(cv_step, 6 * i + 6)
                pool.wait_ge(act_ok, i + 1)
                nc.gpsimd.tensor_tensor(hs[:, 0:SEQ], cv[:, 0, 0:SEQ], cv[:, 1, 0:SEQ], ALU.mult)\
                    .then_inc(h_mul, 1)
                nc.gpsimd.tensor_tensor(
                    hs[:, SEQ:NT].rearrange("p (b t) -> p b t", t=DT),
                    cv[:, 0, SEQ:CEXT].rearrange("p (b t) -> p b t", t=DT + 2)[:, :, 2:DT + 2],
                    cv[:, 1, SEQ:CEXT].rearrange("p (b t) -> p b t", t=DT + 2)[:, :, 2:DT + 2],
                    ALU.mult).then_inc(h_mul, 1)
            pool.wait_ge(h_ok, FT)
            pool.dma_start(gpost2[:, :], g_ffn_post[0].partition_broadcast(P)).then_inc(gp2_in, 16)
            pool.wait_ge(ul_ev, 11)
            pool.dma_start(ffn_prompt[0, 0], ustage[0:2, :]).then_inc(ffn_out, 16)
            pool.dma_start(ffn_sample[0].rearrange("b t f -> (b t) f"), ustage[2:18, :]).then_inc(ffn_out, 16)
            pool.wait_ge(win_out, 16)
            pool.wait_ge(kv_out, 16 * (4 * 2 + 1 + DB))
            pool.wait_ge(cst_out, 16 * (1 + DB))
            pool.wait_ge(ffn_out, 32)

        @block.scalar
        def _(act):
            v = ffn_conv_w[0].rearrange("w (t p) -> (w t) p", p=P)
            act.dma_start(par_raw[:, 0, :], v[0:P, :]).then_inc(par_in, 16)
            act.dma_start(par_raw[0:P_CW - P, 1, :], v[P:P_CW, :]).then_inc(par_in, 16)
            act.dma_start(par_raw[P_CW - P:P_FB - P, 1, :], conv_w[0].rearrange("w (t p) -> (w t) p", p=P))\
                .then_inc(par_in, 16)
            for vec, col in ((ffn_conv_b, P_FB), (conv_b, P_CB), (g_mix_pre, P_GPRE), (g_ffn_pre, P_GFFN),
                             (conv_ln_g, P_LNG), (conv_ln_b, P_LNB)):
                rows = vec[0].rearrange("(t p) -> t p", p=P)
                act.dma_start(par_raw[col - 2 * P:col - 2 * P + rows.shape[0], 2, :], rows).then_inc(par_in, 16)
            for hf in range(2):
                act.dma_start(scv[0:4 * HIST, hf, :], state_conv[0, 4 * hf:4 * hf + 4].rearrange("b t c -> (b t) c"))\
                    .then_inc(scv_in, 16)

            def hi(s):
                act.wait_ge(raw_in[s % 2], raw_value(s))
                if s >= 2:
                    act.wait_ge(slot_used, s - 1)
                n = KT * 24 if s == S_GATE else 1024
                nc.scalar.copy(wh[:, s % 2, 0:n], raw[:, s % 2, 0:n]).then_inc(hi_done, 1)

            for t in range(TT + 1):
                if t < TT:
                    m = ROWS[t]
                    act.wait_ge(x_in[t], 16)
                    nc.scalar.activation(sq_x[0:m, t, :], x[0:m, t, :], ACT.Square,
                                         accum_out=ss[0:m, t:t + 1]).then_inc(sq_done, 1)
                if t >= 1:
                    m = ROWS[t - 1]
                    act.wait_ge(rs_step, 2 * t)
                    nc.scalar.activation(rstd[0:m, t - 1:t], ss[0:m, t - 1:t], ACT.Sqrt).then_inc(rs_ok, 1)
            hi(0)
            hi(1)
            act.wait_ge(par_ok, 2)
            act.wait_ge(sq_done, TT)
            for k in range(KT):
                act.wait_ge(z_full, k + 1)
                nc.scalar.activation(zh[:, k, :], pf[:, 1024 * (k % 2):1024 * (k % 2) + NT], ACT.Copy,
                                     scale=par[:, P_GPRE + k:P_GPRE + k + 1]).then_inc(zhi_ok, 1)
            def cmp_bias(j):
                dst = (kcmp, vcmpT)[j]
                act.wait_ge(cmp_mm, j + 1)
                nc.scalar.activation(dst[:, 0:NCP], ps[:, 4 + j, 0:NCP], ACT.Identity, bias=bphi[:, j:j + 1])\
                    .then_inc(cmp_ok, 1)
                nc.scalar.activation(
                    dst[:, NCP:].rearrange("p (b n) -> p b n", n=NCS),
                    ps[:, 4 + j, SEQ // CS:SEQ // CS + DB * PAST // CS].rearrange("p (b n) -> p b n", b=DB)[:, :, 0:NCS],
                    ACT.Identity, bias=bphi[:, j:j + 1]).then_inc(cmp_ok, 1)

            def state_rows_out():
                act.wait_ge(vcopy, 2 * NPG)
                act.wait_ge(cst_t, 1)
                nc.scalar.copy(cst[96:96 + HIST, 2, :], ps[0:HIST, 5, :]).then_inc(cst_ok, 1)
                for q, (_, nb) in enumerate(SEQ_GROUPS):
                    act.wait_ge(cst_t, q + 2)
                    nc.scalar.copy(cst[0:nb * SB_S, q, :], ps[0:nb * SB_S, 5 + (q + 1) % 3, :]).then_inc(cst_ok, 1)
                act.wait_ge(cst_ok, 4)
                act.dma_start(conv_prompt[0, 0], cst[96:96 + HIST, 2, :]).then_inc(cst_out, 16)
                for b in range(DB):
                    r0 = (b % 3) * SB_S + DT
                    act.dma_start(conv_sample[0, b], cst[r0:r0 + HIST, b // 3, :]).then_inc(cst_out, 16)

            def kv_rows(i):
                act.wait_ge(ktok_t, i + 1)
                nc.scalar.copy(ktok[0:ROWS[i], i, :], pf[0:ROWS[i], 6 * 512:6 * 512 + 768]).then_inc(ktok_ok, 1)

            def kv_rows_out(i):
                act.wait_ge(ktok_ok, i + 1)
                if i < 4:
                    act.dma_start(kvp_v[i * P:(i + 1) * P, :], ktok[:, i, 0:512]).then_inc(kv_out, 16)
                    act.dma_start(winp_v[i * P:(i + 1) * P, :], ktok[:, i, 512:768]).then_inc(kv_out, 16)
                else:
                    act.dma_start(kvs_v, ktok[0:NS, i, 0:512]).then_inc(kv_out, 16)
                    for b in range(DB):
                        act.dma_start(wins_v[b, PAST:PAST + DT, :], ktok[b * DT:(b + 1) * DT, i, 512:768])\
                            .then_inc(kv_out, 16)

            def conv_products(l0, l1):
                for l in range(l0, l1):
                    if l == 0:
                        act.wait_ge(hist_ok, 2 * CT)
                        act.wait_ge(glu_p, CT)
                        act.wait_ge(glu_ok, CT)
                    if l >= 5:
                        act.wait_ge(conv_3, l - 4)
                    for part in range(2):
                        w, src, dst = tap(CT - 1, l, part)
                        if l == 0:
                            nc.scalar.activation(dst, src, ACT.Identity, bias=par[:, P_CB + CT - 1:P_CB + CT],
                                                 scale=w).then_inc(conv_prod, 1)
                            continue
                        prod = cprod[:, l % 4, 0:SEQ] if part == 0 \
                            else cprod[:, l % 4, SEQ:NT].rearrange("p (b t) -> p b t", t=DT)
                        nc.scalar.activation(prod, src, ACT.Copy, scale=w).then_inc(conv_prod, 1)

            for s in range(S_MRG):
                hi(s + 2)
                e = s
                if s < S_KV:
                    if s % 2 == 0:
                        act.wait_ge(glu_p, s // 2)
                        act.wait_ge(glu_ok, s // 2)
                        nc.scalar.activation(sg[:, :], pair(e % 2), ACT.Sigmoid).then_inc(sg_ok, 1)
                elif s < S_Q:
                    nc.scalar.copy(kvT[:, s - S_KV, :], pair(e % 2)).then_inc(kv_ok, 1)
                elif s < S_GATE:
                    nc.scalar.mul(qT[:, s - S_Q, :], pair(e % 2), HD ** -0.5).then_inc(q_ok, 1)
                else:
                    nc.scalar.activation(gT[:, :], pair(e % 2, m=24), ACT.Sigmoid).then_inc(gt_ok, 1)
                if s == S_CMP_K + 1:
                    act.wait_ge(bphi_in, 64)
                    cmp_bias(0)
                if s == S_CMP_V + 1:
                    cmp_bias(1)
                if s > S_CMP_K:
                    n = S_GATE - S_CMP_K
                    conv_products(CW * (s - S_CMP_K - 1) // n, CW * (s - S_CMP_K) // n)
                if s == S_CST:
                    state_rows_out()
                if s >= S_TOK and s < S_GATE:
                    kv_rows(s - S_TOK)
                    if s > S_TOK:
                        kv_rows_out(s - S_TOK - 1)
                if s == S_GATE - 1:
                    kv_rows(TT - 1)
                    kv_rows_out(TT - 2)
                    act.wait_ge(vc_t, 1)
                    nc.scalar.copy(vcp[:, :], ps[0:NCP, 4, 0:P]).then_inc(vc_ok, 1)
                    nc.scalar.copy(vcs[:, :], ps[0:DB * NCS, 4, P:2 * P]).then_inc(vc_ok, 1)
            act.wait_ge(q_ok, G)
            nc.scalar.copy(qs[:, :, :].rearrange("p h (b r t) -> p (h b) r t", r=G, t=DT),
                           qT[:, :, SEQ:NT].rearrange("p r (b t) -> p b r t", t=DT)).then_inc(qs_ok, 1)
            act.wait_ge(mid_t, 1)
            nc.scalar.copy(gtok[:, 0:4, :], ps[:, 5, 0:96].rearrange("p (i c) -> p i c", c=24)).then_inc(gtok_ok, 1)
            nc.scalar.copy(gtok[0:NS, 4, :], ps[0:NS, 5, 96:120]).then_inc(gtok_ok, 1)

            def cmp_exp(i):
                act.wait_ge(ce_in, i + 1)
                if i >= 1:
                    act.wait_ge(pc_ok, i)
                nc.scalar.activation(se[:, :, :], sc[:, :, :], ACT.Exp).then_inc(ce_ok, 1)

            kv_rows_out(TT - 1)
            act.wait_ge(cst_out, 16 * (1 + DB))
            cmp_exp(0)
            act.wait_ge(conv_3, CW - 1)
            for n in range(NU + 4):
                if n < NU:
                    act.wait_ge(nmax_ok, n + 1)
                    if n >= 3:
                        act.wait_ge(pt_full, n - 2)
                    nc.scalar.activation(probs[:, n % 3, 0:width(n)], ps[:, n % 3, 0:width(n)], ACT.Exp,
                                         bias=nmax[:, n:n + 1], accum_out=esum[:, n:n + 1]).then_inc(exp_ok, 1)
                for i in range(1, 4):
                    if n == FIRST[i] - 6:
                        cmp_exp(i)
                for q in range(6):
                    if n == LAST[q] + 3:
                        act.wait_ge(pv_done, LAST[q] + 1)
                        if q < 4:
                            nc.scalar.copy(oh[:, :, q * P:(q + 1) * P],
                                           ps[:, 5 + q % 2, :].rearrange("p (r t) -> p r t", r=G)).then_inc(oh_ok, 1)
                        else:
                            t0 = SEQ + (q - 4) * (NS // 2)
                            nc.scalar.copy(oh[:, :, t0:t0 + NS // 2].rearrange("p r (b t) -> p b r t", t=DT),
                                           ps[:, 5 + q % 2, 0:P].rearrange("p (b r t) -> p b r t", r=G, t=DT))\
                                .then_inc(oh_ok, 1)
            for c in range(CT):
                act.wait_ge(ln_xc, c + 1)
                nc.scalar.activation(lnsq[:, c, :], yc[:, c, :], ACT.Square).then_inc(ln_sq, 1)
            act.wait_ge(ln_step, 2)
            nc.scalar.activation(lnr[:, :], lnv[:, :], ACT.Sqrt).then_inc(ln_rs, 1)
            act.wait_ge(ln_var, 1)
            for c in range(CT):
                act.wait_ge(ln_xn, c + 1)
                nc.scalar.activation(lnsq[:, c, :], yc[:, c, :], ACT.Silu, bias=par[:, P_LNB + c:P_LNB + c + 1],
                                     scale=par[:, P_LNG + c:P_LNG + c + 1]).then_inc(silu_ok, 1)
            with act.Fori(0, KT // 2) as i:
                for j in range(6):
                    b = (S_MRG + j) % 2
                    act.wait_ge(raw_in[b], 16 * mrg_step(b) * i + mrg_raw(j + 2))
                    act.wait_ge(slot_used, 6 * i + (S_MRG + j + 1))
                    nc.scalar.copy(wh[:, b, :], raw[:, b, :]).then_inc(hi_done, 1)
                    if j % 3 < 2:
                        act.wait_ge(m_sum, 2 * i + j // 3)
                        nc.scalar.activation(ms[:, j // 3, j % 3, :], pair(j % 3), ACT.Sigmoid).then_inc(m_sig, 1)

            for kc in range(KT // 2):
                hi(S_OUT + kc + 2)

            def square(i, half, s_end, junk_i, done):
                if half == 1 and i < TT - 1:
                    act.wait_ge(o_tile if s_end == S_UP else d_tile, i + 1)
                else:
                    act.wait_ge(slot_used, s_end)
                m = ROWS[i]
                nc.scalar.activation(junk_i[0:m], ps[0:m, (half * TT + i) % 8, :], ACT.Square,
                                     accum_out=ssh[0:m, half, i:i + 1]).then_inc(done, 1)

            for i in range(TT):
                square(i, 0, S_OUT + KT // 2, junk[:, i, 0:512], o_sq)
            for kc in range(KT // 2, KT - 1):
                hi(S_OUT + kc + 2)
            for t in range(TT + 2):
                if t < TT:
                    square(t, 1, S_UP, junk[:, t, 512:1024], o_sq)
                    act.wait_ge(rs2_step, 2 * t + 2)
                    m = ROWS[t]
                    nc.scalar.activation(rstd[0:m, t:t + 1], ss[0:m, t:t + 1], ACT.Sqrt).then_inc(rs2, 1)
                if 1 <= t <= TT:
                    i, m = t - 1, ROWS[t - 1]
                    act.wait_ge(x1_ok, i + 1)
                    act.wait_ge(o_sq, 2 * TT if t == TT else TT + t + 1)
                    nc.scalar.activation(junk[0:m, i, :], x1[0:m, i, :], ACT.Square,
                                         accum_out=ss[0:m, i:i + 1]).then_inc(sq3, 1)
                if t >= 2:
                    i, m = t - 2, ROWS[t - 2]
                    act.wait_ge(rs3_step, 2 * i + 2)
                    nc.scalar.activation(rstd[0:m, i:i + 1], ss[0:m, i:i + 1], ACT.Sqrt).then_inc(rs3, 1)
                    if i % 2 == 0:
                        act.wait_ge(rs3, i + 1)
                        nc.scalar.activation(hb[0:m, i, :], x1[0:m, i, :], ACT.Copy, scale=rstd[0:m, i:i + 1])\
                            .then_inc(xn2, 1)
            hi(S_UP + 1)
            for k in range(KT):
                act.wait_ge(z2_full, k + 1)
                nc.scalar.activation(zh[:, k, :], pf[:, 1024 * (k % 2):1024 * (k % 2) + NT], ACT.Copy,
                                     scale=par[:, P_GFFN + k:P_GFFN + k + 1]).then_inc(z2_hi, 1)
            act.wait_ge(u_pad, 1)
            with act.Fori(0, FT) as i:
                for j in range(2):
                    b = (S_UP + j) % 2
                    act.wait_ge(raw_in[b], 16 * i + raw_value(S_UP + j + 2))
                    act.wait_ge(slot_used, 2 * i + (S_UP + j + 1))
                    nc.scalar.copy(wh[:, b, :], raw[:, b, :]).then_inc(hi_done, 1)
                    act.wait_ge(cv_step, 6 * i)
                    nc.scalar.copy(u[:, j, 2:2 + SEQ], pair(j, 0, SEQ)).then_inc(u_ev[j], 1)
                    nc.scalar.copy(u[:, j, 2 + SEQ:UEXT].rearrange("p (b t) -> p b t", t=DT + 2)[:, :, 2:DT + 2],
                                   pair(j, SEQ, NT).rearrange("p (b t) -> p b t", t=DT)).then_inc(u_ev[j], 1)
                act.wait_ge(cv_step, 6 * i + 3)
                nc.scalar.activation(cv[:, 0, :], cv[:, 0, :], ACT.Gelu_apprx_tanh).then_inc(act_ok, 1)

            for kc in range(FT // 2):
                hi(S_DOWN + kc + 2)
                for q in range(2 * kc, min(2 * kc + 2, 11)):
                    act.wait_ge(ul_t, q + 1)
                    nc.scalar.copy(ustage[:, q * 512:(q + 1) * 512], ps[0:18, 5 + q % 3, :]).then_inc(ul_ev, 1)
            act.wait_ge(ffn_out, 32)
            act.wait_ge(gp2_in, 16)
            for half in range(2):
                for i in range(TT):
                    jk = junk2[:, i, half * 512:(half + 1) * 512] if i < 4 else junk3[:, half * 512:(half + 1) * 512]
                    square(i, half, S_DOWN + (half + 1) * (FT // 2), jk, d_sq)
                    if half == 1:
                        act.wait_ge(rs4_step, 2 * i + 2)
                        m = ROWS[i]
                        nc.scalar.activation(rstd[0:m, i:i + 1], ss[0:m, i:i + 1], ACT.Sqrt).then_inc(rs4, 1)
                if half == 0:
                    for kc in range(FT // 2, FT - 2):
                        hi(S_DOWN + kc + 2)

        @block.vector
        def _(dve):
            def lo(s):
                dve.wait_ge(hi_done, s + 1)
                n = KT * 24 if s == S_GATE else 1024
                nc.vector.tensor_tensor(wl[:, s % 2, 0:n], raw[:, s % 2, 0:n], wh[:, s % 2, 0:n].bitcast(F32),
                                        ALU.subtract).then_inc(lo_done, 1)

            nc.vector.memset(ext[:, :, 0:HIST], 0.0).then_inc(ext0, 1)
            for t in range(TT + 1):
                if t < TT:
                    m = ROWS[t]
                    dve.wait_ge(sq_done, t + 1)
                    nc.vector.tensor_scalar(ss[0:m, t:t + 1], ss[0:m, t:t + 1], 1.0 / D, EPS, ALU.mult, ALU.add)\
                        .then_inc(rs_step, 1)
                    dve.wait_ge(rs_step, 2 * t + 1)
                    nc.vector.reciprocal(ss[0:m, t:t + 1], ss[0:m, t:t + 1]).then_inc(rs_step, 1)
                if t >= 1:
                    i, m = t - 1, ROWS[t - 1]
                    dve.wait_ge(rs_ok, i + 1)
                    nc.vector.tensor_scalar(x[0:m, i, :], x[0:m, i, :], rstd[0:m, i:i + 1], None,
                                            ALU.mult).then_inc(xn_ok, 1)
            dve.wait_ge(par_t, 1)
            nc.vector.tensor_copy(par[:, 0:2 * P], ps[:, 6, 0:2 * P]).then_inc(par_ok, 1)
            nc.vector.tensor_copy(par[:, 2 * P:P_ALL], ps[:, 6, 2 * P:P_ALL]).then_inc(par_ok, 1)
            for hf in range(2):
                dve.wait_ge(scv_t, hf + 1)
                for c in range(CT):
                    b0 = HIST + SEQ + 4 * hf * SB_S
                    nc.vector.tensor_copy(
                        ext[:, c, b0:b0 + 4 * SB_S].rearrange("p (b t) -> p b t", t=SB_S)[:, :, 0:HIST],
                        ps[:, 4 + hf, c * 120:(c + 1) * 120].rearrange("p (b t) -> p b t", t=HIST)).then_inc(hist_ok, 1)
            for k in range(KT):
                dve.wait_ge(zhi_ok, k + 1)
                nc.vector.scalar_tensor_tensor(zl[:, k, :], pf[:, 1024 * (k % 2):1024 * (k % 2) + NT],
                                               par[:, P_GPRE + k:P_GPRE + k + 1], zh[:, k, :].bitcast(F32),
                                               ALU.mult, ALU.subtract).then_inc(z_ok, 1)
            lo(0)
            lo(1)

            def past(n):
                dve.wait_ge(past_t, n + 1)
                bk = 4 + n % 4
                nc.vector.tensor_copy(cc[:, :, SEQ + n * P:SEQ + (n + 1) * P],
                                      ps[:, bk, 0:256].rearrange("p (j t) -> p j t", j=2)).then_inc(past_ev, 1)
                nc.vector.tensor_copy(kpast[:, :, n * P:(n + 1) * P],
                                      ps[:, bk, 256:512].rearrange("p (j t) -> p j t", j=2)).then_inc(past_ev, 1)

            def conv_taps(done, tiles, l0, l1):
                for l in range(l0, l1):
                    for part in range(2):
                        for n, c in enumerate(tiles):
                            w, src, dst = tap(c, l, part)
                            if l == 0:
                                if part == 0 and n == 0:
                                    dve.wait_ge(hist_ok, 2 * CT)
                                    dve.wait_ge(ext0, 1)
                                    dve.wait_ge(glu_p, tiles[-1] + 1)
                                    dve.wait_ge(glu_ok, tiles[-1] + 1)
                                nc.vector.tensor_scalar(dst, src, w, par[:, P_CB + c:P_CB + c + 1], ALU.mult,
                                                        ALU.add).then_inc(done, 1)
                            else:
                                dve.wait_ge(done, (2 * (l - 1) + part) * len(tiles) + n + 1)
                                nc.vector.scalar_tensor_tensor(dst, src, w, dst, ALU.mult, ALU.add)\
                                    .then_inc(done, 1)

            for s in range(S_MRG):
                lo(s + 2)
                e = s
                if s < S_KV:
                    past(2 * s)
                    past(2 * s + 1)
                    if s % 2:
                        c = s // 2
                        dve.wait_ge(sg_ok, c + 1)
                        dve.wait_ge(slot_used, s + 1)
                        nc.vector.tensor_tensor(ext[:, c, HIST:HIST + SEQ], sg[:, 0:SEQ], pair(e % 2, 0, SEQ),
                                                ALU.mult).then_inc(glu_p, 1)
                        nc.vector.tensor_tensor(
                            ext[:, c, HIST + SEQ:EXT].rearrange("p (b t) -> p b t", t=SB_S)[:, :, HIST:SB_S],
                            sg[:, SEQ:NT].rearrange("p (b t) -> p b t", t=DT),
                            pair(e % 2, SEQ, NT).rearrange("p (b t) -> p b t", t=DT), ALU.mult)\
                            .then_inc(glu_ok, 1)
                for done, tiles in ((conv_01, (0, 1)), (conv_2, (2,))):
                    s0 = S_GLU + 2 * (tiles[-1] + 1)
                    if s >= s0:
                        conv_taps(done, tiles, CW * (s - s0) // (S_MRG - s0), CW * (s + 1 - s0) // (S_MRG - s0))
            cstep = [0]

            def link(ins):
                cstep[0] += 1
                ins.then_inc(cs_step, 1)
                dve.wait_ge(cs_step, cstep[0])

            def cmp_soft(i):
                dve.wait_ge(cs_full, i + 1)
                link(nc.vector.tensor_tensor(
                    sc[:, :, :], ps[:, 7, 0:HEADS * 32].rearrange("p (h n) -> p h n", n=32)[:, :, 0:NCP],
                    cneg[:, i, :].unsqueeze(1).broadcast_to([P, HEADS, NCP]), ALU.add))
                link(nc.vector.tensor_reduce(cmax[:, :], sc[:, :, :], AX.X, ALU.max))
                nc.vector.tensor_tensor(sc[:, :, :], sc[:, :, :],
                                        cmax[:, :].unsqueeze(2).broadcast_to([P, HEADS, NCP]),
                                        ALU.subtract).then_inc(ce_in, 1)

            def cmp_norm(i):
                dve.wait_ge(ce_ok, i + 1)
                if i >= 1:
                    dve.wait_ge(pct_full, 2 * i)
                link(nc.vector.tensor_tensor(se[:, :, :], se[:, :, :],
                                             c01[:, i, :].unsqueeze(1).broadcast_to([P, HEADS, NCP]), ALU.mult))
                link(nc.vector.tensor_reduce(csum[:, :], se[:, :, :], AX.X, ALU.add))
                link(nc.vector.tensor_scalar(csum[:, :], csum[:, :], TINY, None, ALU.max))
                link(nc.vector.reciprocal(csum[:, :], csum[:, :]))
                link(nc.vector.tensor_tensor(cgate[:, :], csum[:, :], gtok[:, i, 0:HEADS], ALU.mult))
                nc.vector.tensor_tensor(sm[:, :, :], se[:, :, :],
                                        cgate[:, :].unsqueeze(2).broadcast_to([P, HEADS, NCP]),
                                        ALU.mult).then_inc(pc_ok, 1)

            def cmp_turn(i, hf):
                dve.wait_ge(pct_full, 2 * i + hf + 1)
                if i >= 2:
                    dve.wait_ge(pv_done, LAST[i - 2] + 1)
                nc.vector.tensor_copy(pcT[:, i % 2, 4 * hf:4 * hf + 4, :].rearrange("p h t -> p (h t)"),
                                      ps[0:NCP, 7, :]).then_inc(pct_ok, 1)

            dve.wait_ge(cst_out, 16 * (1 + DB))
            cmp_soft(0)
            dve.wait_ge(gsel_mm, 1)
            nc.vector.tensor_copy(rsel[:, :], ps[:, 5, 256:256 + G]).then_inc(rsel_ok, 1)
            dve.wait_ge(rsel_ok, 1)
            for hf in range(2):
                nc.vector.tensor_tensor(
                    gsel4[:, hf], ps[:, 5, 128 + 32 * hf:128 + 32 * hf + 24].rearrange("p (c r) -> p c r", r=G),
                    rsel[:, :].unsqueeze(1).broadcast_to([P, 6, G]), ALU.mult).then_inc(rsel_ok, 1)
            dve.wait_ge(rsel_ok, 3)
            nc.vector.tensor_reduce(gsel[:, :, :].rearrange("p h c -> p (h c)"),
                                    gsel4[:, :, :, :].rearrange("p h c r -> p (h c) r"), AX.X, ALU.add)\
                .then_inc(gsel_ok, 1)
            dve.wait_ge(gsel_ok, 1)
            dve.wait_ge(gtok_ok, 2)
            cmp_norm(0)
            for n in range(NU + 4):
                if n < NU:
                    dve.wait_ge(s_full, n + 1)
                    nc.vector.tensor_reduce(nmax[:, n:n + 1], ps[:, n % 3, 0:width(n)], AX.X, ALU.max, negate=True)\
                        .then_inc(nmax_ok, 1)
                if 1 <= n <= NU:
                    dve.wait_ge(exp_ok, n)
                    nc.vector.reciprocal(rinv[:, n - 1:n], esum[:, n - 1:n]).then_inc(rinv_ok, 1)
                if 2 <= n < NU + 2:
                    m = n - 2
                    q, _, _, c = UNITS[m]
                    dve.wait_ge(pt_full, m + 1)
                    if m >= 3:
                        dve.wait_ge(pv_done, m - 2)
                    if q < 4:
                        nc.vector.tensor_copy(pT[:, m % 3, 0:width(m)], ps[:, 3 + m % 2, 0:width(m)]).then_inc(pt_ok, 1)
                    elif c == 0:
                        nc.vector.tensor_copy(pT[0:DB * NCS, m % 3, 0:P], ps[0:DB * NCS, 3 + m % 2, 0:P])\
                            .then_inc(pt_ok, 1)
                    else:
                        nc.vector.tensor_copy(pT[:, m % 3, 0:PAST], ps[:, 3 + m % 2, 0:PAST]).then_inc(pt_part, 1)
                        nc.vector.tensor_copy(pT[0:NS, m % 3, PAST:PAST + P], ps[0:NS, 3 + m % 2, PAST:PAST + P])\
                            .then_inc(pt_ok, 1)
                for i in range(4):
                    if n == FIRST[i] - 7:
                        cmp_soft(i)
                    if n == FIRST[i] - 5:
                        cmp_norm(i)
                    if n == (FIRST[i] - 2 if i else 1):
                        cmp_turn(i, 0)
                    if n == (FIRST[i] if i else 2):
                        cmp_turn(i, 1)
                for q in range(6):
                    if n == LAST[q] + 3:
                        dve.wait_ge(oh_ok, q + 1)
                        if q < 4:
                            nc.vector.tensor_tensor(
                                ol[:, :, q * P:(q + 1) * P], ps[:, 5 + q % 2, :].rearrange("p (r t) -> p r t", r=G),
                                oh[:, :, q * P:(q + 1) * P].bitcast(F32), ALU.subtract).then_inc(ol_ok, 1)
                        else:
                            t0 = SEQ + (q - 4) * (NS // 2)
                            nc.vector.tensor_tensor(
                                ol[:, :, t0:t0 + NS // 2].rearrange("p r (b t) -> p b r t", t=DT),
                                ps[:, 5 + q % 2, 0:P].rearrange("p (b r t) -> p b r t", r=G, t=DT),
                                oh[:, :, t0:t0 + NS // 2].bitcast(F32).rearrange("p r (b t) -> p b r t", t=DT),
                                ALU.subtract).then_inc(ol_ok, 1)
            dve.wait_ge(ln_mean, 1)
            for c in range(CT):
                nc.vector.tensor_tensor(yc[:, c, :], yc[:, c, :], pair(0), ALU.subtract).then_inc(ln_xc, 1)
            dve.wait_ge(ln_var, 1)
            nc.vector.tensor_scalar(lnv[:, :], pair(1), EPS, None, ALU.add).then_inc(ln_step, 1)
            dve.wait_ge(ln_step, 1)
            nc.vector.reciprocal(lnv[:, :], lnv[:, :]).then_inc(ln_step, 1)
            dve.wait_ge(ln_rs, 1)
            dve.wait_ge(ln_sq, CT)
            dve.wait_ge(ln_xc, CT)
            for c in range(CT):
                nc.vector.tensor_tensor(yc[:, c, :], yc[:, c, :], lnr[:, :], ALU.mult).then_inc(ln_xn, 1)
            for c in range(CT):
                dve.wait_ge(silu_ok, c + 1)
                nc.vector.tensor_copy(ch[:, c, :], lnsq[:, c, :]).then_inc(c_step, 1)
                dve.wait_ge(c_step, 2 * c + 1)
                nc.vector.tensor_tensor(cl[:, c, :], lnsq[:, c, :], ch[:, c, :].bitcast(F32), ALU.subtract)\
                    .then_inc(c_step, 1)
            dve.wait_ge(kv_out, 16 * (4 * 2 + 1 + DB))
            with dve.Fori(0, KT // 2) as i:
                for j in range(6):
                    b = (S_MRG + j) % 2
                    dve.wait_ge(hi_done, 6 * i + (S_MRG + j + 3))
                    nc.vector.tensor_tensor(wl[:, b, :], raw[:, b, :], wh[:, b, :].bitcast(F32), ALU.subtract)\
                        .then_inc(lo_done, 1)
                    if j % 3 == 2:
                        h = j // 3
                        m = 2 * i + h
                        for q in range(2):
                            dve.wait_ge(m_sig, 4 * i + 2 * h + q + 1)
                            if q == 0:
                                dve.wait_ge(m_attn, 2 * i + h + 1)
                            else:
                                dve.wait_ge(slot_used, 6 * i + (S_MRG + 3 * h + 3))
                            nc.vector.tensor_tensor(ms[:, h, q, :], ms[:, h, q, :], pair(2 + q), ALU.mult)\
                                .then_inc(m_mul, 1)
                        dve.wait_ge(m_sum, 2 * i + h + 1)
                        nc.vector.tensor_scalar(mh[:, bass.ds(m, 1), :], msum[:, h:h + 1, :], 1.0, None, ALU.mult)\
                            .then_inc(m_hi, 1)
                        dve.wait_ge(m_hi, 2 * i + h + 1)
                        nc.vector.tensor_tensor(ml[:, bass.ds(m, 1), :], msum[:, h:h + 1, :],
                                                mh[:, bass.ds(m, 1), :].bitcast(F32), ALU.subtract).then_inc(m_ok, 1)
            for kc in range(KT // 2):
                lo(S_OUT + kc + 2)

            def gained(i, half, sq, out, gain, done):
                dve.wait_ge(sq, half * TT + i + 1)
                m = ROWS[i]
                cols = slice(half * 512, (half + 1) * 512)
                nc.vector.tensor_tensor(out[0:m, i, cols], ps[0:m, (half * TT + i) % 8, :], gain[0:m, cols],
                                        ALU.mult).then_inc(done, 1)

            def first_half(sq, pre):
                dve.wait_ge(sq, TT)
                nc.vector.tensor_scalar(ssh[:, 0, 0:4], ssh[:, 0, 0:4], 1.0 / D, EPS, ALU.mult, ALU.add)\
                    .then_inc(pre, 1)
                nc.vector.tensor_scalar(ssh[0:NS, 0, 4:5], ssh[0:NS, 0, 4:5], 1.0 / D, EPS, ALU.mult, ALU.add)\
                    .then_inc(pre, 1)

            def mean_square(i, sq, pre, step):
                m = ROWS[i]
                dve.wait_ge(sq, TT + i + 1)
                dve.wait_ge(pre, 2)
                nc.vector.scalar_tensor_tensor(ss[0:m, i:i + 1], ssh[0:m, 1, i:i + 1], 1.0 / D, ssh[0:m, 0, i:i + 1],
                                               ALU.mult, ALU.add).then_inc(step, 1)
                dve.wait_ge(step, 2 * i + 1)
                nc.vector.reciprocal(ss[0:m, i:i + 1], ss[0:m, i:i + 1]).then_inc(step, 1)

            def add_normed(i, src, rs, ev, ok):
                m = ROWS[i]
                dve.wait_ge(rs, i + 1)
                dve.wait_ge(ev, TT + i + 1)
                nc.vector.scalar_tensor_tensor(x1[0:m, i, :], src[0:m, i, :], rstd[0:m, i:i + 1], x1[0:m, i, :],
                                               ALU.mult, ALU.add).then_inc(ok, 1)

            dve.wait_ge(gp_in, 16)
            for i in range(TT):
                gained(i, 0, o_sq, hb, gpost, o_ev)
            first_half(o_sq, rs2_pre)
            dve.wait_ge(x1_in, 16 * TT)
            for kc in range(KT // 2, KT - 1):
                lo(S_OUT + kc + 2)
                if kc == KT // 2:
                    dve.wait_ge(sf_t, 1)
                    nc.vector.tensor_copy(sfT[:, :, :].rearrange("p t r -> p (t r)"), pf[:, 1024:1024 + 2 * FT * 16])\
                        .then_inc(sf_ok, 1)
            for t in range(TT + 2):
                if t < TT:
                    gained(t, 1, o_sq, hb, gpost, o_ev)
                    mean_square(t, o_sq, rs2_pre, rs2_step)
                if 1 <= t <= TT:
                    add_normed(t - 1, hb, rs2, o_ev, x1_ok)
                if t >= 2:
                    i, m = t - 2, ROWS[t - 2]
                    dve.wait_ge(sq3, i + 1)
                    nc.vector.tensor_scalar(ss[0:m, i:i + 1], ss[0:m, i:i + 1], 1.0 / D, EPS, ALU.mult, ALU.add)\
                        .then_inc(rs3_step, 1)
                    dve.wait_ge(rs3_step, 2 * i + 1)
                    nc.vector.reciprocal(ss[0:m, i:i + 1], ss[0:m, i:i + 1]).then_inc(rs3_step, 1)
                    if i % 2:
                        dve.wait_ge(rs3, i + 1)
                        nc.vector.tensor_scalar(hb[0:m, i, :], x1[0:m, i, :], rstd[0:m, i:i + 1], None, ALU.mult)\
                            .then_inc(xn2, 1)
            lo(S_UP + 1)
            for k in range(KT):
                dve.wait_ge(z2_hi, k + 1)
                nc.vector.scalar_tensor_tensor(zl[:, k, :], pf[:, 1024 * (k % 2):1024 * (k % 2) + NT],
                                               par[:, P_GFFN + k:P_GFFN + k + 1], zh[:, k, :].bitcast(F32),
                                               ALU.mult, ALU.subtract).then_inc(z2_ok, 1)
            dve.wait_ge(sf_ok, 1)
            nc.vector.memset(u[:, :, 0:2], 0.0).then_inc(u_pad, 1)
            with dve.Fori(0, FT) as i:
                for j in range(2):
                    b = (S_UP + j) % 2
                    dve.wait_ge(hi_done, 2 * i + (S_UP + j + 3))
                    nc.vector.tensor_tensor(wl[:, b, :], raw[:, b, :], wh[:, b, :].bitcast(F32), ALU.subtract)\
                        .then_inc(lo_done, 1)
                    t = i + FT * j
                    hist = u[:, j, 2 + SEQ:UEXT].rearrange("p (b t) -> p b t", t=DT + 2)
                    dve.wait_ge(cv_step, 6 * i + 3 * j)
                    nc.vector.tensor_scalar(hist[:, :, 0:2],
                                            sfT[:, bass.ds(t, 1), :].rearrange("p o (b t) -> p (o b) t", t=2),
                                            1.0, None, ALU.mult).then_inc(u_hist, 1)
                    dve.wait_ge(u_ev[j], 2 * i + 2)
                    nc.vector.tensor_scalar(ulast[:, bass.ds(t, 1), 0:2], u[:, j:j + 1, SEQ:SEQ + 2], 1.0, None,
                                            ALU.mult).then_inc(u_kept, 1)
                    nc.vector.tensor_scalar(
                        ulast[:, bass.ds(t, 1), 2:18].rearrange("p o (b t) -> p (o b) t", t=2),
                        hist[:, :, DT:DT + 2], 1.0, None, ALU.mult).then_inc(u_kept, 1)
                    if j == 0:
                        dve.wait_ge(h_mul, 2 * i)
                    dve.wait_ge(u_hist, 2 * i + j + 1)
                    nc.vector.tensor_scalar(cv[:, j, :], u[:, j, 0:CEXT], par[:, bass.ds(t + P_FW, 1)],
                                            par[:, bass.ds(t + P_FB, 1)], ALU.mult, ALU.add).then_inc(cv_step, 1)
                    for l in (1, 2):
                        dve.wait_ge(cv_step, 6 * i + 3 * j + l)
                        nc.vector.scalar_tensor_tensor(cv[:, j, :], u[:, j, l:l + CEXT],
                                                       par[:, bass.ds(t + P_FW + l * 2 * FT, 1)],
                                                       cv[:, j, :], ALU.mult, ALU.add).then_inc(cv_step, 1)
                dve.wait_ge(h_mul, 2 * i + 2)
                nc.vector.tensor_scalar(hh[:, bass.ds(i, 1), :], hs[:, :].unsqueeze(1), 1.0, None, ALU.mult)\
                    .then_inc(h_hi, 1)
                dve.wait_ge(h_hi, i + 1)
                nc.vector.tensor_tensor(hl[:, bass.ds(i, 1), :], hs[:, :].unsqueeze(1),
                                        hh[:, bass.ds(i, 1), :].bitcast(F32), ALU.subtract).then_inc(h_ok, 1)
            for kc in range(FT // 2):
                lo(S_DOWN + kc + 2)
            dve.wait_ge(gp2_in, 16)
            dve.wait_ge(ffn_out, 32)
            for i in range(TT):
                gained(i, 0, d_sq, fb, gpost2, d_ev)
            first_half(d_sq, rs4_pre)
            for kc in range(FT // 2, FT - 2):
                lo(S_DOWN + kc + 2)
            for t in range(TT + 1):
                if t < TT:
                    gained(t, 1, d_sq, fb, gpost2, d_ev)
                    mean_square(t, d_sq, rs4_pre, rs4_step)
                if t >= 1:
                    add_normed(t - 1, fb, rs4, d_ev, y_ok)

        @block.tensor
        def _(pe):
            def three(out, a, b, start, stop):
                (ah, al), (bh, bl) = a, b
                nc.tensor.matmul(out, ah, bh, start=start, stop=False)
                nc.tensor.matmul(out, ah, bl, start=False, stop=False)
                return nc.tensor.matmul(out, al, bh, start=False, stop=stop)

            def tile(q, slot, k0, kn, src, m=P, view=None):
                for h in range(2):
                    cols = slice(h * HALF, (h + 1) * HALF)
                    for k in range(kn):
                        if view is None:
                            w = (whk[:, slot, k0 + k, :], wlk[:, slot, k0 + k, :])
                        else:
                            w = (view[0][:, k, :], view[1][:, k, :])
                        last = three(pair(q, h * HALF, (h + 1) * HALF, m), w,
                                     (src[0][:, k, cols], src[1][:, k, cols]), k == 0, k == kn - 1)
                return last

            pe.wait_ge(const_ok, 1)
            pe.wait_ge(par_in, 16 * 9)
            nc.tensor.transpose(ps[:, 6, 0:P], par_raw[:, 0, :], ident[:, :])
            nc.tensor.transpose(ps[:, 6, P:2 * P], par_raw[:, 1, :], ident[:, :])
            m = P_ALL - 2 * P
            nc.tensor.transpose(ps[:, 6, 2 * P:P_ALL], par_raw[0:m, 2, :], ident[0:m, 0:m]).then_inc(par_t, 1)
            pe.wait_ge(scv_in, 32)
            for hf in range(2):
                for c in range(CT):
                    mm = nc.tensor.transpose(ps[:, 4 + hf, c * 120:(c + 1) * 120],
                                             scv[0:120, hf, c * P:(c + 1) * P], ident[0:120, 0:120])
                mm.then_inc(scv_t, 1)
            def turn_x(src, full, taken):
                for k in range(KT):
                    if k >= 2:
                        pe.wait_ge(taken, k - 1)
                    for i in range(TT):
                        c0 = 1024 * (k % 2) + i * P
                        mm = nc.tensor.transpose(pf[:, c0:c0 + ROWS[i]], src[0:ROWS[i], i, k * P:(k + 1) * P],
                                                 ident[0:ROWS[i], 0:ROWS[i]])
                    mm.then_inc(full, 1)
                pe.wait_ge(taken, KT)

            pe.wait_ge(xn_ok, TT)
            turn_x(x, z_full, z_ok)

            def past(n):
                pe.wait_ge(page_in[n % 2], 32 * (n // 2 + 1))
                if n == 0:
                    pe.wait_ge(hist_ok, 2 * CT)
                    pe.wait_ge(par_ok, 2)
                if n >= 4:
                    pe.wait_ge(past_ev, 2 * (n - 3))
                for j, c0 in enumerate((0, 128, 256, 512)):
                    mm = nc.tensor.transpose(ps[:, 4 + n % 4, j * P:(j + 1) * P], page[:, n % 2, c0:c0 + P],
                                             ident[:, :])
                mm.then_inc(past_t, 1)

            def compress(j):
                pe.wait_ge(phi_in, 32 * (j + 1))
                pe.wait_ge(cc_ok, j + 1)
                pe.wait_ge(past_ev, 2 * NPG)
                for t in range(CL):
                    mm = nc.tensor.matmul(ps[:, 4 + j, 0:NCALL], phi[:, t, :],
                                          cc[:, j, t:t + CS * (NCALL - 1) + 1:CS],
                                          start=(t == 0), stop=(t == CL - 1))
                mm.then_inc(cmp_mm, 1)

            def state_rows():
                for c in range(CT):
                    mm = nc.tensor.transpose(ps[0:HIST, 5, c * P:(c + 1) * P], ext[:, c, SEQ:SEQ + HIST], ident[:, :])
                mm.then_inc(cst_t, 1)
                for q, (b0, nb) in enumerate(SEQ_GROUPS):
                    if q == 2:
                        pe.wait_ge(cst_ok, 1)
                    for c in range(CT):
                        c0 = HIST + SEQ + b0 * SB_S
                        mm = nc.tensor.transpose(ps[0:nb * SB_S, 5 + (q + 1) % 3, c * P:(c + 1) * P],
                                                 ext[:, c, c0:c0 + nb * SB_S], ident[:, :])
                    mm.then_inc(cst_t, 1)

            def kv_rows(i):
                if i == 0:
                    pe.wait_ge(kv_ok, 6)
                    pe.wait_ge(cst_ok, 4)
                else:
                    pe.wait_ge(ktok_ok, i)
                for j in range(6):
                    c0 = 6 * 512 + j * P
                    mm = nc.tensor.transpose(pf[0:ROWS[i], c0:c0 + P], kvT[:, j, i * P:i * P + ROWS[i]], ident[:, :])
                mm.then_inc(ktok_t, 1)

            z = (zh, zl)
            for s in range(S_MRG):
                pe.wait_ge(lo_done, s + 1)
                if s >= 2:
                    t = s - 2
                    if t < S_KV and t % 2 == 0:
                        pe.wait_ge(sg_ok, t // 2 + 1)
                    elif t < S_KV:
                        pe.wait_ge(glu_p, t // 2 + 1)
                        pe.wait_ge(glu_ok, t // 2 + 1)
                    elif t < S_Q:
                        pe.wait_ge(kv_ok, t - S_KV + 1)
                    else:
                        pe.wait_ge(q_ok, t - S_Q + 1)
                if s == S_GATE:
                    vh = wh[:, s % 2, 0:KT * 24].rearrange("p (k n) -> p k n", n=24)
                    vl = wl[:, s % 2, 0:KT * 24].rearrange("p (k n) -> p k n", n=24)
                    tile(s % 2, s % 2, 0, KT, z, 24, (vh, vl)).then_inc(slot_used, 1)
                else:
                    tile(s % 2, s % 2, 0, KT, z).then_inc(slot_used, 1)
                if s < S_KV:
                    past(2 * s)
                    past(2 * s + 1)
                if s == S_CMP_K:
                    compress(0)
                if s == S_CMP_V:
                    compress(1)
                if s == S_CST:
                    state_rows()
                if s >= S_TOK and s < S_GATE:
                    kv_rows(s - S_TOK)
                if s == S_GATE - 1:
                    kv_rows(TT - 1)
                    pe.wait_ge(cmp_ok, 4)
                    nc.tensor.transpose(ps[0:NCP, 4, 0:P], vcmpT[:, 0:NCP], ident[:, :])
                    nc.tensor.transpose(ps[0:DB * NCS, 4, P:2 * P], vcmpT[:, NCP:], ident[:, :]).then_inc(vc_t, 1)
            for c in range(CT):
                mm = nc.tensor.transpose(ps[0:HIST, 5, c * P:(c + 1) * P], ext[:, c, SEQ:SEQ + HIST], ident[:, :])
            mm.then_inc(cst_t, 1)
            def cmp_scores(i):
                if i == 0:
                    pe.wait_ge(q_ok, G)
                    pe.wait_ge(ktok_ok, TT)
                else:
                    pe.wait_ge(pct_ok, 2 * i)
                for h in range(HEADS):
                    g, r = h // G, h % G
                    if h == G:
                        pe.wait_ge(cs_half, i + 1)
                    mm = nc.tensor.matmul(ps[:, 7, h * 32:h * 32 + NCP], qT[g * HD:(g + 1) * HD, r, i * P:(i + 1) * P],
                                          kcmp[g * HD:(g + 1) * HD, 0:NCP], start=True, stop=True)
                    if h == G - 1:
                        mm.then_inc(cs_half, 1)
                mm.then_inc(cs_full, 1)

            def cmp_turn(i, hf):
                if hf == 0:
                    pe.wait_ge(pc_ok, i + 1)
                else:
                    pe.wait_ge(pct_ok, 2 * i + 1)
                for h in range(4):
                    mm = nc.tensor.transpose(ps[0:NCP, 7, h * P:(h + 1) * P], sm[:, 4 * hf + h, :], ident[:, :])
                mm.then_inc(pct_full, 1)

            def scores(n):
                q, r, g, c = UNITS[n]
                if n >= 3:
                    pe.wait_ge(exp_ok, n - 2)
                rows = slice(g * HD, (g + 1) * HD)
                bk, w = n % 3, width(n)
                if q < 4:
                    if q:
                        nc.tensor.matmul(ps[:, bk, 0:w - P], qT[rows, r, q * P:(q + 1) * P], kvT[rows, 2 * c, 0:w - P],
                                         start=True, stop=True)
                    nc.tensor.matmul(ps[:, bk, w - P:w], qT[rows, r, q * P:(q + 1) * P], kvT[rows, 2 * c, w - P:w],
                                     start=True, stop=False)
                    nc.tensor.matmul(ps[:, bk, w - P:w], identb[:, :], causal[:, :], start=False, stop=True)\
                        .then_inc(s_full, 1)
                    return
                hf = q - 4
                if c == 0:
                    nc.tensor.matmul(ps[:, bk, 0:w], qs[rows, hf, :], kcmp[rows, NCP:], start=True, stop=False)
                    nc.tensor.matmul(ps[:, bk, 0:w], rowsel[rows, hf, :], cmpmask[rows, :], start=False, stop=True)\
                        .then_inc(s_full, 1)
                    return
                for b in range(4):
                    k0 = (4 * hf + b) * PAST
                    nc.tensor.matmul(ps[32 * b:32 * b + 32, bk, 0:PAST], qs[rows, hf, 32 * b:32 * b + 32],
                                     kpast[rows, c - 1, k0:k0 + PAST], start=True, stop=True)
                nc.tensor.matmul(ps[:, bk, PAST:w], qs[rows, hf, :], kvT[rows, 2 * c, SEQ:NT], start=True, stop=False)
                nc.tensor.matmul(ps[:, bk, PAST:w], rowsel[rows, hf, :], newmask[rows, :], start=False, stop=True)\
                    .then_inc(s_full, 1)

            def turn(n):
                q, _, _, c = UNITS[n]
                pe.wait_ge(scaled, n + 1)
                if n >= 2:
                    pe.wait_ge(pt_ok, n - 1)
                bk, w = 3 + n % 2, width(n)
                c0 = 0
                while c0 < w:
                    m = min(P, w - c0)
                    mm = nc.tensor.transpose(ps[0:m, bk, c0:c0 + P], probs[:, n % 3, c0:c0 + m], ident[:, :])
                    c0 += P
                mm.then_inc(pt_full, 1)

            def values(n):
                q, r, g, c = UNITS[n]
                if q >= 2 and n == FIRST[q]:
                    pe.wait_ge(ol_ok, q - 1)
                pe.wait_ge(pt_ok, n + 1)
                rows = slice(g * HD, (g + 1) * HD)
                v0 = (2 * c + 1) * P + g * HD
                pt = pT[:, n % 3, :]
                if q < 4:
                    out = ps[rows, 5 + q % 2, r * P:(r + 1) * P]
                    if c == 1:
                        pe.wait_ge(pct_ok, 2 * q + 2)
                        nc.tensor.matmul(out, vcp[:, rows], pcT[:, q % 2, g * G + r, :], start=True, stop=False)
                    for j in range(q + 1):
                        mm = nc.tensor.matmul(out, ktok[:, j, v0:v0 + HD], pt[:, j * P:(j + 1) * P],
                                              start=False, stop=(c == 2 and j == q))
                    mm.then_inc(pv_done, 1)
                    return
                out = ps[rows, 5 + q % 2, 0:P]
                if c == 0:
                    nc.tensor.matmul(out, vcs[:, rows], pt[0:DB * NCS, 0:P], start=True, stop=False)\
                        .then_inc(pv_done, 1)
                    return
                vp = vsel if c == 1 else vwin
                for b in range(4):
                    for j in range(2):
                        nc.tensor.matmul(ps[rows, 5 + q % 2, 32 * b:32 * b + 32],
                                         vp[:, 2 * (4 * (q - 4) + b) + j, rows],
                                         pt[:, j * P + 32 * b:j * P + 32 * b + 32], start=False, stop=False)
                mm = nc.tensor.matmul(out, ktok[0:NS, 4, v0:v0 + HD], pt[0:NS, PAST:PAST + P],
                                      start=False, stop=(c == 2))
                mm.then_inc(pv_done, 1)

            cmp_scores(0)
            pe.wait_ge(gt_ok, 1)
            for i in range(TT):
                mm = nc.tensor.transpose(ps[0:ROWS[i], 5, i * 24:(i + 1) * 24], gT[:, i * P:i * P + ROWS[i]],
                                         ident[0:24, 0:24])
            mm.then_inc(mid_t, 1)
            pe.wait_ge(const_ok, 2)
            pe.wait_ge(gtok_ok, 2)
            nc.tensor.transpose(ps[:, 5, 256:256 + G], rselT[:, :], ident[0:G, 0:G])
            for hf in range(2):
                mm = nc.tensor.matmul(ps[:, 5, 128 + 32 * hf:128 + 32 * hf + 24], rowsel[0:NS, hf, :],
                                      gtok[0:NS, 4, :], start=True, stop=True)
            mm.then_inc(gsel_mm, 1)
            pe.wait_ge(gsel_ok, 1)
            pe.wait_ge(vc_ok, 2)
            pe.wait_ge(qs_ok, 1)
            for n in range(NU + 3):
                if n < NU:
                    scores(n)
                if 2 <= n < NU + 2:
                    turn(n - 2)
                if n >= 3:
                    values(n - 3)
                for i in range(4):
                    if n == FIRST[i] - 8:
                        cmp_scores(i)
                    if n == (FIRST[i] - 3 if i else 1):
                        cmp_turn(i, 0)
                    if n == (FIRST[i] - 1 if i else 2):
                        cmp_turn(i, 1)
            pe.wait_ge(conv_01, 4 * CW)
            pe.wait_ge(conv_2, 2 * CW)
            pe.wait_ge(conv_3, CW - 1)
            pe.wait_ge(exp_ok, NU)
            pe.wait_ge(pt_ok, NU)
            for q, (src, done) in enumerate(((yc, ln_mean), (lnsq, ln_var))):
                if q == 1:
                    pe.wait_ge(ln_sq, CT)
                for h in range(2):
                    for c in range(CT):
                        mm = nc.tensor.matmul(pair(q, h * HALF, (h + 1) * HALF), mean_w[:, :],
                                              src[:, c, h * HALF:(h + 1) * HALF], start=(c == 0), stop=(c == CT - 1))
                mm.then_inc(done, 1)
            pe.wait_ge(ln_step, 1)
            pe.wait_ge(c_step, 2 * CT)
            pe.wait_ge(ol_ok, 6)
            with pe.Fori(0, KT // 2) as i:
                for j in range(6):
                    b = (S_MRG + j) % 2
                    h = j // 3
                    pe.wait_ge(lo_done, 6 * i + (S_MRG + j + 1))
                    if j % 3 < 2:
                        pe.wait_ge(m_sig, 4 * i + 2 * h)
                        tile(j % 3, b, 0, KT, z).then_inc(slot_used, 1)
                    else:
                        pe.wait_ge(m_mul, 4 * i + 2 * h)
                        tile(2, b, 0, CT, (oh, ol)).then_inc(m_attn, 1)
                        tile(3, b, CT, CT, (ch, cl)).then_inc(slot_used, 1)

            def token_major(s0, kn, lhs, lhs_ok, bank4, taken, tile_done, after):
                for half in range(2):
                    for kc in range(kn // 2):
                        s = s0 + half * (kn // 2) + kc
                        pe.wait_ge(lo_done, s + 1)
                        pe.wait_ge(lhs_ok, 2 * kc + 2)
                        for i in range(TT):
                            bk = half * TT + i
                            if half == 0 and kc == 0 and bk == 4:
                                pe.wait_ge(bank4[0], bank4[1])
                            if kc == 0 and bk >= 8:
                                pe.wait_ge(taken, bk - 8 + 1)
                            for kk in range(2):
                                k = 2 * kc + kk
                                mm = three(ps[0:ROWS[i], bk % 8, :],
                                           (lhs[0][:, k, i * P:i * P + ROWS[i]], lhs[1][:, k, i * P:i * P + ROWS[i]]),
                                           (whc[:, s % 2, kk, :], wlc[:, s % 2, kk, :]), k == 0, k == kn - 1)
                            if half == 1 and kc == kn // 2 - 1 and i < TT - 1:
                                mm.then_inc(tile_done, 1)
                        mm.then_inc(slot_used, 1)
                        after(half, kc)

            def ffn_history(half, kc):
                if half == 0 or kc > 0:
                    return
                pe.wait_ge(sf_in, 16)
                pe.wait_ge(o_ev, TT)
                pe.wait_ge(o_sq, TT)
                for t in range(2 * FT):
                    mm = nc.tensor.transpose(pf[:, 1024 + 16 * t:1024 + 16 * (t + 1)], sf[:, t * P:(t + 1) * P],
                                             ident[0:16, 0:16])
                mm.then_inc(sf_t, 1)

            pe.wait_ge(m_sig, 2 * KT)
            token_major(S_OUT, KT, (mh, ml), m_ok, (m_mul, 2 * KT), o_ev, o_tile, ffn_history)
            pe.wait_ge(sf_ok, 1)
            pe.wait_ge(o_ev, 2 * TT)
            pe.wait_ge(o_sq, 2 * TT)
            pe.wait_ge(xn2, TT)
            turn_x(hb, z2_full, z2_ok)
            with pe.Fori(0, FT) as i:
                for j in range(2):
                    pe.wait_ge(lo_done, 2 * i + (S_UP + j + 1))
                    pe.wait_ge(u_ev[j], 2 * i)
                    tile(j, (S_UP + j) % 2, 0, KT, z).then_inc(slot_used, 1)

            def last_rows(half, kc):
                if half or kc > 5:
                    return
                pe.wait_ge(u_kept, 4 * FT)
                for q in range(2 * kc, min(2 * kc + 2, 11)):
                    if q >= 3:
                        pe.wait_ge(ul_ev, q - 2)
                    for t in range(4):
                        mm = nc.tensor.transpose(ps[0:18, 5 + q % 3, t * P:(t + 1) * P], ulast[:, 4 * q + t, :],
                                                 ident[:, :])
                    mm.then_inc(ul_t, 1)

            pe.wait_ge(u_ev[0], 2 * FT)
            pe.wait_ge(u_ev[1], 2 * FT)
            token_major(S_DOWN, FT, (hh, hl), h_ok, (u_ev[1], 2 * FT), d_ev, d_tile, last_rows)


_INS = ["x_prompt", "x_sample", "cache_kv", "state_kv_win", "state_conv", "state_ffn", "page_table",
        "norm_mix_pre", "norm_mix_post", "norm_ffn_pre", "norm_ffn_post", "w_in", "w_phi_k", "b_phi_k",
        "w_phi_v", "b_phi_v", "w_attn_out", "conv_w", "conv_b", "conv_ln_g", "conv_ln_b", "w_conv_out",
        "w_out", "w_up", "ffn_conv_w", "ffn_conv_b", "w_down"]
_OUTS = [(1, SEQ, D), (DB, DT, D), (1, 1, SEQ, 4, KVH, HD), (1, DB, DT, 4, KVH, HD), (1, 1, SEQ, 2, KVH, HD),
         (1, DB, PAST + DT, 2, KVH, HD), (1, 1, HIST, CH), (1, DB, HIST, CH), (1, 1, FW - 1, 2 * FF),
         (1, DB, FW - 1, 2 * FF)]


def kernel(**inputs):
    import numpy as _np
    import concourse.bacc as _bacc
    from concourse import mybir as _mybir
    from concourse.bass_utils import run_bass_kernel_spmd as _run

    nc = _bacc.Bacc("TRN2", target_bir_lowering=False, num_devices=1)
    arrays, args = {}, []
    for name in _INS:
        a = _np.ascontiguousarray(inputs[name])
        arrays[f"in_{name}_dram"] = a
        args.append(nc.dram_tensor(f"in_{name}_dram", a.shape, _mybir.dt.from_np(a.dtype), kind="ExternalInput").ap())
    for i, shape in enumerate(_OUTS):
        args.append(nc.dram_tensor(f"out_{i}_dram", shape, _mybir.dt.float32, kind="ExternalOutput").ap())
    build_layer(nc, *args)
    r = _run(nc, [arrays], core_ids=[0])
    return tuple(r.results[0][f"out_{i}_dram"] for i in range(len(_OUTS)))
```

```python
from contextlib import ExitStack

import concourse.bass as bass
from concourse import mybir

F32 = mybir.dt.float32
F32R = mybir.dt.float32r
BF16 = mybir.dt.bfloat16
I32 = mybir.dt.int32
ALU = mybir.AluOpType
ACT = mybir.ActivationFunctionType
AX = mybir.AxisListType

P = 128
D = 1024
KT = D // P
SEQ = 512
DB, DT = 8, 8
NS = DB * DT
NT = SEQ + NS
TT = 5
HALF = NT // 2
PAST = 256
PAGE = 128
NPG = DB * PAST // PAGE
HEADS, KVH, G, HD = 8, 2, 4, 64
CL, CS = 32, 16
NCP = (SEQ - CL) // CS + 1
NCS = (PAST + DT - CL) // CS + 1
CC_T = SEQ + DB * PAST
NCALL = (CC_T - CL) // CS + 1
CH = 512
CT = CH // P
CW = 31
HIST = CW - 1
SB_S = HIST + DT
EXT = HIST + SEQ + DB * SB_S
FF = 2816
FT = FF // P
FW = 3
UEXT = 2 + SEQ + DB * (2 + DT)
CEXT = UEXT - 2
EPS = 1e-6
NEG = -1e30
TINY = 1e-30
OFF_KV = 512
OFF_GATE = OFF_KV + 6 * 128
OFF_GLU = OFF_GATE + 24
OFF_MRG = OFF_GLU + 2 * CH
IN_W = OFF_MRG + 2 * D
ROWS = [P] * 4 + [NS]

P_FW = 0
P_CW = P_FW + FW * 2 * FT
P_FB = P_CW + CW * CT
P_CB = P_FB + 2 * FT
P_GPRE = P_CB + CT
P_GFFN = P_GPRE + KT
P_LNG = P_GFFN + KT
P_LNB = P_LNG + CT
P_ALL = P_LNB + CT

S_GLU = 0
S_KV = S_GLU + 2 * CT
S_Q = S_KV + 6
S_GATE = S_Q + 4
S_MRG = S_GATE + 1
S_OUT = S_MRG + 3 * KT
S_UP = S_OUT + KT
S_DOWN = S_UP + 2 * FT
S_END = S_DOWN + FT
MRG_DMAS = [1, 1, 3]
S_CMP_K = S_KV + 1
S_CST = S_KV + 4
S_TOK = S_Q
LN_MEAN, LN_XC, LN_SQ, LN_VAR, LN_TAKE = (49, 55), (50, 56), (51, 57), (61, 63), (62, 64)
SEQ_GROUPS = [(0, 3), (3, 3), (6, 2)]


AHEAD = 1


def slot_dmas(s):
    if S_Q <= s < S_GATE:
        return 2
    if S_MRG <= s < S_OUT:
        return MRG_DMAS[(s - S_MRG) % 3]
    return 1


def raw_value(s):
    return 16 * sum(slot_dmas(x) for x in range(s % 2, s + 1, 2))


UNITS = [(i, r, g, c) for i in (3, 2, 1, 0) for r in range(G) for g in range(KVH) for c in (1, 2)]
UNITS += [(4 + hf, 0, g, c) for hf in range(2) for g in range(KVH) for c in (0, 1, 2)]
NU = len(UNITS)
LAST = [max(n for n, u in enumerate(UNITS) if u[0] == q) for q in range(6)]
LN_ROOT, LN_NORM, LN_SWISH = NU, NU, NU + 4
FIRST = [min(n for n, u in enumerate(UNITS) if u[0] == q) for q in range(6)]


def place(q):
    return 3 - q if q < 4 else q


def width(n):
    q, _, _, c = UNITS[n]
    return (q + 1) * P if q < 4 else (DB * NCS if c == 0 else PAST + NS)


def build_layer(nc, x_prompt, x_sample, cache_kv, state_kv_win, state_conv, state_ffn, page_table,
                g_mix_pre, g_mix_post, g_ffn_pre, g_ffn_post, w_in, w_phi_k, b_phi_k, w_phi_v, b_phi_v,
                w_attn_out, conv_w, conv_b, conv_ln_g, conv_ln_b, w_conv_out, w_out, w_up,
                ffn_conv_w, ffn_conv_b, w_down,
                y_prompt, y_sample, kv_prompt, kv_sample, win_prompt, win_sample,
                conv_prompt, conv_sample, ffn_prompt, ffn_sample):
    ctx = ExitStack()
    with ctx:
        base = (nc.sbuf_base + 63) // 32 * 32

        def at(name, shape, dt, col):
            return nc.alloc_sbuf_tensor_at(name, shape, dt, offset=base + 4 * col)

        A = 0
        B = A + 2 * KT * NT
        C = B + 6 * 1024
        DD = C + 4 * NT
        E = DD + 6 * NT
        FV = E + TT * 768
        GK = FV + NPG * P
        H = GK + 2 * DB * PAST
        I = H + NPG * P
        J = I + 4096 + 2 * CC_T + 2 * 768
        K = J + CT * EXT + CT * NT

        zh = at("zh", [P, KT, NT], F32R, A)
        zl = at("zl", [P, KT, NT], F32R, A + KT * NT)
        sq_x = at("sq_x", [P, TT, D], F32, A)
        raw = at("raw", [P, 2, 1024], F32, B)
        wh = at("wh", [P, 2, 1024], F32R, B + 2048)
        wl = at("wl", [P, 2, 1024], F32R, B + 4096)
        x = at("x", [P, TT, D], F32, C)
        qT = at("qT", [P, G, NT], F32, C)
        kvT = at("kvT", [P, 6, NT], F32, DD)
        ktok = at("ktok", [P, TT, 768], F32, E)
        par_raw = at("par_raw", [P, 3, P], F32, E)
        scv = at("scv", [P, 2, CH], F32, E + 384)
        sg = at("sg", [P, NT], F32, E + 384 + 1024)
        gT = at("gT", [24, NT], F32, DD)
        vwin = at("vwin", [P, NPG, P], F32, FV)
        kpast = at("kpast", [P, 2, DB * PAST], F32, GK)
        vsel = at("vsel", [P, NPG, P], F32, H)
        phi = at("phi", [P, CL, P], F32, I)
        cc = at("cc", [P, 2, CC_T], F32, I + 4096)
        page = at("page", [P, 2, 768], F32, I + 4096 + 2 * CC_T)
        cst = at("cst", [P, 3, CH], F32, I + 4096 + 2 * CC_T)
        oh = at("oh", [P, G, NT], F32R, I)
        ol = at("ol", [P, G, NT], F32R, I + G * NT)
        probs = at("probs", [P, 3, 512], F32, I + 4608)
        cprod = at("cprod", [P, 4, NT], F32, I + 4096)
        probs3 = at("probs3", [P, 512], F32, DD)
        probs_at = [probs[:, 0, :], probs[:, 1, :], probs[:, 2, :], probs3[:, :]]
        pT = at("pT", [P, 3, 512], F32, I + 6144)
        pcT = at("pcT", [NCP, 2, HEADS, P], F32, I + 7680)
        sc = at("sc", [P, HEADS, NCP], F32, I + 9728)
        se = at("se", [P, HEADS, NCP], F32, I + 9728 + 256)
        sm = at("sm", [P, HEADS, NCP], F32, I + 9728 + 512)
        ext = at("ext", [P, CT, EXT], F32, J)
        yc = at("yc", [P, CT, NT], F32, J + CT * EXT)
        lnsq = at("lnsq", [P, CT, NT], F32, J)
        lnv = at("lnv", [P, NT], F32, J + CT * NT)
        ch = at("ch", [P, CT, NT], F32R, FV)
        cl = at("cl", [P, CT, NT], F32R, FV + CT * NT)
        mh = at("mh", [P, KT, NT], F32R, C)
        ml = at("ml", [P, KT, NT], F32R, C + KT * NT)
        ms = at("ms", [P, 2, 2, NT], F32, J)
        msum = at("msum", [P, 2, NT], F32, J + 4 * NT)
        hb = at("hb", [P, TT, D], F32, FV)
        sf = at("sf", [2 * DB, 2 * FF], F32, H)
        gpost = at("gpost", [P, D], F32, H + 2 * FF)
        junk = at("junk", [P, TT, D], F32, H + 2 * FF + D)
        x1 = at("x1", [P, TT, D], F32, K - TT * D)
        hh = at("hh", [P, FT, NT], F32R, C)
        hl = at("hl", [P, FT, NT], F32R, C + FT * NT)
        u = at("u", [P, 2, UEXT], F32, C + 2 * FT * NT)
        U2 = C + 2 * FT * NT + (2 * UEXT + 7) // 8 * 8
        cv = at("cv", [P, 2, CEXT], F32, U2)
        hs = at("hs", [P, NT], F32, U2 + 2 * CEXT)
        ulast = at("ulast", [P, 2 * FT, 18], F32, U2 + 2 * CEXT + NT)
        assert U2 + 2 * CEXT + NT + 2 * FT * 18 <= K - TT * D
        fb = at("fb", [P, TT, D], F32, A)
        ustage = at("ustage", [18, 2 * FF], F32, A + 2 * KT * NT - 2 * FF)
        junk2 = at("junk2", [P, 4, D], F32, A + TT * D)
        gpost2 = at("gpost2", [P, D], F32, C + 2 * FT * NT)
        junk3 = at("junk3", [P, D], F32, C + 2 * FT * NT + D)

        used = [K]

        def small(name, shape, dt=F32):
            cols = 1
            for d in shape[1:]:
                cols *= d
            if dt == BF16:
                cols = (cols + 1) // 2
            t = at(name, shape, dt, used[0])
            used[0] += (cols + 7) // 8 * 8
            return t

        ident = small("ident", [P, P])
        identb = small("identb", [P, P], BF16)
        causal = small("causal", [P, P], BF16)
        rowsel = small("rowsel", [P, 2, P])
        newmask = small("newmask", [P, NS])
        cmpmask = small("cmpmask", [P, DB * NCS])
        rselT = small("rselT", [G, P])
        rsel = small("rsel", [P, G])
        cneg = small("cneg", [P, 4, NCP])
        c01 = small("c01", [P, 4, NCP])
        mean_w = small("mean_w", [P, P])
        par = small("par", [P, P_ALL])
        bphi = small("bphi", [P, 2])
        ss = small("ss", [P, TT])
        ssh = small("ssh", [P, 2, TT])
        rstd = small("rstd", [P, TT])
        nmax = small("nmax", [P, NU])
        esum = small("esum", [P, NU])
        rinv = small("rinv", [P, NU])
        gtok = small("gtok", [P, TT, 24])
        gsel4 = small("gsel4", [P, 2, 6, G])
        gsel = small("gsel", [P, 2, 6])
        kcmp = small("kcmp", [P, NCP + DB * NCS])
        vcmpT = small("vcmpT", [P, NCP + DB * NCS])
        vcp = small("vcp", [NCP, P])
        vcs = small("vcs", [DB * NCS, P])
        qs = small("qs", [P, 2, P])
        cmax = small("cmax", [P, HEADS])
        csum = small("csum", [P, HEADS])
        cgate = small("cgate", [P, HEADS])
        ptab = small("ptab", [1, NPG], I32)
        sfT = small("sfT", [P, 2 * FT, 2 * DB])
        assert base + 4 * used[0] <= nc.sbuf_usable_end, (base + 4 * used[0], nc.sbuf_usable_end)

        ps = ctx.enter_context(nc.psum_tensor("ps", [P, 8, 512], F32))
        pf = ps[:, :, :].rearrange("p b n -> p (b n)")
        LO = 512 - HALF

        def pair(q, a=0, b=NT, m=P):
            return pf[0:m, 1024 * q + LO + a:1024 * q + LO + b]

        def sem(name):
            return ctx.enter_context(nc.semaphore(name))

        raw_in = [sem("raw_in0"), sem("raw_in1")]
        hi_done = sem("hi_done")
        lo_done = sem("lo_done")
        slot_used = sem("slot_used")
        par_in = sem("par_in")
        scv_in = sem("scv_in")
        x_in = [sem(f"x_in{i}") for i in range(TT)]
        ptab_in = sem("ptab_in")
        bphi_in = sem("bphi_in")
        page_in = [sem("page_in0"), sem("page_in1")]
        phi_in = sem("phi_in")
        pool_init = sem("pool_init")
        const_ok = sem("const_ok")
        par_t = sem("par_t")
        par_ok = sem("par_ok")
        scv_t = sem("scv_t")
        hist_ok = sem("hist_ok")
        sq_done = sem("sq_done")
        rs_step = sem("rs_step")
        rs_ok = sem("rs_ok")
        xn_ok = sem("xn_ok")
        z_full = sem("z_full")
        zhi_ok = sem("zhi_ok")
        z_ok = sem("z_ok")
        past_t = sem("past_t")
        past_ev = sem("past_ev")
        vcopy = sem("vcopy")
        sg_ok = sem("sg_ok")
        glu_ok = sem("glu_ok")
        ext0 = sem("ext0")
        glu_p = sem("glu_p")
        conv_01 = sem("conv_01")
        conv_2 = sem("conv_2")
        conv_3 = sem("conv_3")
        conv_prod = sem("conv_prod")
        kv_ok = sem("kv_ok")
        cc_ok = sem("cc_ok")
        q_ok = sem("q_ok")
        gt_ok = sem("gt_ok")
        mid_t = sem("mid_t")
        gtok_ok = sem("gtok_ok")
        ktok_t = sem("ktok_t")
        ktok_ok = sem("ktok_ok")
        cst_t = sem("cst_t")
        cst_ok = sem("cst_ok")
        cst_out = sem("cst_out")
        kv_out = sem("kv_out")
        win_out = sem("win_out")
        cmp_mm = sem("cmp_mm")
        cmp_ok = sem("cmp_ok")
        vc_t = sem("vc_t")
        vc_ok = sem("vc_ok")
        rsel_ok = sem("rsel_ok")
        gsel_mm = sem("gsel_mm")
        gsel_ok = sem("gsel_ok")
        qs_ok = sem("qs_ok")
        s_full = sem("s_full")
        nmax_ok = sem("nmax_ok")
        exp_ok = sem("exp_ok")
        rinv_ok = sem("rinv_ok")
        scaled = sem("scaled")
        pt_full = sem("pt_full")
        pt_part = sem("pt_part")
        pt_ok = sem("pt_ok")
        pv_done = sem("pv_done")
        cs_half = sem("cs_half")
        cs_full = sem("cs_full")
        cs_step = sem("cs_step")
        ce_in = sem("ce_in")
        ce_ok = sem("ce_ok")
        pc_ok = sem("pc_ok")
        pct_full = sem("pct_full")
        pct_ok = sem("pct_ok")
        oh_ok = sem("oh_ok")
        ol_ok = sem("ol_ok")
        ln_mean = sem("ln_mean")
        ln_xc = sem("ln_xc")
        ln_sq = sem("ln_sq")
        ln_var = sem("ln_var")
        ln_step = sem("ln_step")
        ln_rs = sem("ln_rs")
        ln_xn = sem("ln_xn")
        silu_ok = sem("silu_ok")
        c_step = sem("c_step")
        m_attn = sem("m_attn")
        m_sig = sem("m_sig")
        m_mul = sem("m_mul")
        m_sum = sem("m_sum")
        m_hi = sem("m_hi")
        m_ok = sem("m_ok")
        x1_in = sem("x1_in")
        sf_in = sem("sf_in")
        gp_in = sem("gp_in")
        o_ev = sem("o_ev")
        sf_t = sem("sf_t")
        sf_ok = sem("sf_ok")
        o_tile = sem("o_tile")
        o_sq = sem("o_sq")
        rs2_pre = sem("rs2_pre")
        rs2_step = sem("rs2_step")
        rs2 = sem("rs2")
        x1_ok = sem("x1_ok")
        sq3 = sem("sq3")
        rs3_step = sem("rs3_step")
        rs3 = sem("rs3")
        xn2 = sem("xn2")
        z2_full = sem("z2_full")
        z2_hi = sem("z2_hi")
        z2_ok = sem("z2_ok")
        u_ev = [sem("u_ev0"), sem("u_ev1")]
        u_hist = sem("u_hist")
        u_kept = sem("u_kept")
        u_pad = sem("u_pad")
        cv_step = sem("cv_step")
        act_ok = sem("act_ok")
        h_mul = sem("h_mul")
        h_hi = sem("h_hi")
        h_ok = sem("h_ok")
        ul_t = sem("ul_t")
        ul_ev = sem("ul_ev")
        ffn_out = sem("ffn_out")
        d_ev = sem("d_ev")
        gp2_in = sem("gp2_in")
        d_tile = sem("d_tile")
        d_sq = sem("d_sq")
        rs4_pre = sem("rs4_pre")
        rs4_step = sem("rs4_step")
        rs4 = sem("rs4")
        y_ok = sem("y_ok")
        y_out = sem("y_out")

        w_in_v = w_in[0].rearrange("(k p) n -> p k n", p=P)
        w_up_v = w_up[0].rearrange("(k p) n -> p k n", p=P)
        w_ao_v = w_attn_out[0].rearrange("(g r h) n -> g h r n", g=KVH, r=G)
        w_co_v = w_conv_out[0].rearrange("(k p) n -> p k n", p=P)
        w_out_v = w_out[0].rearrange("(k p) n -> p k n", p=P)
        w_down_v = w_down[0].rearrange("(k p) n -> p k n", p=P)
        xs_v = x_sample.rearrange("b t d -> (b t) d")
        ys_v = y_sample.rearrange("b t d -> (b t) d")
        cache_v = cache_kv[0].rearrange("n t a g h -> n t (a g h)")
        swin_v = state_kv_win[0].rearrange("b (j t) a g h -> (b j) t (a g h)", t=PAGE)
        kvp_v = kv_prompt[0, 0].rearrange("t a g h -> t (a g h)")
        kvs_v = kv_sample[0].rearrange("b t a g h -> (b t) (a g h)")
        winp_v = win_prompt[0, 0].rearrange("t a g h -> t (a g h)")
        wins_v = win_sample[0].rearrange("b t a g h -> b t (a g h)")
        rawk = raw[:, :, :].rearrange("p s (k n) -> p s k n", n=P)
        whk = wh[:, :, :].rearrange("p s (k n) -> p s k n", n=P)
        wlk = wl[:, :, :].rearrange("p s (k n) -> p s k n", n=P)
        rawc = raw[:, :, :].rearrange("p s (k n) -> p s k n", n=512)
        whc = wh[:, :, :].rearrange("p s (k n) -> p s k n", n=512)
        wlc = wl[:, :, :].rearrange("p s (k n) -> p s k n", n=512)

        def mrg_step(b):
            return sum(MRG_DMAS[j % 3] for j in range(6) if (S_MRG + j) % 2 == b)

        def mrg_raw(j):
            return raw_value(S_MRG + j)

        def tap(c, l, part):
            w = par[:, P_CW + l * CT + c:P_CW + l * CT + c + 1]
            if part == 0:
                return w, ext[:, c, l:l + SEQ], yc[:, c, 0:SEQ]
            return (w, ext[:, c, HIST + SEQ:EXT].rearrange("p (b t) -> p b t", t=SB_S)[:, :, l:l + DT],
                    yc[:, c, SEQ:NT].rearrange("p (b t) -> p b t", t=DT))

        block = ctx.enter_context(nc.Block())

        @block.sync
        def _(sp):
            for i in range(4):
                sp.dma_start(x[:, i, :], x_prompt[0, i * P:(i + 1) * P, :]).then_inc(x_in[i], 16)
            sp.dma_start(x[0:NS, 4, :], xs_v).then_inc(x_in[4], 16)

            def ring_free(s):
                sp.wait_ge(hi_done, s - 1)
                sp.wait_ge(lo_done, s - 1)

            def col_tile(s, v, c0, n=P):
                if s >= 2:
                    ring_free(s)
                dst = rawk[:, s % 2] if n == P else raw[:, s % 2, 0:KT * n].rearrange("p (k n) -> p k n", n=n)
                sp.dma_start(dst, v[:, :, c0:c0 + n]).then_inc(raw_in[s % 2], 16)

            for c in range(CT):
                col_tile(S_GLU + 2 * c, w_in_v, OFF_GLU + CH + c * P)
                col_tile(S_GLU + 2 * c + 1, w_in_v, OFF_GLU + c * P)
            for j in range(6):
                col_tile(S_KV + j, w_in_v, OFF_KV + j * P)
            for r in range(G):
                s = S_Q + r
                ring_free(s)
                for g in range(KVH):
                    c0 = (g * G + r) * HD
                    sp.dma_start(rawk[:, s % 2, :, g * HD:(g + 1) * HD], w_in_v[:, :, c0:c0 + HD])\
                      .then_inc(raw_in[s % 2], 16)
            col_tile(S_GATE, w_in_v, OFF_GATE, 24)
            with sp.Fori(0, KT // 2) as i:
                for j in range(6):
                    b = (S_MRG + j) % 2
                    c1 = sp.snap((2 * i + j // 3 + 1) * P + (OFF_MRG + (j % 3) * D if j % 3 < 2 else 0))
                    split = sp.snap(6 * i + (S_MRG + j - 1))
                    sp.wait_ge(lo_done, split)
                    if j % 3 < 2:
                        sp.dma_start(rawk[:, b], w_in_v[:, :, bass.ds(c1 - P, P)]).then_inc(raw_in[b], 16)
                    else:
                        for g in range(KVH):
                            sp.dma_start(rawk[g * HD:(g + 1) * HD, b, 0:G], w_ao_v[g, :, :, bass.ds(c1 - P, P)])\
                              .then_inc(raw_in[b], 16)
                        sp.dma_start(rawk[:, b, G:KT], w_co_v[:, :, bass.ds(c1 - P, P)]).then_inc(raw_in[b], 16)
            for half in range(2):
                for kc in range(KT // 2):
                    s = S_OUT + half * (KT // 2) + kc
                    ring_free(s)
                    sp.dma_start(rawc[:, s % 2], w_out_v[:, 2 * kc:2 * kc + 2, half * 512:(half + 1) * 512])\
                      .then_inc(raw_in[s % 2], 16)
            with sp.Fori(0, FT) as i:
                for j in range(2):
                    b = (S_UP + j) % 2
                    c1 = sp.snap((i + 1) * P + j * FF)
                    split = sp.snap(2 * i + (S_UP + j - 1))
                    sp.wait_ge(lo_done, split)
                    sp.dma_start(rawk[:, b], w_up_v[:, :, bass.ds(c1 - P, P)]).then_inc(raw_in[b], 16)
            for half in range(2):
                for kc in range(FT // 2):
                    s = S_DOWN + half * (FT // 2) + kc
                    ring_free(s)
                    sp.dma_start(rawc[:, s % 2], w_down_v[:, 2 * kc:2 * kc + 2, half * 512:(half + 1) * 512])\
                      .then_inc(raw_in[s % 2], 16)
            for i in range(TT):
                sp.wait_ge(y_ok, i + 1)
                dst = y_prompt[0, i * P:(i + 1) * P, :] if i < 4 else ys_v
                sp.dma_start(dst, x1[0:ROWS[i], i, :]).then_inc(y_out, 16)
            sp.wait_ge(y_out, 16 * TT)

        @block.gpsimd
        def _(pool):
            for counted in (m_sum, h_mul):
                pool.sem_inc(counted, AHEAD)
            pool.dma_start(ptab[:, :], page_table.rearrange("b j -> (b j)").unsqueeze(0)).then_inc(ptab_in, 16)
            init = [0]

            def fill(t, v):
                pool.wait_ge(pool_init, init[0])
                nc.gpsimd.memset(t, v).then_inc(pool_init, 1)
                init[0] += 1

            def select(t, op, fillv, b0, pattern, cm):
                pool.wait_ge(pool_init, init[0])
                nc.gpsimd.affine_select(out=t, in_=t, compare_op=op, fill=fillv, base=b0, pattern=pattern,
                                        channel_multiplier=cm).then_inc(pool_init, 1)
                init[0] += 1

            fill(ident[:, :], 0.0)
            select(ident[:, :], ALU.not_equal, 1.0, 0, [[-1, P]], 1)
            pool.wait_ge(pool_init, init[0])
            nc.gpsimd.tensor_copy(identb[:, :], ident[:, :]).then_inc(const_ok, 1)
            pool.wait_ge(ptab_in, 16)

            def load_page(n):
                if n >= 2:
                    pool.wait_ge(past_t, n - 1)
                    pool.wait_ge(vcopy, 2 * (n - 1))
                pg = pool.value_load(ptab[0:1, n:n + 1], min_val=0, max_val=cache_kv.shape[1] - 1)
                pool.dma_start(page[:, n % 2, 0:512], cache_v[bass.ds(pg, 1)].rearrange("a t n -> (a t) n"))\
                    .then_inc(page_in[n % 2], 16)
                pool.dma_start(page[:, n % 2, 512:768], swin_v[n]).then_inc(page_in[n % 2], 16)

            load_page(0)
            load_page(1)
            fill(causal[:, :], 0.0)
            select(causal[:, :], ALU.is_ge, NEG, 0, [[-1, P]], 1)
            fill(rowsel[:, :, :], 1.0)
            for g in range(KVH):
                select(rowsel[g * HD:(g + 1) * HD, :, :].rearrange("k h p -> k (h p)"), ALU.is_equal, 0.0, 0,
                       [[-DT, DB], [0, G], [-1, DT]], 1)
            fill(newmask[:, :], 0.0)
            for g in range(KVH):
                rows = slice(g * HD, (g + 1) * HD)
                select(newmask[rows, :], ALU.is_ge, NEG, 0, [[-1, NS]], 1)
                select(newmask[rows, :], ALU.is_ge, NEG, DT - 1, [[DT, DB], [0, DT]], -1)
            fill(cmpmask[:, :], 0.0)
            for g in range(KVH):
                rows = slice(g * HD, (g + 1) * HD)
                select(cmpmask[rows, :], ALU.is_ge, NEG, 0, [[-DT, DB], [0, NCS]], 1)
                select(cmpmask[rows, :], ALU.is_ge, NEG, DT - 1, [[DT, DB], [0, NCS]], -1)
            fill(rselT[:, :], 1.0)
            select(rselT[:, :], ALU.is_equal, 0.0, 0, [[0, 4], [-1, G], [0, DT]], 1)
            fill(cneg[:, :, :], 0.0)
            select(cneg[:, :, :], ALU.is_ge, NEG, 1 - CL, [[P, 4], [-CS, NCP]], 1)
            fill(c01[:, :, :], 1.0)
            select(c01[:, :, :], ALU.is_ge, 0.0, 1 - CL, [[P, 4], [-CS, NCP]], 1)
            fill(phi[:, :, :], 0.0)
            pool.wait_ge(pool_init, init[0])
            nc.gpsimd.memset(mean_w[:, :], 1.0 / CH).then_inc(const_ok, 1)

            def load_phi(w):
                for g in range(KVH):
                    pool.dma_start(phi[g * HD:(g + 1) * HD, :, g * HD:(g + 1) * HD],
                                   w[0].rearrange("(l h) e -> h l e", h=HD)).then_inc(phi_in, 16)

            load_phi(w_phi_k)
            for g in range(KVH):
                for q, b in enumerate((b_phi_k, b_phi_v)):
                    pool.dma_start(bphi[g * HD:(g + 1) * HD, q:q + 1], b[0].unsqueeze(1)).then_inc(bphi_in, 16)
            for n in range(NPG):
                pool.wait_ge(page_in[n % 2], 32 * (n // 2 + 1))
                nc.gpsimd.tensor_copy(vsel[:, n, :], page[:, n % 2, 384:512]).then_inc(vcopy, 1)
                nc.gpsimd.tensor_copy(vwin[:, n, :], page[:, n % 2, 640:768]).then_inc(vcopy, 1)
                if n + 2 < NPG:
                    load_page(n + 2)
            pool.dma_start(wins_v[:, 0:PAST, :], state_kv_win[0].rearrange("b t a g h -> b t (a g h)"))\
                .then_inc(win_out, 16)
            for j in range(2):
                pool.wait_ge(kv_ok, j + 1)
                nc.gpsimd.tensor_copy(cc[:, j, 0:SEQ], kvT[:, j, 0:SEQ]).then_inc(cc_ok, 1)
            pool.wait_ge(cmp_mm, 1)
            load_phi(w_phi_v)
            for l in range(1, CW):
                pool.wait_ge(conv_prod, 2 * (l + 1))
                if l > 1:
                    pool.wait_ge(conv_3, l - 1)
                nc.gpsimd.tensor_tensor(yc[:, CT - 1, :], yc[:, CT - 1, :], cprod[:, l % 4, :], ALU.add)\
                    .then_inc(conv_3, 1)
            for n, (q, r, g, c) in enumerate(UNITS):
                pool.wait_ge(rinv_ok, n + 1)
                gate = gtok[:, q, c * HEADS + g * G + r:c * HEADS + g * G + r + 1] if q < 4 \
                    else gsel[:, q - 4, c * KVH + g:c * KVH + g + 1]
                w = probs_at[n % 4][:, 0:width(n)]
                nc.gpsimd.tensor_scalar(w, w, rinv[:, n:n + 1], gate, ALU.mult, ALU.mult).then_inc(scaled, 1)
            with pool.Fori(0, KT // 2) as i:
                for j in range(2):
                    pool.wait_ge(m_ok, 2 * i + j + AHEAD)
                    pool.wait_ge(m_mul, 4 * i + 2 * j + 2 + AHEAD)
                    nc.gpsimd.tensor_tensor(msum[:, j, :], ms[:, j, 0, :], ms[:, j, 1, :], ALU.add)\
                        .then_inc(m_sum, 1)
            pool.wait_ge(m_ok, KT + AHEAD)
            for i in range(TT):
                src = x_prompt[0, i * P:(i + 1) * P, :] if i < 4 else xs_v
                pool.dma_start(x1[0:ROWS[i], i, :], src).then_inc(x1_in, 16)
            pool.wait_ge(slot_used, S_OUT)
            pool.dma_start(sf[:, :], state_ffn[0].rearrange("b t f -> (b t) f")).then_inc(sf_in, 16)
            pool.dma_start(gpost[:, :], g_mix_post[0].partition_broadcast(P)).then_inc(gp_in, 16)
            with pool.Fori(0, FT) as i:
                pool.wait_ge(h_ok, i + AHEAD)
                pool.wait_ge(cv_step, 6 * i + 6 + AHEAD)
                pool.wait_ge(act_ok, i + 1)
                nc.gpsimd.tensor_tensor(hs[:, 0:SEQ], cv[:, 0, 0:SEQ], cv[:, 1, 0:SEQ], ALU.mult)\
                    .then_inc(h_mul, 1)
                nc.gpsimd.tensor_tensor(
                    hs[:, SEQ:NT].rearrange("p (b t) -> p b t", t=DT),
                    cv[:, 0, SEQ:CEXT].rearrange("p (b t) -> p b t", t=DT + 2)[:, :, 2:DT + 2],
                    cv[:, 1, SEQ:CEXT].rearrange("p (b t) -> p b t", t=DT + 2)[:, :, 2:DT + 2],
                    ALU.mult).then_inc(h_mul, 1)
            pool.wait_ge(h_ok, FT + AHEAD)
            pool.dma_start(gpost2[:, :], g_ffn_post[0].partition_broadcast(P)).then_inc(gp2_in, 16)
            pool.wait_ge(ul_ev, 11)
            pool.dma_start(ffn_prompt[0, 0], ustage[0:2, :]).then_inc(ffn_out, 16)
            pool.dma_start(ffn_sample[0].rearrange("b t f -> (b t) f"), ustage[2:18, :]).then_inc(ffn_out, 16)
            pool.wait_ge(win_out, 16)
            pool.wait_ge(kv_out, 16 * (4 * 2 + 1 + DB))
            pool.wait_ge(cst_out, 16 * (1 + DB))
            pool.wait_ge(ffn_out, 32)

        @block.scalar
        def _(act):
            for counted in (m_sig, u_ev[0], u_ev[1]):
                act.sem_inc(counted, AHEAD)
            v = ffn_conv_w[0].rearrange("w (t p) -> (w t) p", p=P)
            act.dma_start(par_raw[:, 0, :], v[0:P, :]).then_inc(par_in, 16)
            act.dma_start(par_raw[0:P_CW - P, 1, :], v[P:P_CW, :]).then_inc(par_in, 16)
            act.dma_start(par_raw[P_CW - P:P_FB - P, 1, :], conv_w[0].rearrange("w (t p) -> (w t) p", p=P))\
                .then_inc(par_in, 16)
            for vec, col in ((ffn_conv_b, P_FB), (conv_b, P_CB), (g_mix_pre, P_GPRE), (g_ffn_pre, P_GFFN),
                             (conv_ln_g, P_LNG), (conv_ln_b, P_LNB)):
                rows = vec[0].rearrange("(t p) -> t p", p=P)
                act.dma_start(par_raw[col - 2 * P:col - 2 * P + rows.shape[0], 2, :], rows).then_inc(par_in, 16)
            def hi(s):
                act.wait_ge(raw_in[s % 2], raw_value(s))
                if s >= 2:
                    act.wait_ge(slot_used, s - 1)
                n = KT * 24 if s == S_GATE else 1024
                nc.scalar.copy(wh[:, s % 2, 0:n], raw[:, s % 2, 0:n]).then_inc(hi_done, 1)

            for t in range(TT + 1):
                if t < TT:
                    m = ROWS[t]
                    act.wait_ge(x_in[t], 16)
                    nc.scalar.activation(sq_x[0:m, t, :], x[0:m, t, :], ACT.Square,
                                         accum_out=ss[0:m, t:t + 1]).then_inc(sq_done, 1)
                if t >= 1:
                    m = ROWS[t - 1]
                    act.wait_ge(rs_step, 2 * t)
                    nc.scalar.activation(rstd[0:m, t - 1:t], ss[0:m, t - 1:t], ACT.Sqrt).then_inc(rs_ok, 1)
            for hf in range(2):
                act.dma_start(scv[0:4 * HIST, hf, :], state_conv[0, 4 * hf:4 * hf + 4].rearrange("b t c -> (b t) c"))\
                    .then_inc(scv_in, 16)
            hi(0)
            hi(1)
            act.wait_ge(par_ok, 2)
            act.wait_ge(sq_done, TT)
            for k in range(KT):
                act.wait_ge(z_full, k + 1)
                nc.scalar.activation(zh[:, k, :], pf[:, 1024 * (k % 4):1024 * (k % 4) + NT], ACT.Copy,
                                     scale=par[:, P_GPRE + k:P_GPRE + k + 1]).then_inc(zhi_ok, 1)
            def cmp_bias(j):
                dst = (kcmp, vcmpT)[j]
                act.wait_ge(cmp_mm, j + 1)
                bk = (4, 6)[j]
                nc.scalar.activation(dst[:, 0:NCP], ps[:, bk, 0:NCP], ACT.Identity, bias=bphi[:, j:j + 1])\
                    .then_inc(cmp_ok, 1)
                nc.scalar.activation(
                    dst[:, NCP:].rearrange("p (b n) -> p b n", n=NCS),
                    ps[:, bk, SEQ // CS:SEQ // CS + DB * PAST // CS].rearrange("p (b n) -> p b n", b=DB)[:, :, 0:NCS],
                    ACT.Identity, bias=bphi[:, j:j + 1]).then_inc(cmp_ok, 1)

            def state_rows_out():
                act.wait_ge(vcopy, 2 * NPG)
                act.wait_ge(cst_t, 1)
                nc.scalar.copy(cst[96:96 + HIST, 2, :], ps[0:HIST, 5, :]).then_inc(cst_ok, 1)
                for q, (_, nb) in enumerate(SEQ_GROUPS):
                    act.wait_ge(cst_t, q + 2)
                    nc.scalar.copy(cst[0:nb * SB_S, q, :], ps[0:nb * SB_S, (6, 7, 4)[q], :]).then_inc(cst_ok, 1)
                act.wait_ge(cst_ok, 4)
                act.dma_start(conv_prompt[0, 0], cst[96:96 + HIST, 2, :]).then_inc(cst_out, 16)
                for b in range(DB):
                    r0 = (b % 3) * SB_S + DT
                    act.dma_start(conv_sample[0, b], cst[r0:r0 + HIST, b // 3, :]).then_inc(cst_out, 16)

            def kv_rows(i):
                act.wait_ge(ktok_t, i + 1)
                b0 = (6 if i < 4 else 4) * 512
                nc.scalar.copy(ktok[0:ROWS[i], i, :], pf[0:ROWS[i], b0:b0 + 768]).then_inc(ktok_ok, 1)

            def kv_rows_out(i):
                act.wait_ge(ktok_ok, i + 1)
                act.dma_start(kvp_v[i * P:(i + 1) * P, :], ktok[:, i, 0:512]).then_inc(kv_out, 16)
                act.dma_start(winp_v[i * P:(i + 1) * P, :], ktok[:, i, 512:768]).then_inc(kv_out, 16)

            def conv_products(l0, l1):
                for l in range(l0, l1):
                    if l == 0:
                        act.wait_ge(hist_ok, 2 * CT)
                        act.wait_ge(glu_p, CT)
                        act.wait_ge(glu_ok, CT)
                    if l >= 5:
                        act.wait_ge(conv_3, l - 4)
                    for part in range(2):
                        w, src, dst = tap(CT - 1, l, part)
                        if l == 0:
                            nc.scalar.activation(dst, src, ACT.Identity, bias=par[:, P_CB + CT - 1:P_CB + CT],
                                                 scale=w).then_inc(conv_prod, 1)
                            continue
                        prod = cprod[:, l % 4, 0:SEQ] if part == 0 \
                            else cprod[:, l % 4, SEQ:NT].rearrange("p (b t) -> p b t", t=DT)
                        nc.scalar.activation(prod, src, ACT.Copy, scale=w).then_inc(conv_prod, 1)

            def cmp_exp(i):
                act.wait_ge(ce_in, i + 1)
                if i >= 1:
                    act.wait_ge(pc_ok, i)
                nc.scalar.activation(se[:, :, :], sc[:, :, :], ACT.Exp).then_inc(ce_ok, 1)

            for s in range(S_MRG):
                act.wait_ge(slot_used, s + 1)
                if s < S_GATE - 1:
                    hi(s + 2)
                e = s
                if s < S_KV:
                    if s % 2 == 0:
                        act.wait_ge(glu_p, s // 2)
                        act.wait_ge(glu_ok, s // 2)
                        nc.scalar.activation(sg[:, :], pair(e % 2), ACT.Sigmoid).then_inc(sg_ok, 1)
                elif s < S_Q:
                    nc.scalar.copy(kvT[:, s - S_KV, :], pair(e % 2)).then_inc(kv_ok, 1)
                elif s < S_GATE:
                    nc.scalar.mul(qT[:, s - S_Q, :], pair(e % 2), HD ** -0.5).then_inc(q_ok, 1)
                else:
                    nc.scalar.activation(gT[:, :], pair(e % 2, m=24), ACT.Sigmoid).then_inc(gt_ok, 1)
                if s == S_CMP_K + 1:
                    act.wait_ge(bphi_in, 64)
                    cmp_bias(0)
                if S_CMP_K < s < S_GATE:
                    n = S_GATE - 1 - S_CMP_K
                    conv_products(CW * (s - S_CMP_K - 1) // n, CW * (s - S_CMP_K) // n)
                if s == S_CST:
                    state_rows_out()
                if s >= S_TOK and s < S_GATE:
                    kv_rows(s - S_TOK)
                    if s > S_TOK:
                        kv_rows_out(s - S_TOK - 1)
                if s == S_GATE - 1:
                    kv_rows(TT - 1)
                    kv_rows_out(TT - 2)
                    hi(s + 2)
            act.wait_ge(q_ok, G)
            nc.scalar.copy(qs[:, :, :].rearrange("p h (b r t) -> p (h b) r t", r=G, t=DT),
                           qT[:, :, SEQ:NT].rearrange("p r (b t) -> p b r t", t=DT)).then_inc(qs_ok, 1)
            act.wait_ge(mid_t, 1)
            nc.scalar.copy(gtok[:, 0:4, :], ps[:, 5, 0:96].rearrange("p (i c) -> p i c", c=24)).then_inc(gtok_ok, 1)
            nc.scalar.copy(gtok[0:NS, 4, :], ps[0:NS, 5, 96:120]).then_inc(gtok_ok, 1)

            act.wait_ge(cst_out, 16 * (1 + DB))
            cmp_exp(0)
            cmp_bias(1)
            act.wait_ge(conv_3, CW - 1)
            for n in range(NU + 5):
                if n < NU:
                    act.wait_ge(nmax_ok, n + 1)
                    if n >= 4:
                        act.wait_ge(pt_full, n - 3)
                    nc.scalar.activation(probs_at[n % 4][:, 0:width(n)], ps[:, n % 3, 0:width(n)], ACT.Exp,
                                         bias=nmax[:, n:n + 1], accum_out=esum[:, n:n + 1]).then_inc(exp_ok, 1)
                if n == 2:
                    act.wait_ge(vc_t, 1)
                    nc.scalar.copy(vcp[:, :], ps[0:NCP, 6, 256:256 + P]).then_inc(vc_ok, 1)
                    nc.scalar.copy(vcs[:, :], ps[0:DB * NCS, 6, 384:384 + P]).then_inc(vc_ok, 1)
                if n == 4:
                    hi(S_MRG + 1)
                if n == 5:
                    act.wait_ge(ktok_ok, TT)
                    act.dma_start(kvs_v, ktok[0:NS, TT - 1, 0:512]).then_inc(kv_out, 16)
                if 6 <= n < 6 + DB:
                    b = n - 6
                    act.dma_start(wins_v[b, PAST:PAST + DT, :], ktok[b * DT:(b + 1) * DT, TT - 1, 512:768])\
                        .then_inc(kv_out, 16)
                for i in range(1, 4):
                    if n == FIRST[3 - i] - 6:
                        cmp_exp(i)
                for h in range(2):
                    c = n - LN_SQ[h]
                    if 0 <= c < CT:
                        act.wait_ge(ln_xc, CT * h + c + 1)
                        cols = slice(h * HALF, (h + 1) * HALF)
                        nc.scalar.activation(lnsq[:, c, cols], yc[:, c, cols], ACT.Square).then_inc(ln_sq, 1)
                if n == LN_ROOT:
                    act.wait_ge(ln_step, 2 + CT)
                    nc.scalar.activation(lnv[:, :], lnv[:, :], ACT.Sqrt).then_inc(ln_rs, 1)
                if n == LN_SWISH:
                    for c in range(CT):
                        act.wait_ge(ln_xn, c + 1)
                        nc.scalar.activation(lnsq[:, c, :], yc[:, c, :], ACT.Silu,
                                             bias=par[:, P_LNB + c:P_LNB + c + 1],
                                             scale=par[:, P_LNG + c:P_LNG + c + 1]).then_inc(silu_ok, 1)
                for q in (3, 2, 1, 0, 4, 5):
                    if n == LAST[q] + 4:
                        act.wait_ge(pv_done, LAST[q] + 1)
                        if q < 4:
                            nc.scalar.copy(oh[:, :, q * P:(q + 1) * P],
                                           ps[:, 5 + place(q) % 2, :].rearrange("p (r t) -> p r t", r=G)).then_inc(oh_ok, 1)
                        else:
                            t0 = SEQ + (q - 4) * (NS // 2)
                            nc.scalar.copy(oh[:, :, t0:t0 + NS // 2].rearrange("p r (b t) -> p b r t", t=DT),
                                           ps[:, 5 + place(q) % 2, 0:P].rearrange("p (b r t) -> p b r t", r=G, t=DT))\
                                .then_inc(oh_ok, 1)
            with act.Fori(0, KT // 2) as i:
                for j in range(6):
                    b = (S_MRG + j) % 2
                    act.wait_ge(raw_in[b], 16 * mrg_step(b) * i + mrg_raw(j + 2))
                    act.wait_ge(slot_used, 6 * i + (S_MRG + j + 1))
                    nc.scalar.copy(wh[:, b, :], raw[:, b, :]).then_inc(hi_done, 1)
                    if j % 3 < 2:
                        act.wait_ge(m_sum, 2 * i + j // 3 + AHEAD)
                        act.wait_ge(c_step, 2 * CT)
                        nc.scalar.activation(ms[:, j // 3, j % 3, :], pair(j % 3), ACT.Sigmoid).then_inc(m_sig, 1)

            for kc in range(KT // 2):
                hi(S_OUT + kc + 2)

            def square(i, half, s_end, junk_i, done):
                if half == 1 and i < TT - 1:
                    act.wait_ge(o_tile if s_end == S_UP else d_tile, i + 1)
                else:
                    act.wait_ge(slot_used, s_end)
                m = ROWS[i]
                nc.scalar.activation(junk_i[0:m], ps[0:m, (half * TT + i) % 8, :], ACT.Square,
                                     accum_out=ssh[0:m, half, i:i + 1]).then_inc(done, 1)

            for i in range(TT):
                square(i, 0, S_OUT + KT // 2, junk[:, i, 0:512], o_sq)
            for kc in range(KT // 2, KT - 1):
                hi(S_OUT + kc + 2)
            for t in range(TT + 3):
                if t < TT:
                    square(t, 1, S_UP, junk[:, t, 512:1024], o_sq)
                if 1 <= t <= TT:
                    i, m = t - 1, ROWS[t - 1]
                    act.wait_ge(rs2_step, 2 * i + 2)
                    nc.scalar.activation(rstd[0:m, i:i + 1], ss[0:m, i:i + 1], ACT.Sqrt).then_inc(rs2, 1)
                if 2 <= t <= TT + 1:
                    i, m = t - 2, ROWS[t - 2]
                    act.wait_ge(x1_ok, i + 1)
                    act.wait_ge(o_sq, TT + i + 1)
                    nc.scalar.activation(junk[0:m, i, :], x1[0:m, i, :], ACT.Square,
                                         accum_out=ss[0:m, i:i + 1]).then_inc(sq3, 1)
                if t >= 3:
                    i, m = t - 3, ROWS[t - 3]
                    act.wait_ge(rs3_step, 2 * i + 2)
                    nc.scalar.activation(rstd[0:m, i:i + 1], ss[0:m, i:i + 1], ACT.Sqrt).then_inc(rs3, 1)
                    if i % 2 == 0:
                        act.wait_ge(rs3, i + 1)
                        nc.scalar.activation(hb[0:m, i, :], x1[0:m, i, :], ACT.Copy, scale=rstd[0:m, i:i + 1])\
                            .then_inc(xn2, 1)
            for k in range(KT):
                act.wait_ge(z2_full, k + 1)
                nc.scalar.activation(zh[:, k, :], pf[:, 1024 * (k % 4):1024 * (k % 4) + NT], ACT.Copy,
                                     scale=par[:, P_GFFN + k:P_GFFN + k + 1]).then_inc(z2_hi, 1)
            hi(S_UP + 1)
            act.wait_ge(u_pad, 1)
            with act.Fori(0, FT) as i:
                for j in range(2):
                    b = (S_UP + j) % 2
                    act.wait_ge(raw_in[b], 16 * i + raw_value(S_UP + j + 2))
                    act.wait_ge(slot_used, 2 * i + (S_UP + j + 1))
                    nc.scalar.copy(wh[:, b, :], raw[:, b, :]).then_inc(hi_done, 1)
                    act.wait_ge(cv_step, 6 * i + AHEAD)
                    nc.scalar.copy(u[:, j, 2:2 + SEQ], pair(j, 0, SEQ)).then_inc(u_ev[j], 1)
                    nc.scalar.copy(u[:, j, 2 + SEQ:UEXT].rearrange("p (b t) -> p b t", t=DT + 2)[:, :, 2:DT + 2],
                                   pair(j, SEQ, NT).rearrange("p (b t) -> p b t", t=DT)).then_inc(u_ev[j], 1)
                act.wait_ge(cv_step, 6 * i + 3 + AHEAD)
                nc.scalar.activation(cv[:, 0, :], cv[:, 0, :], ACT.Gelu_apprx_tanh).then_inc(act_ok, 1)

            for kc in range(FT // 2):
                hi(S_DOWN + kc + 2)
                for q in range(2 * kc, min(2 * kc + 2, 11)):
                    act.wait_ge(ul_t, q + 1)
                    nc.scalar.copy(ustage[:, q * 512:(q + 1) * 512], ps[0:18, 5 + q % 3, :]).then_inc(ul_ev, 1)
            act.wait_ge(ffn_out, 32)
            act.wait_ge(gp2_in, 16)

            def root4(i):
                act.wait_ge(rs4_step, 2 * i + 2)
                m = ROWS[i]
                nc.scalar.activation(rstd[0:m, i:i + 1], ss[0:m, i:i + 1], ACT.Sqrt).then_inc(rs4, 1)

            for half in range(2):
                for i in range(TT):
                    jk = junk2[:, i, half * 512:(half + 1) * 512] if i < 4 else junk3[:, half * 512:(half + 1) * 512]
                    square(i, half, S_DOWN + (half + 1) * (FT // 2), jk, d_sq)
                    if half == 1 and i > 0:
                        root4(i - 1)
                if half == 1:
                    root4(TT - 1)
                if half == 0:
                    for kc in range(FT // 2, FT - 2):
                        hi(S_DOWN + kc + 2)

        @block.vector
        def _(dve):
            def lo(s):
                dve.wait_ge(hi_done, s + 1)
                n = KT * 24 if s == S_GATE else 1024
                nc.vector.tensor_tensor(wl[:, s % 2, 0:n], raw[:, s % 2, 0:n], wh[:, s % 2, 0:n].bitcast(F32),
                                        ALU.subtract).then_inc(lo_done, 1)

            for counted in (m_mul, m_ok, cv_step, h_ok):
                dve.sem_inc(counted, AHEAD)
            nc.vector.memset(ext[:, :, 0:HIST], 0.0).then_inc(ext0, 1)
            for t in range(TT + 1):
                if t < TT:
                    m = ROWS[t]
                    dve.wait_ge(sq_done, t + 1)
                    nc.vector.tensor_scalar(ss[0:m, t:t + 1], ss[0:m, t:t + 1], 1.0 / D, EPS, ALU.mult, ALU.add)\
                        .then_inc(rs_step, 1)
                    dve.wait_ge(rs_step, 2 * t + 1)
                    nc.vector.reciprocal(ss[0:m, t:t + 1], ss[0:m, t:t + 1]).then_inc(rs_step, 1)
                if t >= 1:
                    i, m = t - 1, ROWS[t - 1]
                    dve.wait_ge(rs_ok, i + 1)
                    nc.vector.tensor_scalar(x[0:m, i, :], x[0:m, i, :], rstd[0:m, i:i + 1], None,
                                            ALU.mult).then_inc(xn_ok, 1)
            dve.wait_ge(par_t, 1)
            nc.vector.tensor_copy(par[:, 0:2 * P], ps[:, 6, 0:2 * P]).then_inc(par_ok, 1)
            nc.vector.tensor_copy(par[:, 2 * P:P_ALL], ps[:, 6, 2 * P:P_ALL]).then_inc(par_ok, 1)
            lo(0)
            for k in range(KT):
                dve.wait_ge(zhi_ok, k + 1)
                nc.vector.scalar_tensor_tensor(zl[:, k, :], pf[:, 1024 * (k % 4):1024 * (k % 4) + NT],
                                               par[:, P_GPRE + k:P_GPRE + k + 1], zh[:, k, :].bitcast(F32),
                                               ALU.mult, ALU.subtract).then_inc(z_ok, 1)
            lo(1)
            for hf in range(2):
                dve.wait_ge(scv_t, hf + 1)
                for c in range(CT):
                    b0 = HIST + SEQ + 4 * hf * SB_S
                    nc.vector.tensor_copy(
                        ext[:, c, b0:b0 + 4 * SB_S].rearrange("p (b t) -> p b t", t=SB_S)[:, :, 0:HIST],
                        ps[:, 4 + hf, c * 120:(c + 1) * 120].rearrange("p (b t) -> p b t", t=HIST)).then_inc(hist_ok, 1)

            def past(n):
                dve.wait_ge(past_t, n + 1)
                bk = 4 + n % 4
                nc.vector.tensor_copy(cc[:, :, SEQ + n * P:SEQ + (n + 1) * P],
                                      ps[:, bk, 0:256].rearrange("p (j t) -> p j t", j=2)).then_inc(past_ev, 1)
                nc.vector.tensor_copy(kpast[:, :, n * P:(n + 1) * P],
                                      ps[:, bk, 256:512].rearrange("p (j t) -> p j t", j=2)).then_inc(past_ev, 1)

            def conv_taps(done, tiles, l0, l1):
                for l in range(l0, l1):
                    for part in range(2):
                        for n, c in enumerate(tiles):
                            w, src, dst = tap(c, l, part)
                            if l == 0:
                                if part == 0 and n == 0:
                                    dve.wait_ge(hist_ok, 2 * CT)
                                    dve.wait_ge(ext0, 1)
                                    dve.wait_ge(glu_p, tiles[-1] + 1)
                                    dve.wait_ge(glu_ok, tiles[-1] + 1)
                                nc.vector.tensor_scalar(dst, src, w, par[:, P_CB + c:P_CB + c + 1], ALU.mult,
                                                        ALU.add).then_inc(done, 1)
                            else:
                                dve.wait_ge(done, (2 * (l - 1) + part) * len(tiles) + n + 1)
                                nc.vector.scalar_tensor_tensor(dst, src, w, dst, ALU.mult, ALU.add)\
                                    .then_inc(done, 1)

            cstep = [0]

            def link(ins):
                cstep[0] += 1
                ins.then_inc(cs_step, 1)
                dve.wait_ge(cs_step, cstep[0])

            def cmp_soft(i):
                dve.wait_ge(cs_full, i + 1)
                link(nc.vector.tensor_tensor(
                    sc[:, :, :], ps[:, 7, 0:HEADS * 32].rearrange("p (h n) -> p h n", n=32)[:, :, 0:NCP],
                    cneg[:, 3 - i, :].unsqueeze(1).broadcast_to([P, HEADS, NCP]), ALU.add))
                link(nc.vector.tensor_reduce(cmax[:, :], sc[:, :, :], AX.X, ALU.max))
                nc.vector.tensor_tensor(sc[:, :, :], sc[:, :, :],
                                        cmax[:, :].unsqueeze(2).broadcast_to([P, HEADS, NCP]),
                                        ALU.subtract).then_inc(ce_in, 1)

            def cmp_norm(i):
                dve.wait_ge(ce_ok, i + 1)
                if i >= 1:
                    dve.wait_ge(pct_full, 2 * i)
                link(nc.vector.tensor_tensor(se[:, :, :], se[:, :, :],
                                             c01[:, 3 - i, :].unsqueeze(1).broadcast_to([P, HEADS, NCP]), ALU.mult))
                link(nc.vector.tensor_reduce(csum[:, :], se[:, :, :], AX.X, ALU.add))
                link(nc.vector.tensor_scalar(csum[:, :], csum[:, :], TINY, None, ALU.max))
                link(nc.vector.reciprocal(csum[:, :], csum[:, :]))
                link(nc.vector.tensor_tensor(cgate[:, :], csum[:, :], gtok[:, 3 - i, 0:HEADS], ALU.mult))
                nc.vector.tensor_tensor(sm[:, :, :], se[:, :, :],
                                        cgate[:, :].unsqueeze(2).broadcast_to([P, HEADS, NCP]),
                                        ALU.mult).then_inc(pc_ok, 1)

            def cmp_turn(i, hf):
                dve.wait_ge(pct_full, 2 * i + hf + 1)
                if i >= 2:
                    dve.wait_ge(pv_done, LAST[3 - (i - 2)] + 1)
                nc.vector.tensor_copy(pcT[:, i % 2, 4 * hf:4 * hf + 4, :].rearrange("p h t -> p (h t)"),
                                      ps[0:NCP, 7, :]).then_inc(pct_ok, 1)

            for s in range(S_MRG):
                if s < S_GATE - 1:
                    lo(s + 2)
                e = s
                if s < S_KV:
                    past(2 * s)
                    past(2 * s + 1)
                    if s % 2:
                        c = s // 2
                        dve.wait_ge(sg_ok, c + 1)
                        dve.wait_ge(slot_used, s + 1)
                        nc.vector.tensor_tensor(ext[:, c, HIST:HIST + SEQ], sg[:, 0:SEQ], pair(e % 2, 0, SEQ),
                                                ALU.mult).then_inc(glu_p, 1)
                        nc.vector.tensor_tensor(
                            ext[:, c, HIST + SEQ:EXT].rearrange("p (b t) -> p b t", t=SB_S)[:, :, HIST:SB_S],
                            sg[:, SEQ:NT].rearrange("p (b t) -> p b t", t=DT),
                            pair(e % 2, SEQ, NT).rearrange("p (b t) -> p b t", t=DT), ALU.mult)\
                            .then_inc(glu_ok, 1)
                for done, tiles in ((conv_01, (0, 1)), (conv_2, (2,))):
                    s0 = S_GLU + 2 * (tiles[-1] + 1)
                    if s0 <= s < S_GATE:
                        conv_taps(done, tiles, CW * (s - s0) // (S_GATE - s0), CW * (s + 1 - s0) // (S_GATE - s0))
                if s == S_GATE - 1:
                    dve.wait_ge(cst_out, 16 * (1 + DB))
                    cmp_soft(0)
                    lo(s + 2)
            dve.wait_ge(gtok_ok, 2)
            cmp_norm(0)
            for n in range(NU + 5):
                if n < NU:
                    dve.wait_ge(s_full, n + 1)
                    nc.vector.tensor_reduce(nmax[:, n:n + 1], ps[:, n % 3, 0:width(n)], AX.X, ALU.max, negate=True)\
                        .then_inc(nmax_ok, 1)
                if 1 <= n <= NU:
                    dve.wait_ge(exp_ok, n)
                    nc.vector.reciprocal(rinv[:, n - 1:n], esum[:, n - 1:n]).then_inc(rinv_ok, 1)
                if 3 <= n < NU + 3:
                    m = n - 3
                    q, _, _, c = UNITS[m]
                    dve.wait_ge(pt_full, m + 1)
                    if m >= 3:
                        dve.wait_ge(pv_done, m - 2)
                    if q < 4:
                        nc.vector.tensor_copy(pT[:, m % 3, 0:width(m)], ps[:, 3 + m % 2, 0:width(m)]).then_inc(pt_ok, 1)
                    elif c == 0:
                        nc.vector.tensor_copy(pT[0:DB * NCS, m % 3, 0:P], ps[0:DB * NCS, 3 + m % 2, 0:P])\
                            .then_inc(pt_ok, 1)
                    else:
                        nc.vector.tensor_copy(pT[:, m % 3, 0:PAST], ps[:, 3 + m % 2, 0:PAST]).then_inc(pt_part, 1)
                        nc.vector.tensor_copy(pT[0:NS, m % 3, PAST:PAST + P], ps[0:NS, 3 + m % 2, PAST:PAST + P])\
                            .then_inc(pt_ok, 1)
                if n == 4:
                    lo(S_MRG + 1)
                for i in range(4):
                    if n == FIRST[3 - i] - 7:
                        cmp_soft(i)
                    if n == FIRST[3 - i] - 5:
                        cmp_norm(i)
                    if n == (FIRST[3 - i] - 2 if i else 0):
                        cmp_turn(i, 0)
                    if n == (FIRST[3 - i] if i else 1):
                        cmp_turn(i, 1)
                if n == 1:
                    dve.wait_ge(gsel_mm, 1)
                    nc.vector.tensor_copy(rsel[:, :], ps[:, 5, 256:256 + G]).then_inc(rsel_ok, 1)
                    dve.wait_ge(rsel_ok, 1)
                    for hf in range(2):
                        nc.vector.tensor_tensor(
                            gsel4[:, hf], ps[:, 5, 128 + 32 * hf:128 + 32 * hf + 24].rearrange("p (c r) -> p c r", r=G),
                            rsel[:, :].unsqueeze(1).broadcast_to([P, 6, G]), ALU.mult).then_inc(rsel_ok, 1)
                    dve.wait_ge(rsel_ok, 3)
                    nc.vector.tensor_reduce(gsel[:, :, :].rearrange("p h c -> p (h c)"),
                                            gsel4[:, :, :, :].rearrange("p h c r -> p (h c) r"), AX.X, ALU.add)\
                        .then_inc(gsel_ok, 1)
                for h in range(2):
                    cols = slice(h * HALF, (h + 1) * HALF)
                    c = n - LN_XC[h]
                    if 0 <= c < CT:
                        dve.wait_ge(ln_mean, h + 1)
                        nc.vector.tensor_tensor(yc[:, c, cols], yc[:, c, cols], ps[:, 7, 0:HALF], ALU.subtract)\
                            .then_inc(ln_xc, 1)
                    if n == LN_TAKE[h]:
                        dve.wait_ge(ln_var, h + 1)
                        nc.vector.tensor_scalar(lnv[:, cols], ps[:, 7, 0:HALF], EPS, None, ALU.add)\
                            .then_inc(ln_step, 1)
                c = n - LN_TAKE[1] - 1
                if 0 <= c < CT:
                    dve.wait_ge(ln_step, 2)
                    cols = slice(c * NT // CT, (c + 1) * NT // CT)
                    nc.vector.reciprocal(lnv[:, cols], lnv[:, cols]).then_inc(ln_step, 1)
                for c in range(CT):
                    if n == LN_NORM + c:
                        dve.wait_ge(ln_rs, 1)
                        dve.wait_ge(ln_sq, 2 * CT)
                        dve.wait_ge(ln_xc, 2 * CT)
                        nc.vector.tensor_tensor(yc[:, c, :], yc[:, c, :], lnv[:, :], ALU.mult).then_inc(ln_xn, 1)
                for q in (3, 2, 1, 0, 4, 5):
                    if n == LAST[q] + 4:
                        dve.wait_ge(oh_ok, place(q) + 1)
                        if q < 4:
                            nc.vector.tensor_tensor(
                                ol[:, :, q * P:(q + 1) * P], ps[:, 5 + place(q) % 2, :].rearrange("p (r t) -> p r t", r=G),
                                oh[:, :, q * P:(q + 1) * P].bitcast(F32), ALU.subtract).then_inc(ol_ok, 1)
                        else:
                            t0 = SEQ + (q - 4) * (NS // 2)
                            nc.vector.tensor_tensor(
                                ol[:, :, t0:t0 + NS // 2].rearrange("p r (b t) -> p b r t", t=DT),
                                ps[:, 5 + place(q) % 2, 0:P].rearrange("p (b r t) -> p b r t", r=G, t=DT),
                                oh[:, :, t0:t0 + NS // 2].bitcast(F32).rearrange("p r (b t) -> p b r t", t=DT),
                                ALU.subtract).then_inc(ol_ok, 1)
            for c in range(CT):
                dve.wait_ge(silu_ok, c + 1)
                nc.vector.tensor_copy(ch[:, c, :], lnsq[:, c, :]).then_inc(c_step, 1)
                dve.wait_ge(c_step, 2 * c + 1)
                nc.vector.tensor_tensor(cl[:, c, :], lnsq[:, c, :], ch[:, c, :].bitcast(F32), ALU.subtract)\
                    .then_inc(c_step, 1)
            dve.wait_ge(kv_out, 16 * (4 * 2 + 1 + DB))
            with dve.Fori(0, KT // 2) as i:
                for j in range(6):
                    b = (S_MRG + j) % 2
                    dve.wait_ge(hi_done, 6 * i + (S_MRG + j + 3))
                    nc.vector.tensor_tensor(wl[:, b, :], raw[:, b, :], wh[:, b, :].bitcast(F32), ALU.subtract)\
                        .then_inc(lo_done, 1)
                    if j % 3 == 2:
                        h = j // 3
                        m = 2 * i + h
                        for q in range(2):
                            dve.wait_ge(m_sig, 4 * i + 2 * h + q + 1 + AHEAD)
                            if q == 0:
                                dve.wait_ge(m_attn, 2 * i + h + 1)
                            else:
                                dve.wait_ge(slot_used, 6 * i + (S_MRG + 3 * h + 3))
                            nc.vector.tensor_tensor(ms[:, h, q, :], ms[:, h, q, :], pair(2 + q), ALU.mult)\
                                .then_inc(m_mul, 1)
                        dve.wait_ge(m_sum, 2 * i + h + 1 + AHEAD)
                        nc.vector.tensor_scalar(mh[:, bass.ds(m, 1), :], msum[:, h:h + 1, :], 1.0, None, ALU.mult)\
                            .then_inc(m_hi, 1)
                        dve.wait_ge(m_hi, 2 * i + h + 1)
                        nc.vector.tensor_tensor(ml[:, bass.ds(m, 1), :], msum[:, h:h + 1, :],
                                                mh[:, bass.ds(m, 1), :].bitcast(F32), ALU.subtract).then_inc(m_ok, 1)
            for kc in range(KT // 2):
                lo(S_OUT + kc + 2)

            def gained(i, half, sq, out, gain, done):
                dve.wait_ge(sq, half * TT + i + 1)
                m = ROWS[i]
                cols = slice(half * 512, (half + 1) * 512)
                nc.vector.tensor_tensor(out[0:m, i, cols], ps[0:m, (half * TT + i) % 8, :], gain[0:m, cols],
                                        ALU.mult).then_inc(done, 1)

            def first_half(sq, pre):
                dve.wait_ge(sq, TT)
                nc.vector.tensor_scalar(ssh[:, 0, 0:4], ssh[:, 0, 0:4], 1.0 / D, EPS, ALU.mult, ALU.add)\
                    .then_inc(pre, 1)
                nc.vector.tensor_scalar(ssh[0:NS, 0, 4:5], ssh[0:NS, 0, 4:5], 1.0 / D, EPS, ALU.mult, ALU.add)\
                    .then_inc(pre, 1)

            def mean_square(i, sq, pre, step):
                m = ROWS[i]
                dve.wait_ge(sq, TT + i + 1)
                dve.wait_ge(pre, 2)
                nc.vector.scalar_tensor_tensor(ss[0:m, i:i + 1], ssh[0:m, 1, i:i + 1], 1.0 / D, ssh[0:m, 0, i:i + 1],
                                               ALU.mult, ALU.add).then_inc(step, 1)
                dve.wait_ge(step, 2 * i + 1)
                nc.vector.reciprocal(ss[0:m, i:i + 1], ss[0:m, i:i + 1]).then_inc(step, 1)

            def add_normed(i, src, rs, ev, ok):
                m = ROWS[i]
                dve.wait_ge(rs, i + 1)
                dve.wait_ge(ev, TT + i + 1)
                nc.vector.scalar_tensor_tensor(x1[0:m, i, :], src[0:m, i, :], rstd[0:m, i:i + 1], x1[0:m, i, :],
                                               ALU.mult, ALU.add).then_inc(ok, 1)

            dve.wait_ge(gp_in, 16)
            for i in range(TT):
                gained(i, 0, o_sq, hb, gpost, o_ev)
            first_half(o_sq, rs2_pre)
            dve.wait_ge(x1_in, 16 * TT)
            for kc in range(KT // 2, KT - 1):
                lo(S_OUT + kc + 2)
            for t in range(TT + 3):
                if t < TT:
                    gained(t, 1, o_sq, hb, gpost, o_ev)
                    mean_square(t, o_sq, rs2_pre, rs2_step)
                if 1 <= t <= TT:
                    add_normed(t - 1, hb, rs2, o_ev, x1_ok)
                if t == TT + 1:
                    dve.wait_ge(sf_t, 1)
                    nc.vector.tensor_copy(sfT[:, :, :].rearrange("p t r -> p (t r)"), pf[:, 1024:1024 + 2 * FT * 16])\
                        .then_inc(sf_ok, 1)
                if 2 <= t <= TT + 1:
                    i, m = t - 2, ROWS[t - 2]
                    dve.wait_ge(sq3, i + 1)
                    nc.vector.tensor_scalar(ss[0:m, i:i + 1], ss[0:m, i:i + 1], 1.0 / D, EPS, ALU.mult, ALU.add)\
                        .then_inc(rs3_step, 1)
                    dve.wait_ge(rs3_step, 2 * i + 1)
                    nc.vector.reciprocal(ss[0:m, i:i + 1], ss[0:m, i:i + 1]).then_inc(rs3_step, 1)
                if t >= 3 and t % 2 == 0:
                    i, m = t - 3, ROWS[t - 3]
                    dve.wait_ge(rs3, i + 1)
                    nc.vector.tensor_scalar(hb[0:m, i, :], x1[0:m, i, :], rstd[0:m, i:i + 1], None, ALU.mult)\
                        .then_inc(xn2, 1)
            for k in range(KT):
                dve.wait_ge(z2_hi, k + 1)
                nc.vector.scalar_tensor_tensor(zl[:, k, :], pf[:, 1024 * (k % 4):1024 * (k % 4) + NT],
                                               par[:, P_GFFN + k:P_GFFN + k + 1], zh[:, k, :].bitcast(F32),
                                               ALU.mult, ALU.subtract).then_inc(z2_ok, 1)
            lo(S_UP + 1)
            dve.wait_ge(sf_ok, 1)
            nc.vector.memset(u[:, :, 0:2], 0.0).then_inc(u_pad, 1)
            with dve.Fori(0, FT) as i:
                for j in range(2):
                    b = (S_UP + j) % 2
                    dve.wait_ge(hi_done, 2 * i + (S_UP + j + 3))
                    nc.vector.tensor_tensor(wl[:, b, :], raw[:, b, :], wh[:, b, :].bitcast(F32), ALU.subtract)\
                        .then_inc(lo_done, 1)
                    t = i + FT * j
                    hist = u[:, j, 2 + SEQ:UEXT].rearrange("p (b t) -> p b t", t=DT + 2)
                    dve.wait_ge(cv_step, 6 * i + 3 * j + AHEAD)
                    nc.vector.tensor_scalar(hist[:, :, 0:2],
                                            sfT[:, bass.ds(t, 1), :].rearrange("p o (b t) -> p (o b) t", t=2),
                                            1.0, None, ALU.mult).then_inc(u_hist, 1)
                    dve.wait_ge(u_ev[j], 2 * i + 2 + AHEAD)
                    nc.vector.tensor_scalar(ulast[:, bass.ds(t, 1), 0:2], u[:, j:j + 1, SEQ:SEQ + 2], 1.0, None,
                                            ALU.mult).then_inc(u_kept, 1)
                    nc.vector.tensor_scalar(
                        ulast[:, bass.ds(t, 1), 2:18].rearrange("p o (b t) -> p (o b) t", t=2),
                        hist[:, :, DT:DT + 2], 1.0, None, ALU.mult).then_inc(u_kept, 1)
                    if j == 0:
                        dve.wait_ge(h_mul, 2 * i + AHEAD)
                    dve.wait_ge(u_hist, 2 * i + j + 1)
                    nc.vector.tensor_scalar(cv[:, j, :], u[:, j, 0:CEXT], par[:, bass.ds(t + P_FW, 1)],
                                            par[:, bass.ds(t + P_FB, 1)], ALU.mult, ALU.add).then_inc(cv_step, 1)
                    for l in (1, 2):
                        dve.wait_ge(cv_step, 6 * i + 3 * j + l + AHEAD)
                        nc.vector.scalar_tensor_tensor(cv[:, j, :], u[:, j, l:l + CEXT],
                                                       par[:, bass.ds(t + P_FW + l * 2 * FT, 1)],
                                                       cv[:, j, :], ALU.mult, ALU.add).then_inc(cv_step, 1)
                dve.wait_ge(h_mul, 2 * i + 2 + AHEAD)
                nc.vector.tensor_scalar(hh[:, bass.ds(i, 1), :], hs[:, :].unsqueeze(1), 1.0, None, ALU.mult)\
                    .then_inc(h_hi, 1)
                dve.wait_ge(h_hi, i + 1)
                nc.vector.tensor_tensor(hl[:, bass.ds(i, 1), :], hs[:, :].unsqueeze(1),
                                        hh[:, bass.ds(i, 1), :].bitcast(F32), ALU.subtract).then_inc(h_ok, 1)
            for kc in range(FT // 2):
                lo(S_DOWN + kc + 2)
            dve.wait_ge(gp2_in, 16)
            dve.wait_ge(ffn_out, 32)
            for i in range(TT):
                gained(i, 0, d_sq, fb, gpost2, d_ev)
            first_half(d_sq, rs4_pre)
            for kc in range(FT // 2, FT - 2):
                lo(S_DOWN + kc + 2)
            for t in range(TT + 1):
                if t < TT:
                    gained(t, 1, d_sq, fb, gpost2, d_ev)
                    mean_square(t, d_sq, rs4_pre, rs4_step)
                if t >= 1:
                    add_normed(t - 1, fb, rs4, d_ev, y_ok)

        @block.tensor
        def _(pe):
            def three(out, a, b, start, stop):
                (ah, al), (bh, bl) = a, b
                nc.tensor.matmul(out, ah, bh, start=start, stop=False)
                nc.tensor.matmul(out, ah, bl, start=False, stop=False)
                return nc.tensor.matmul(out, al, bh, start=False, stop=stop)

            def tile(q, slot, k0, kn, src, m=P, view=None, halves=(0, 1)):
                for h in halves:
                    cols = slice(h * HALF, (h + 1) * HALF)
                    for k in range(kn):
                        if view is None:
                            w = (whk[:, slot, k0 + k, :], wlk[:, slot, k0 + k, :])
                        else:
                            w = (view[0][:, k, :], view[1][:, k, :])
                        last = three(pair(q, h * HALF, (h + 1) * HALF, m), w,
                                     (src[0][:, k, cols], src[1][:, k, cols]), k == 0, k == kn - 1)
                return last

            pe.wait_ge(const_ok, 1)
            pe.wait_ge(par_in, 16 * 9)
            nc.tensor.transpose(ps[:, 6, 0:P], par_raw[:, 0, :], ident[:, :])
            nc.tensor.transpose(ps[:, 6, P:2 * P], par_raw[:, 1, :], ident[:, :])
            m = P_ALL - 2 * P
            nc.tensor.transpose(ps[:, 6, 2 * P:P_ALL], par_raw[0:m, 2, :], ident[0:m, 0:m]).then_inc(par_t, 1)
            def turn_x(src, full, taken):
                for k in range(KT):
                    if k == 3:
                        pe.wait_ge(par_ok, 2)
                    if k >= 4:
                        pe.wait_ge(taken, k - 3)
                    for i in range(TT):
                        c0 = 1024 * (k % 4) + i * P
                        mm = nc.tensor.transpose(pf[:, c0:c0 + ROWS[i]], src[0:ROWS[i], i, k * P:(k + 1) * P],
                                                 ident[0:ROWS[i], 0:ROWS[i]])
                    mm.then_inc(full, 1)
                pe.wait_ge(taken, KT)

            pe.wait_ge(xn_ok, TT)
            turn_x(x, z_full, z_ok)
            pe.wait_ge(scv_in, 32)
            for hf in range(2):
                for c in range(CT):
                    mm = nc.tensor.transpose(ps[:, 4 + hf, c * 120:(c + 1) * 120],
                                             scv[0:120, hf, c * P:(c + 1) * P], ident[0:120, 0:120])
                mm.then_inc(scv_t, 1)

            def past(n):
                pe.wait_ge(page_in[n % 2], 32 * (n // 2 + 1))
                if n == 0:
                    pe.wait_ge(hist_ok, 2 * CT)
                    pe.wait_ge(par_ok, 2)
                if n >= 4:
                    pe.wait_ge(past_ev, 2 * (n - 3))
                for j, c0 in enumerate((0, 128, 256, 512)):
                    mm = nc.tensor.transpose(ps[:, 4 + n % 4, j * P:(j + 1) * P], page[:, n % 2, c0:c0 + P],
                                             ident[:, :])
                mm.then_inc(past_t, 1)

            def compress(j, t0=0, t1=CL):
                if t0 == 0:
                    pe.wait_ge(phi_in, 32 * (j + 1))
                    pe.wait_ge(cc_ok, j + 1)
                    pe.wait_ge(past_ev, 2 * NPG)
                    if j == 1:
                        pe.wait_ge(ktok_ok, TT - 1)
                for t in range(t0, t1):
                    mm = nc.tensor.matmul(ps[:, (4, 6)[j], 0:NCALL], phi[:, t, :],
                                          cc[:, j, t:t + CS * (NCALL - 1) + 1:CS],
                                          start=(t == 0), stop=(t == CL - 1))
                if t1 == CL:
                    mm.then_inc(cmp_mm, 1)

            def state_rows():
                for c in range(CT):
                    mm = nc.tensor.transpose(ps[0:HIST, 5, c * P:(c + 1) * P], ext[:, c, SEQ:SEQ + HIST], ident[:, :])
                mm.then_inc(cst_t, 1)
                for q, (b0, nb) in enumerate(SEQ_GROUPS):
                    if q == 2:
                        pe.wait_ge(cmp_ok, 2)
                    for c in range(CT):
                        c0 = HIST + SEQ + b0 * SB_S
                        mm = nc.tensor.transpose(ps[0:nb * SB_S, (6, 7, 4)[q], c * P:(c + 1) * P],
                                                 ext[:, c, c0:c0 + nb * SB_S], ident[:, :])
                    mm.then_inc(cst_t, 1)

            def kv_rows(i):
                if i == 0:
                    pe.wait_ge(kv_ok, 6)
                    pe.wait_ge(cst_ok, 4)
                elif i < 4:
                    pe.wait_ge(ktok_ok, i)
                else:
                    pe.wait_ge(cmp_ok, 2)
                for j in range(6):
                    c0 = (6 if i < 4 else 4) * 512 + j * P
                    mm = nc.tensor.transpose(pf[0:ROWS[i], c0:c0 + P], kvT[:, j, i * P:i * P + ROWS[i]], ident[:, :])
                mm.then_inc(ktok_t, 1)

            def cmp_scores(i):
                q0 = (3 - i) * P
                if i == 0:
                    pe.wait_ge(q_ok, G)
                    pe.wait_ge(ktok_ok, TT - 1)
                else:
                    pe.wait_ge(pct_ok, 2 * i)
                for h in range(HEADS):
                    g, r = h // G, h % G
                    if h == G:
                        pe.wait_ge(cs_half, i + 1)
                    mm = nc.tensor.matmul(ps[:, 7, h * 32:h * 32 + NCP], qT[g * HD:(g + 1) * HD, r, q0:q0 + P],
                                          kcmp[g * HD:(g + 1) * HD, 0:NCP], start=True, stop=True)
                    if h == G - 1:
                        mm.then_inc(cs_half, 1)
                mm.then_inc(cs_full, 1)

            z = (zh, zl)
            for s in range(S_MRG):
                pe.wait_ge(lo_done, s + 1)
                if s >= 2:
                    t = s - 2
                    if t < S_KV and t % 2 == 0:
                        pe.wait_ge(sg_ok, t // 2 + 1)
                    elif t < S_KV:
                        pe.wait_ge(glu_p, t // 2 + 1)
                        pe.wait_ge(glu_ok, t // 2 + 1)
                    elif t < S_Q:
                        pe.wait_ge(kv_ok, t - S_KV + 1)
                    else:
                        pe.wait_ge(q_ok, t - S_Q + 1)
                if s == S_GATE:
                    vh = wh[:, s % 2, 0:KT * 24].rearrange("p (k n) -> p k n", n=24)
                    vl = wl[:, s % 2, 0:KT * 24].rearrange("p (k n) -> p k n", n=24)
                    tile(s % 2, s % 2, 0, KT, z, 24, (vh, vl), (0,))
                    cmp_scores(0)
                    tile(s % 2, s % 2, 0, KT, z, 24, (vh, vl), (1,)).then_inc(slot_used, 1)
                else:
                    tile(s % 2, s % 2, 0, KT, z).then_inc(slot_used, 1)
                if s < S_KV:
                    past(2 * s)
                    past(2 * s + 1)
                if s == S_CMP_K:
                    compress(0)
                if s == S_CST:
                    state_rows()
                if s >= S_TOK and s < S_GATE:
                    kv_rows(s - S_TOK)
                if s == S_GATE - 1:
                    kv_rows(TT - 1)
            def cmp_turn(i, hf):
                if hf == 0:
                    pe.wait_ge(pc_ok, i + 1)
                else:
                    pe.wait_ge(pct_ok, 2 * i + 1)
                for h in range(4):
                    mm = nc.tensor.transpose(ps[0:NCP, 7, h * P:(h + 1) * P], sm[:, 4 * hf + h, :], ident[:, :])
                mm.then_inc(pct_full, 1)

            def scores(n):
                q, r, g, c = UNITS[n]
                if n >= 3:
                    pe.wait_ge(exp_ok, n - 2)
                rows = slice(g * HD, (g + 1) * HD)
                bk, w = n % 3, width(n)
                if q < 4:
                    if q:
                        nc.tensor.matmul(ps[:, bk, 0:w - P], qT[rows, r, q * P:(q + 1) * P], kvT[rows, 2 * c, 0:w - P],
                                         start=True, stop=True)
                    nc.tensor.matmul(ps[:, bk, w - P:w], qT[rows, r, q * P:(q + 1) * P], kvT[rows, 2 * c, w - P:w],
                                     start=True, stop=False)
                    nc.tensor.matmul(ps[:, bk, w - P:w], identb[:, :], causal[:, :], start=False, stop=True)\
                        .then_inc(s_full, 1)
                    return
                hf = q - 4
                if c == 0:
                    nc.tensor.matmul(ps[:, bk, 0:w], qs[rows, hf, :], kcmp[rows, NCP:], start=True, stop=False)
                    nc.tensor.matmul(ps[:, bk, 0:w], rowsel[rows, hf, :], cmpmask[rows, :], start=False, stop=True)\
                        .then_inc(s_full, 1)
                    return
                for b in range(4):
                    k0 = (4 * hf + b) * PAST
                    nc.tensor.matmul(ps[32 * b:32 * b + 32, bk, 0:PAST], qs[rows, hf, 32 * b:32 * b + 32],
                                     kpast[rows, c - 1, k0:k0 + PAST], start=True, stop=True)
                nc.tensor.matmul(ps[:, bk, PAST:w], qs[rows, hf, :], kvT[rows, 2 * c, SEQ:NT], start=True, stop=False)
                nc.tensor.matmul(ps[:, bk, PAST:w], rowsel[rows, hf, :], newmask[rows, :], start=False, stop=True)\
                    .then_inc(s_full, 1)

            def turn(n):
                q, _, _, c = UNITS[n]
                pe.wait_ge(scaled, n + 1)
                if n >= 2:
                    pe.wait_ge(pt_ok, n - 1)
                bk, w = 3 + n % 2, width(n)
                c0 = 0
                while c0 < w:
                    m = min(P, w - c0)
                    mm = nc.tensor.transpose(ps[0:m, bk, c0:c0 + P], probs_at[n % 4][:, c0:c0 + m], ident[:, :])
                    c0 += P
                mm.then_inc(pt_full, 1)

            def values(n):
                q, r, g, c = UNITS[n]
                if place(q) >= 2 and n == FIRST[q]:
                    pe.wait_ge(ol_ok, place(q) - 1)
                pe.wait_ge(pt_ok, n + 1)
                rows = slice(g * HD, (g + 1) * HD)
                v0 = (2 * c + 1) * P + g * HD
                pt = pT[:, n % 3, :]
                if q < 4:
                    out = ps[rows, 5 + place(q) % 2, r * P:(r + 1) * P]
                    if c == 1:
                        pe.wait_ge(pct_ok, 2 * place(q) + 2)
                        nc.tensor.matmul(out, vcp[:, rows], pcT[:, place(q) % 2, g * G + r, :], start=True, stop=False)
                    for j in range(q + 1):
                        mm = nc.tensor.matmul(out, ktok[:, j, v0:v0 + HD], pt[:, j * P:(j + 1) * P],
                                              start=False, stop=(c == 2 and j == q))
                    mm.then_inc(pv_done, 1)
                    return
                out = ps[rows, 5 + place(q) % 2, 0:P]
                if c == 0:
                    nc.tensor.matmul(out, vcs[:, rows], pt[0:DB * NCS, 0:P], start=True, stop=False)\
                        .then_inc(pv_done, 1)
                    return
                vp = vsel if c == 1 else vwin
                for b in range(4):
                    for j in range(2):
                        nc.tensor.matmul(ps[rows, 5 + place(q) % 2, 32 * b:32 * b + 32],
                                         vp[:, 2 * (4 * (q - 4) + b) + j, rows],
                                         pt[:, j * P + 32 * b:j * P + 32 * b + 32], start=False, stop=False)
                mm = nc.tensor.matmul(out, ktok[0:NS, 4, v0:v0 + HD], pt[0:NS, PAST:PAST + P],
                                      start=False, stop=(c == 2))
                mm.then_inc(pv_done, 1)

            compress(1, 0, CL // 2)
            pe.wait_ge(gt_ok, 1)
            pe.wait_ge(ktok_ok, TT)
            for i in range(TT):
                mm = nc.tensor.transpose(ps[0:ROWS[i], 5, i * 24:(i + 1) * 24], gT[:, i * P:i * P + ROWS[i]],
                                         ident[0:24, 0:24])
            mm.then_inc(mid_t, 1)
            compress(1, CL // 2, CL)
            for n in range(NU + 4):
                if n == 2:
                    pe.wait_ge(cmp_ok, 4)
                    nc.tensor.transpose(ps[0:NCP, 6, 256:256 + P], vcmpT[:, 0:NCP], ident[:, :])
                    nc.tensor.transpose(ps[0:DB * NCS, 6, 384:384 + P], vcmpT[:, NCP:], ident[:, :]).then_inc(vc_t, 1)
                if n == 4:
                    pe.wait_ge(gsel_ok, 1)
                    pe.wait_ge(vc_ok, 2)
                    pe.wait_ge(qs_ok, 1)
                if n < NU:
                    scores(n)
                if 3 <= n < NU + 3:
                    turn(n - 3)
                if n >= 4:
                    values(n - 4)
                if n == 1:
                    pe.wait_ge(const_ok, 2)
                    pe.wait_ge(gtok_ok, 2)
                    nc.tensor.transpose(ps[:, 5, 256:256 + G], rselT[:, :], ident[0:G, 0:G])
                    for hf in range(2):
                        mm = nc.tensor.matmul(ps[:, 5, 128 + 32 * hf:128 + 32 * hf + 24], rowsel[0:NS, hf, :],
                                              gtok[0:NS, 4, :], start=True, stop=True)
                    mm.then_inc(gsel_mm, 1)
                for i in range(4):
                    if n == FIRST[3 - i] - 8:
                        cmp_scores(i)
                    if n == (FIRST[3 - i] - 3 if i else 0):
                        cmp_turn(i, 0)
                    if n == (FIRST[3 - i] - 1 if i else 1):
                        cmp_turn(i, 1)
                for h in range(2):
                    cols = slice(h * HALF, (h + 1) * HALF)
                    if n == LN_MEAN[h]:
                        if h == 0:
                            pe.wait_ge(pct_ok, 8)
                            pe.wait_ge(conv_01, 4 * CW)
                            pe.wait_ge(conv_2, 2 * CW)
                            pe.wait_ge(conv_3, CW - 1)
                        else:
                            pe.wait_ge(ln_xc, CT)
                        for c in range(CT):
                            mm = nc.tensor.matmul(ps[:, 7, 0:HALF], mean_w[:, :], yc[:, c, cols],
                                                  start=(c == 0), stop=(c == CT - 1))
                        mm.then_inc(ln_mean, 1)
                    if n == LN_VAR[h]:
                        pe.wait_ge(ln_sq, CT * (h + 1))
                        if h == 0:
                            pe.wait_ge(ln_xc, 2 * CT)
                        else:
                            pe.wait_ge(ln_step, 1)
                        for c in range(CT):
                            mm = nc.tensor.matmul(ps[:, 7, 0:HALF], mean_w[:, :], lnsq[:, c, cols],
                                                  start=(c == 0), stop=(c == CT - 1))
                        mm.then_inc(ln_var, 1)
            pe.wait_ge(exp_ok, NU)
            pe.wait_ge(pt_ok, NU)
            pe.wait_ge(ln_step, 2)
            with pe.Fori(0, KT // 2) as i:
                for j in range(6):
                    b = (S_MRG + j) % 2
                    h = j // 3
                    pe.wait_ge(lo_done, 6 * i + (S_MRG + j + 1))
                    if j % 3 < 2:
                        pe.wait_ge(m_sig, 4 * i + 2 * h + AHEAD)
                        tile(j % 3, b, 0, KT, z).then_inc(slot_used, 1)
                    else:
                        pe.wait_ge(m_mul, 4 * i + 2 * h + AHEAD)
                        pe.wait_ge(ol_ok, 6)
                        tile(2, b, 0, CT, (oh, ol)).then_inc(m_attn, 1)
                        pe.wait_ge(c_step, 2 * CT)
                        tile(3, b, CT, CT, (ch, cl)).then_inc(slot_used, 1)

            def token_major(s0, kn, lhs, lhs_ok, bank4, taken, tile_done, after):
                for half in range(2):
                    for kc in range(kn // 2):
                        s = s0 + half * (kn // 2) + kc
                        pe.wait_ge(lo_done, s + 1)
                        pe.wait_ge(lhs_ok, 2 * kc + 2 + AHEAD)
                        for i in range(TT):
                            bk = half * TT + i
                            if half == 0 and kc == 0 and bk == 4:
                                pe.wait_ge(bank4[0], bank4[1])
                            if kc == 0 and bk >= 8:
                                pe.wait_ge(taken, bk - 8 + 1)
                            for kk in range(2):
                                k = 2 * kc + kk
                                mm = three(ps[0:ROWS[i], bk % 8, :],
                                           (lhs[0][:, k, i * P:i * P + ROWS[i]], lhs[1][:, k, i * P:i * P + ROWS[i]]),
                                           (whc[:, s % 2, kk, :], wlc[:, s % 2, kk, :]), k == 0, k == kn - 1)
                            if half == 1 and kc == kn // 2 - 1 and i < TT - 1:
                                mm.then_inc(tile_done, 1)
                        mm.then_inc(slot_used, 1)
                        after(half, kc)

            pe.wait_ge(m_sig, 2 * KT + AHEAD)
            token_major(S_OUT, KT, (mh, ml), m_ok, (m_mul, 2 * KT + AHEAD), o_ev, o_tile, lambda half, kc: None)
            pe.wait_ge(sf_in, 16)
            for t in range(2 * FT):
                mm = nc.tensor.transpose(pf[:, 1024 + 16 * t:1024 + 16 * (t + 1)], sf[:, t * P:(t + 1) * P],
                                         ident[0:16, 0:16])
            mm.then_inc(sf_t, 1)
            pe.wait_ge(sf_ok, 1)
            pe.wait_ge(o_ev, 2 * TT)
            pe.wait_ge(o_sq, 2 * TT)
            pe.wait_ge(xn2, TT)
            turn_x(hb, z2_full, z2_ok)
            with pe.Fori(0, FT) as i:
                for j in range(2):
                    pe.wait_ge(lo_done, 2 * i + (S_UP + j + 1))
                    pe.wait_ge(u_ev[j], 2 * i + AHEAD)
                    tile(j, (S_UP + j) % 2, 0, KT, z).then_inc(slot_used, 1)

            def last_rows(half, kc):
                if half or kc > 5:
                    return
                pe.wait_ge(u_kept, 4 * FT)
                for q in range(2 * kc, min(2 * kc + 2, 11)):
                    if q >= 3:
                        pe.wait_ge(ul_ev, q - 2)
                    for t in range(4):
                        mm = nc.tensor.transpose(ps[0:18, 5 + q % 3, t * P:(t + 1) * P], ulast[:, 4 * q + t, :],
                                                 ident[:, :])
                    mm.then_inc(ul_t, 1)

            pe.wait_ge(u_ev[0], 2 * FT + AHEAD)
            pe.wait_ge(u_ev[1], 2 * FT + AHEAD)
            token_major(S_DOWN, FT, (hh, hl), h_ok, (u_ev[1], 2 * FT + AHEAD), d_ev, d_tile, last_rows)


_INS = ["x_prompt", "x_sample", "cache_kv", "state_kv_win", "state_conv", "state_ffn", "page_table",
        "norm_mix_pre", "norm_mix_post", "norm_ffn_pre", "norm_ffn_post", "w_in", "w_phi_k", "b_phi_k",
        "w_phi_v", "b_phi_v", "w_attn_out", "conv_w", "conv_b", "conv_ln_g", "conv_ln_b", "w_conv_out",
        "w_out", "w_up", "ffn_conv_w", "ffn_conv_b", "w_down"]
_OUTS = [(1, SEQ, D), (DB, DT, D), (1, 1, SEQ, 4, KVH, HD), (1, DB, DT, 4, KVH, HD), (1, 1, SEQ, 2, KVH, HD),
         (1, DB, PAST + DT, 2, KVH, HD), (1, 1, HIST, CH), (1, DB, HIST, CH), (1, 1, FW - 1, 2 * FF),
         (1, DB, FW - 1, 2 * FF)]


def kernel(**inputs):
    import numpy as _np
    import concourse.bacc as _bacc
    from concourse import mybir as _mybir
    from concourse.bass_utils import run_bass_kernel_spmd as _run

    nc = _bacc.Bacc("TRN2", target_bir_lowering=False, num_devices=1)
    arrays, args = {}, []
    for name in _INS:
        a = _np.ascontiguousarray(inputs[name])
        arrays[f"in_{name}_dram"] = a
        args.append(nc.dram_tensor(f"in_{name}_dram", a.shape, _mybir.dt.from_np(a.dtype), kind="ExternalInput").ap())
    for i, shape in enumerate(_OUTS):
        args.append(nc.dram_tensor(f"out_{i}_dram", shape, _mybir.dt.float32, kind="ExternalOutput").ap())
    build_layer(nc, *args)
    r = _run(nc, [arrays], core_ids=[0])
    return tuple(r.results[0][f"out_{i}_dram"] for i in range(len(_OUTS)))
```
